# Optimizing a Trainium2 kernel written in Bass

```python
import math
import jax, jax.numpy as jnp
from jax import lax
import numpy as np

D_MODEL = 1024
BATCH = 1
SEQ = 512
DEPTH = 2

EPS = 1e-6
HEAD_DIM = 64
BRANCH_W = 512
N_BRANCH = 4
HG_HEADS = 8
HG_DK = 64
HG_DV = 64
HG_CHUNK = 64
MLA_HEADS = 8
MLA_Q_RANK = 256
MLA_KV_RANK = 128
MLA_NOPE = 64
MLA_ROPE = 32
MLA_V = 64
ROPE_BASE = 10000.0
MAX_POS_OFFSET = 4096
DIFF_HEADS = 4
DIFF_QK = 64
DIFF_V = 128
SWA_Q_HEADS = 8
SWA_KV_HEADS = 2
SWA_WINDOW = 128
Q_BLOCK = 128
N_EXPERTS = 16
N_GROUPS = 4
TOP_K = 2
D_FF_EXPERT = 256

IN_SPLITS = (
    HG_HEADS * HG_DK, HG_HEADS * HG_DK, HG_HEADS * HG_DV, HG_HEADS * HG_DV,
    MLA_Q_RANK, MLA_KV_RANK, MLA_ROPE,
    DIFF_HEADS * 2 * DIFF_QK, DIFF_HEADS * 2 * DIFF_QK, DIFF_HEADS * DIFF_V,
    SWA_Q_HEADS * HEAD_DIM, SWA_KV_HEADS * HEAD_DIM, SWA_KV_HEADS * HEAD_DIM,
    N_BRANCH * D_MODEL,
)
N_IN = sum(IN_SPLITS)
SPLIT_POINTS = tuple(sum(IN_SPLITS[:i + 1]) for i in range(len(IN_SPLITS) - 1))

kernel_name = 'hybrid_gated_hgrn2_mla_diff_swa_moe'

def rmsnorm(x, gain):
    xf = x.astype(jnp.float32)
    xf = xf * lax.rsqrt(jnp.mean(xf * xf, axis=-1, keepdims=True) + EPS)
    return xf.astype(x.dtype) * gain

def modulate(h, shift, scale):
    return h * (1 + scale[:, None, :]) + shift[:, None, :]

def apply_rope(x, cos, sin):
    half = x.shape[-1] // 2
    x1, x2 = x[..., :half], x[..., half:]
    return jnp.concatenate([x1 * cos - x2 * sin, x1 * sin + x2 * cos], axis=-1)

def causal_probs(q_blk, k, q_start, scale):
    s = jnp.einsum('bqhd,bkhd->bhqk', q_blk, k).astype(jnp.float32) * scale
    q_pos = q_start + jnp.arange(q_blk.shape[1])
    k_pos = jnp.arange(k.shape[1])
    s = jnp.where(k_pos[None, :] <= q_pos[:, None], s, -jnp.inf)
    return jax.nn.softmax(s, axis=-1)

def sweep_query_blocks(body, q):
    B, S = q.shape[:2]
    nb = S // Q_BLOCK
    qb = jnp.moveaxis(q.reshape((B, nb, Q_BLOCK) + q.shape[2:]), 1, 0)
    starts = jnp.arange(nb, dtype=jnp.int32) * Q_BLOCK
    out = lax.map(lambda a: body(a[0], a[1]), (qb, starts))
    out = jnp.moveaxis(out, 0, 1)
    return out.reshape((B, S) + out.shape[3:])

def hgrn2_mixer(q_raw, f_raw, i_raw, g_raw, lb, o_gain):
    B, S, _ = q_raw.shape
    nc = S // HG_CHUNK
    f32 = jnp.float32
    lbf = lb.astype(f32)
    logf = jnp.logaddexp(jnp.log(lbf), jnp.log1p(-lbf) + jax.nn.log_sigmoid(f_raw.astype(f32)))
    k = -jnp.expm1(logf)
    q = jax.nn.silu(q_raw.astype(f32))
    v = i_raw.astype(f32)

    def to_chunks(t, d):
        t = t.reshape(B, nc, HG_CHUNK, HG_HEADS, d)
        return jnp.transpose(t, (1, 0, 3, 2, 4))

    qc, kc, vc, lfc = to_chunks(q, HG_DK), to_chunks(k, HG_DK), to_chunks(v, HG_DV), to_chunks(logf, HG_DK)
    tri = jnp.tril(jnp.ones((HG_CHUNK, HG_CHUNK), dtype=bool))[None, None, :, :, None]

    def step(state, inp):
        qt, kt, vt, lf = inp
        b = jnp.cumsum(lf, axis=2)
        o_inter = jnp.einsum('bhck,bhkv->bhcv', qt * jnp.exp(b), state)
        diff = b[:, :, :, None, :] - b[:, :, None, :, :]
        decay = jnp.exp(jnp.where(tri, diff, -jnp.inf))
        attn = jnp.einsum('bhtk,bhtsk,bhsk->bhts', qt, decay, kt)
        o_intra = jnp.einsum('bhts,bhsv->bhtv', attn, vt)
        b_last = b[:, :, -1:, :]
        new_state = jnp.exp(b_last[:, :, 0, :])[..., None] * state + \
            jnp.einsum('bhck,bhcv->bhkv', kt * jnp.exp(b_last - b), vt)
        return new_state, o_inter + o_intra

    state0 = jnp.zeros((B, HG_HEADS, HG_DK, HG_DV), f32)
    _, o = lax.scan(step, state0, (qc, kc, vc, lfc))
    o = jnp.transpose(o, (1, 0, 3, 2, 4)).reshape(B, S, HG_HEADS, HG_DV)
    o = rmsnorm(o, o_gain).astype(g_raw.dtype).reshape(B, S, HG_HEADS * HG_DV)
    return o * jax.nn.silu(g_raw)

def mla_mixer(c_q, c_kv, k_rope, q_norm_g, kv_norm_g, w_uq, w_ukv, qk_g, cos, sin):
    B, S, _ = c_q.shape
    q = (rmsnorm(c_q, q_norm_g) @ w_uq).reshape(B, S, MLA_HEADS, MLA_NOPE + MLA_ROPE)
    kv = (rmsnorm(c_kv, kv_norm_g) @ w_ukv).reshape(B, S, MLA_HEADS, MLA_NOPE + MLA_V)
    k_nope, v = kv[..., :MLA_NOPE], kv[..., MLA_NOPE:]
    k = jnp.concatenate([k_nope, jnp.broadcast_to(k_rope[:, :, None, :], (B, S, MLA_HEADS, MLA_ROPE))], axis=-1)
    q = rmsnorm(q, qk_g[0])
    k = rmsnorm(k, qk_g[1])
    q = jnp.concatenate([q[..., :MLA_NOPE], apply_rope(q[..., MLA_NOPE:], cos, sin)], axis=-1)
    k = jnp.concatenate([k[..., :MLA_NOPE], apply_rope(k[..., MLA_NOPE:], cos, sin)], axis=-1)
    scale = (MLA_NOPE + MLA_ROPE) ** -0.5

    def body(q_blk, start):
        p = causal_probs(q_blk, k, start, scale)
        return jnp.einsum('bhqk,bkhd->bqhd', p.astype(v.dtype), v)

    o = sweep_query_blocks(body, q)
    return o.reshape(B, S, MLA_HEADS * MLA_V)

def diff_mixer(q, k, v, qk_g, lam_p, o_g, lam_init):
    B, S, _ = q.shape
    q = rmsnorm(q.reshape(B, S, DIFF_HEADS, 2, DIFF_QK), qk_g[0])
    k = rmsnorm(k.reshape(B, S, DIFF_HEADS, 2, DIFF_QK), qk_g[1])
    v = v.reshape(B, S, DIFF_HEADS, DIFF_V)
    k1, k2 = k[:, :, :, 0], k[:, :, :, 1]
    lp = lam_p.astype(jnp.float32)
    lam = jnp.exp(jnp.sum(lp[0] * lp[1])) - jnp.exp(jnp.sum(lp[2] * lp[3])) + lam_init
    scale = DIFF_QK ** -0.5

    def body(q_blk, start):
        p1 = causal_probs(q_blk[:, :, :, 0], k1, start, scale)
        p2 = causal_probs(q_blk[:, :, :, 1], k2, start, scale)
        return jnp.einsum('bhqk,bkhd->bqhd', (p1 - lam * p2).astype(v.dtype), v)

    o = sweep_query_blocks(body, q)
    o = rmsnorm(o, o_g) * (1.0 - lam_init)
    return o.reshape(B, S, DIFF_HEADS * DIFF_V)

def swa_mixer(q, k, v, qk_g, sinks):
    B, S, _ = q.shape
    G = SWA_Q_HEADS // SWA_KV_HEADS
    W = SWA_WINDOW
    nb = S // W
    q = rmsnorm(q.reshape(B, S, SWA_KV_HEADS, G, HEAD_DIM), qk_g[0])
    k = rmsnorm(k.reshape(B, S, SWA_KV_HEADS, HEAD_DIM), qk_g[1])
    v = v.reshape(B, S, SWA_KV_HEADS, HEAD_DIM)

    def band(t):
        tp = jnp.pad(t, ((0, 0), (W, 0), (0, 0), (0, 0)))
        tb = tp.reshape(B, nb + 1, W, SWA_KV_HEADS, HEAD_DIM)
        return jnp.concatenate([tb[:, :-1], tb[:, 1:]], axis=2)

    kw, vw = band(k), band(v)
    qb = q.reshape(B, nb, W, SWA_KV_HEADS, G, HEAD_DIM)
    s = jnp.einsum('bnqhgd,bnkhd->bnhgqk', qb, kw).astype(jnp.float32) * HEAD_DIM ** -0.5
    qi = jnp.arange(W)[:, None]
    kj = jnp.arange(2 * W)[None, :]
    delta = qi + W - kj
    blk = jnp.arange(nb)[:, None, None]
    valid = (delta >= 0) & (delta < W) & (blk * W + kj[None] - W >= 0)
    s = jnp.where(valid[None, :, None, None], s, -jnp.inf)
    sink = jnp.broadcast_to(sinks.astype(jnp.float32).reshape(1, 1, SWA_KV_HEADS, G, 1, 1), s.shape[:-1] + (1,))
    p = jax.nn.softmax(jnp.concatenate([s, sink], axis=-1), axis=-1)[..., :-1]
    o = jnp.einsum('bnhgqk,bnkhd->bnqhgd', p.astype(v.dtype), vw)
    return o.reshape(B, S, SWA_Q_HEADS * HEAD_DIM)

def moe(h, router_w, router_bias, w_gate, w_up, w_down):
    B, S, _ = h.shape
    f32 = jnp.float32
    per = N_EXPERTS // N_GROUPS
    scores = jax.nn.sigmoid(jnp.einsum('bsd,de->bse', h, router_w).astype(f32))
    sel = scores + router_bias.astype(f32)
    grp = lax.top_k(sel.reshape(B, S, N_GROUPS, per), TOP_K)[0].sum(-1)
    g_idx = jnp.argmax(grp, axis=-1)
    in_grp = (jnp.arange(N_EXPERTS) // per)[None, None, :] == g_idx[..., None]
    _, e_idx = lax.top_k(jnp.where(in_grp, sel, -jnp.inf), TOP_K)
    w = jnp.take_along_axis(scores, e_idx, axis=-1)
    w = w / jnp.sum(w, axis=-1, keepdims=True)
    combine = jnp.sum(jax.nn.one_hot(e_idx, N_EXPERTS, dtype=f32) * w[..., None], axis=-2)
    hid = jax.nn.silu(jnp.einsum('bsd,edf->bsef', h, w_gate)) * jnp.einsum('bsd,edf->bsef', h, w_up)
    return jnp.einsum('bsef,bse,efd->bsd', hid, combine.astype(h.dtype), w_down)

def setup_inputs(seed: int = 0) -> dict:
    key = jax.random.key(seed)
    ks = jax.random.split(key, 32)
    f32 = jnp.float32
    L, D = DEPTH, D_MODEL

    def nrm(k, shape, scale):
        return jax.random.normal(k, shape, f32) * scale

    def gain(k, shape):
        return 1.0 + 0.02 * jax.random.normal(k, shape, f32)

    offs = jax.random.randint(ks[2], (BATCH, 1), 0, MAX_POS_OFFSET, dtype=jnp.int32)
    return {
        'x': nrm(ks[0], (BATCH, SEQ, D), 1.0),
        'c': nrm(ks[1], (BATCH, D), 1.0),
        'positions': offs + jnp.arange(SEQ, dtype=jnp.int32)[None, :],
        'ada_w': nrm(ks[3], (L, D, 6 * D), 0.5 * D ** -0.5),
        'ada_b': nrm(ks[4], (L, 6 * D), 0.02),
        'norm_mix': gain(ks[5], (L, D)),
        'norm_ffn': gain(ks[6], (L, D)),
        'w_in': nrm(ks[7], (L, D, N_IN), D ** -0.5),
        'hg_lb_logits': nrm(ks[8], (L, HG_HEADS * HG_DK), 1.0),
        'hg_onorm': gain(ks[9], (L, HG_DV)),
        'mla_q_norm': gain(ks[10], (L, MLA_Q_RANK)),
        'mla_kv_norm': gain(ks[11], (L, MLA_KV_RANK)),
        'mla_w_uq': nrm(ks[12], (L, MLA_Q_RANK, MLA_HEADS * (MLA_NOPE + MLA_ROPE)), MLA_Q_RANK ** -0.5),
        'mla_w_ukv': nrm(ks[13], (L, MLA_KV_RANK, MLA_HEADS * (MLA_NOPE + MLA_V)), MLA_KV_RANK ** -0.5),
        'mla_qk_norm': gain(ks[14], (L, 2, MLA_NOPE + MLA_ROPE)),
        'diff_qk_norm': gain(ks[15], (L, 2, DIFF_QK)),
        'diff_lam': nrm(ks[16], (L, 4, DIFF_QK), 0.1),
        'diff_onorm': gain(ks[17], (L, DIFF_V)),
        'swa_qk_norm': gain(ks[18], (L, 2, HEAD_DIM)),
        'swa_sinks': nrm(ks[19], (L, SWA_Q_HEADS), 1.0),
        'w_branch': nrm(ks[20], (L, N_BRANCH, BRANCH_W, D), BRANCH_W ** -0.5),
        'w_out': nrm(ks[21], (L, D, D), D ** -0.5),
        'router_w': nrm(ks[22], (D, N_EXPERTS), D ** -0.5),
        'router_bias': nrm(ks[23], (N_EXPERTS,), 0.01),
        'moe_w_gate': nrm(ks[24], (L, N_EXPERTS, D, D_FF_EXPERT), D ** -0.5),
        'moe_w_up': nrm(ks[25], (L, N_EXPERTS, D, D_FF_EXPERT), D ** -0.5),
        'moe_w_down': nrm(ks[26], (L, N_EXPERTS, D_FF_EXPERT, D), D_FF_EXPERT ** -0.5),
    }

def reference(x, c, positions, ada_w, ada_b, norm_mix, norm_ffn, w_in, hg_lb_logits, hg_onorm,
              mla_q_norm, mla_kv_norm, mla_w_uq, mla_w_ukv, mla_qk_norm, diff_qk_norm, diff_lam,
              diff_onorm, swa_qk_norm, swa_sinks, w_branch, w_out, router_w, router_bias,
              moe_w_gate, moe_w_up, moe_w_down):
    B, S, D = x.shape
    f32 = jnp.float32
    inv_freq = ROPE_BASE ** (-jnp.arange(0, MLA_ROPE, 2, dtype=f32) / MLA_ROPE)
    ang = positions.astype(f32)[..., None] * inv_freq
    cos = jnp.cos(ang)[:, :, None, :].astype(x.dtype)
    sin = jnp.sin(ang)[:, :, None, :].astype(x.dtype)
    lb_all = jnp.cumsum(jax.nn.softmax(hg_lb_logits.astype(f32), axis=0), axis=0)
    lb_all = lb_all - lb_all[0]
    c_act = jax.nn.silu(c)

    for l in range(DEPTH):
        mod = c_act @ ada_w[l] + ada_b[l]
        sh1, sc1, gt1, sh2, sc2, gt2 = jnp.split(mod, 6, axis=-1)
        h = modulate(rmsnorm(x, norm_mix[l]), sh1, sc1)
        proj = h @ w_in[l]
        (hq, hf, hi, hg, mcq, mckv, mkr, dq, dk, dv, sq, sk, sv, gates) = jnp.split(proj, SPLIT_POINTS, axis=-1)
        y_a = hgrn2_mixer(hq, hf, hi, hg, lb_all[l], hg_onorm[l])
        y_b = mla_mixer(mcq, mckv, mkr, mla_q_norm[l], mla_kv_norm[l], mla_w_uq[l], mla_w_ukv[l],
                        mla_qk_norm[l], cos, sin)
        lam_init = 0.8 - 0.6 * math.exp(-0.3 * l)
        y_c = diff_mixer(dq, dk, dv, diff_qk_norm[l], diff_lam[l], diff_onorm[l], lam_init)
        y_d = swa_mixer(sq, sk, sv, swa_qk_norm[l], swa_sinks[l])
        ys = jnp.stack([y_a, y_b, y_c, y_d], axis=2)
        branch = jnp.einsum('bsnw,nwd->bsnd', ys, w_branch[l])
        gate = jax.nn.sigmoid(gates.reshape(B, S, N_BRANCH, D))
        merged = jnp.sum(gate * branch, axis=2)
        x = x + gt1[:, None, :] * (merged @ w_out[l])
        h2 = modulate(rmsnorm(x, norm_ffn[l]), sh2, sc2)
        x = x + gt2[:, None, :] * moe(h2, router_w, router_bias, moe_w_gate[l], moe_w_up[l], moe_w_down[l])
    return x


_drawn_inputs = setup_inputs


def setup_inputs(seed=0):
    import zlib

    import numpy as np

    out = dict(_drawn_inputs(seed))
    spreads = {}
    factors = {'norm_mix': 2.833,
     'hg_lb_logits': 2.699,
     'hg_onorm': 4.308,
     'mla_q_norm': 8.0,
     'mla_kv_norm': 6.514,
     'mla_qk_norm': 6.731,
     'diff_qk_norm': 6.94,
     'diff_onorm': 10.546,
     'swa_qk_norm': 7.507,
     'swa_sinks': 27.79}
    for name, (base, spread) in spreads.items():
        noise = np.random.default_rng([zlib.crc32(name.encode()), seed]).standard_normal(out[name].shape)
        drawn = base * np.exp(spread * noise) if base else spread * noise
        out[name] = __import__('jax').numpy.asarray(drawn.astype(out[name].dtype))
    for name, factor in factors.items():
        out[name] = (out[name] * factor).astype(out[name].dtype)
    return out
```

```python
import math
from contextlib import ExitStack, contextmanager

import numpy as np

import concourse.bass as bass
from concourse import mybir
from concourse.alu_op_type import AluOpType as ALU

F32, I32 = mybir.dt.float32, mybir.dt.int32
ACT = mybir.ActivationFunctionType
AX = mybir.AxisListType.X

P = 128
D, S, DEPTH = 1024, 512, 2
NT, NC = S // P, D // P
EPS = 1e-6
HEADS, HD = 8, 64
QR, KVR, NOPE, ROPE = 256, 128, 64, 32
QKD = NOPE + ROPE
HALF = ROPE // 2
DH, DV = 4, 128
BW, NB = 512, 4
NE, NG, FF = 16, 4, 256
PER = NE // NG
SLOT = 2048
RING = 4
LEVELS = 7
NEG = -1e30
LN0 = -1e30

WIDTHS = (512, 512, 512, 512, QR, KVR, ROPE, 512, 512, 512, 512, 128, 128, NB * D)
COL = dict(zip("hq hf hi hg cq ckv kr dq dk dv sq sk sv gate".split(),
               (sum(WIDTHS[:i]) for i in range(len(WIDTHS)))))
N_IN = sum(WIDTHS)

ROWS = (("hg_onorm", 64), ("mla_q_norm", QR), ("mla_kv_norm", KVR), ("mla_qk_norm", 2 * QKD),
        ("diff_qk_norm", 128), ("diff_onorm", DV), ("swa_qk_norm", 128), ("swa_sinks", 8),
        ("diff_lam", 256))
ROW_AT = {}
for _n, _w in ROWS:
    ROW_AT[_n] = (sum(w for _, w in ROW_AT.values()), _w)
NROW = sum(w for _, w in ROWS)
NCOLP = 6 * NC + 2 * NC


PRIMED = "emptied handed slot_used sq_used qk_used attn_used tile_used added params_used comb_loaded qs_ready".split()


class Program:

    def __init__(self, eng, name, rate):
        self.eng, self.name, self.rate = eng, name, rate
        self.count, self.frames = {}, []

    def value(self, kind, sem):
        key = kind, sem.name
        v, fixed = None, self.count.get(key, 0) + (sem.name.rstrip("0123456789") in PRIMED)
        path = ()
        for loop, i, before in self.frames:
            path += (loop,)
            fixed += before.get(key, 0)
            r = self.rate.get((self.name, path, key), 0)
            if r:
                v = i * r if v is None else v + i * r
        if v is None:
            return fixed
        assert fixed > 0, key
        return v + fixed

    def mark(self, sem, n=1):
        key = "seen", sem.name
        self.count[key] = self.count.get(key, 0) + n

    def next(self, sem, n=1):
        self.mark(sem, n)
        return self.value("seen", sem)

    def so_far(self, sem):
        return self.value("seen", sem)

    def gives(self, sem, n=1):
        key = "sent", sem.name
        self.count[key] = self.count.get(key, 0) + n
        return n

    def given(self, sem):
        return self.value("sent", sem)

    @contextmanager
    def loop(self, name, n):
        with self.eng.Fori(0, n) as i:
            self.frames.append((name, i, self.count))
            self.count = {}
            yield i
            path = tuple(f[0] for f in self.frames)
            done, self.count = self.count, self.frames.pop()[2]
        for key, c in done.items():
            self.rate[self.name, path, key] = c
            self.count[key] = self.count.get(key, 0) + c * n


class Sweep:

    def __init__(self, kind, per_tile):
        self.kind, self.per_tile, self.units = kind, per_tile, NT * per_tile

    def tile(self, n):
        return n // self.per_tile

    def head(self, n):
        h = n % self.per_tile
        return (h % 2) * 4 + h // 2 if self.kind == "swa" else h

    def first(self, n):
        return n % self.per_tile == 0

    def last(self, n):
        return n % self.per_tile == self.per_tile - 1

    def banks(self, n):
        return (6, 7) if self.kind == "diff" else (6 + n % 2,)

    def blocks(self, n):
        t = self.tile(n)
        return list(range(max(t - 1, 0) if self.kind == "swa" else 0, t + 1))


MLA, DIFF, SWA = Sweep("mla", HEADS), Sweep("diff", DH), Sweep("swa", HEADS)

SCHEDULE = [("hg_norm", 0), ("c", 0), ("c", 1), ("hg_y", 0), ("c_norm", 0), ("c", 2), ("c_turn", 0),
            ("up", 0), ("c", 3), ("up", 1), ("turn", 0), ("c", 4), ("up", 2), ("turn", 1), ("up", 3),
            ("turn", 2), ("c", 5), ("turn", 3), ("sweep", MLA),
            ("dif_norm", 0), ("d", 0), ("dif_norm", 1), ("d", 1), ("dif_norm", 2), ("d", 2),
            ("dif_norm", 3), ("mla_y", 0), ("swa_norm", 0), ("swa_norm", 1), ("swa_norm", 2),
            ("swa_norm", 3), ("dif_turn", 0), ("swa_turn", 0), ("sweep", DIFF), ("dif_post", 0),
            ("sweep", SWA), ("dif_y", 0), ("swa_y", 0)]


def build(nc, a, out, scratch, rate):
    with ExitStack() as ctx:
        def sb(name, *shape, dt=F32):
            return ctx.enter_context(nc.sbuf_tensor(name, [P, *shape], dt))

        ring = sb("ring", RING, SLOT)
        X = sb("X", NC, S)
        H = sb("H", NC, S)
        M16 = sb("M16", 4096)
        Y = sb("Y", NB, NT, S)
        TM = sb("TM", NT, 1024)
        CM = sb("CM", NT, 416)
        DQK = sb("DQK", NT, 1024)
        DVt = sb("DVt", NT, 512)
        SQKV = sb("SQKV", NT, 768)
        SC = sb("SC", 6, S)
        ident = sb("ident", P)
        ones = sb("ones", P)
        cmask = sb("cmask", P)
        swmask = sb("swmask", 2 * P)
        lmask = sb("lmask", LEVELS, P)
        rows = sb("rows", NROW)
        bias_row = sb("bias_row", NE)
        pcols = sb("pcols", P)
        colT = sb("colT", NCOLP)
        mod = sb("mod", 6 * NC)
        gain = sb("gain", NC)
        cact = sb("cact", NC)
        rw = sb("rw", NC, NE)
        cosT = sb("cosT", NT, HALF)
        sinT = sb("sinT", NT, HALF)
        ang = sb("ang", NT, HALF)
        angk = sb("angk", 2, NT, HALF)
        ifr = sb("ifr", HALF)
        posi = sb("posi", NT, dt=I32)
        posf = sb("posf", NT)
        lbz = sb("lbz", 2, NT)
        lbt = sb("lbt", DEPTH, 2 * NT)
        lbc = sb("lbc", 2 * NT)
        lbw = sb("lbw", 2, NT)
        litab = sb("litab", DEPTH, 2)
        lic = sb("lic", 2)
        lamp = sb("lamp", 2, HD)
        lams = sb("lams", 4)
        neglam = sb("neglam", 1)
        consts = sb("consts", 2)
        ssq = sb("ssq", 16)
        rsq = sb("rsq", 16)
        edec = sb("edec", NT)
        nmax = sb("nmax", 2, 2)
        lsum = sb("lsum", 2, HEADS)
        lrec = sb("lrec", HEADS)
        esink = sb("esink", 2, HEADS)
        nsink = sb("nsink", HEADS)
        dl = sb("dl", 2, 2)
        dr = sb("dr", 2)
        rt = sb("rt", 6, NT * NE)
        rg = sb("rg", 6, NT * NG)
        wexp = sb("wexp", NE)
        wgrp = sb("wgrp", NG)

        ps = ctx.enter_context(nc.psum_tensor("ps", [P, 8, 512], F32))
        def signal(name):
            return ctx.enter_context(nc.semaphore(name))

        def signals(name, n=2):
            return [signal(f"{name}{i}") for i in range(n)]

        filled, emptied, handed = (signals(n, 8) for n in ("filled", "emptied", "handed"))
        slot_loaded, slot_used = (signals(n, RING) for n in ("slot_loaded", "slot_used"))
        (sq_ready, sq_used, d_ready, e_ready, qs_ready, ks_ready, qk_used, attn_used, tile_used,
         added) = (signals(n) for n in (
             "sq_ready", "sq_used", "d_ready", "e_ready", "qs_ready", "ks_ready", "qk_used",
             "attn_used", "tile_used", "added"))
        (x_loaded, router_loaded, c_loaded, positions_loaded, lb_loaded, bias_loaded, rows_loaded,
         cols_loaded, comb_stored, comb_loaded, out_stored) = (signal(n) for n in (
             "x_loaded", "router_loaded", "c_loaded", "positions_loaded", "lb_loaded", "bias_loaded",
             "rows_loaded", "cols_loaded", "comb_stored", "comb_loaded", "out_stored"))
        vector_step, scalar_step, pool_step = (
            signal(n) for n in ("vector_step", "scalar_step", "pool_step"))
        (constants_ready, lbdiff_ready, lbln_ready, angles_ready, rope_ready, cact_ready,
         params_used, rows_ready, lamsum_ready, lamexp_ready, h_ready, f_ready, ln_ready, logk_ready,
         k_ready, logt_ready, logaddexp_ready, b_ready, qin_ready, edec_ready, squares_ready,
         sums_ready, rms_ready, normed, gained, rowmax_ready, probs_ready, comb_ready,
         weighted) = (signal(n) for n in (
             "constants_ready", "lbdiff_ready", "lbln_ready", "angles_ready", "rope_ready",
             "cact_ready", "params_used", "rows_ready", "lamsum_ready", "lamexp_ready", "h_ready",
             "f_ready", "ln_ready", "logk_ready", "k_ready", "logt_ready", "logaddexp_ready",
             "b_ready", "qin_ready", "edec_ready", "squares_ready", "sums_ready", "rms_ready",
             "normed", "gained", "rowmax_ready", "probs_ready", "comb_ready", "weighted"))
        waited = {n: signal(f"waited_{n}") for n in ("sp", "pe", "dve", "pool")}

        block = ctx.enter_context(nc.Block())

        def row(name, lo=0, n=None):
            at, w = ROW_AT[name]
            return rows[:, at + lo:at + lo + (w if n is None else n)]

        def bank(b, n=512):
            return ps[:, b, 0:n]

        def bank3(b, k, n):
            return ps[:, b, 0:k * n].rearrange("p (k n) -> p k n", k=k)

        def tt(t):
            return slice(t * P, (t + 1) * P)

        def heads(ap, n):
            return ap.rearrange("p (h d) -> p h d", h=n)

        def flat(ap):
            return ap.rearrange("p a b -> p (a b)")

        def spread(ap, n):
            return ap.unsqueeze(2).to_broadcast([P, ap.shape[1], n])

        def repeat(ap, n):
            return ap.unsqueeze(1).to_broadcast([P, n, ap.shape[1]])

        def pick(ap, i):
            return ap[:, bass.ds(i, 1)].rearrange("p a s -> p (a s)")

        M3 = M16[:, :].rearrange("p (c s) -> p c s", c=NC)
        xin = M16[:, :].rearrange("p (t d) -> p t d", t=NT)
        hgQ, hgB, hgK = M3[:, 0:4], M3[:, 4:8], Y[:, 2]
        hgO = Y[:, 3]
        hgE = [Y[:, 0, i] for i in range(2)]
        hgQs = [Y[:, 0, 2 + i] for i in range(2)]
        hgKs = [Y[:, 1, i] for i in range(2)]
        hgQin = [Y[:, 1, 2 + i] for i in range(2)]
        attnT = [[heads(DQK[:, i, h * S:(h + 1) * S], NT) for h in range(2)] for i in range(2)]
        KdT = [heads(DQK[:, 2, i * S:(i + 1) * S], NT) for i in range(2)]
        state = [heads(DQK[:, 3, i * S:(i + 1) * S], NT) for i in range(2)]
        cT = Y[:, 3]
        sqkv = flat(SQKV[:, :, :])
        qk_tile = [sqkv[:, i * 1536:(i + 1) * 1536] for i in range(2)]
        TM8 = flat(TM[:, :, :]).rearrange("p (h s) -> p h s", h=8)
        mlaQ, mlaK, mlaV = TM8, M3, Y[:, 2]
        difQ, difK = M3[:, 0:4], M3[:, 4:8]
        swaQ, swaK = TM8[:, 0:4], TM8[:, 4]
        swa_sq = flat(TM8[:, 5:7])[:, 0:640]
        sc = flat(SC[:, :, :])
        y_tok = {"mla": Y[:, 3], "diff": flat(DQK[:, 0:2]).rearrange("p (t s) -> p t s", t=NT),
                 "swa": flat(DQK[:, 2:4]).rearrange("p (t s) -> p t s", t=NT)}
        probs = [[SC[:, 2 * i + j] for j in range(2)] for i in range(2)]
        probsT = [heads(SC[:, 4 + i], NT) for i in range(2)]
        merged, hid = M3, M3
        comb = Y[:, :, :, :].rearrange("p b t s -> p (b t) s")
        combT = SC[0:NE, 4]

        def swa_cols(t, u):
            if u == 2:
                return SQKV[:, t, 512:768]
            return SQKV[:, t, 0:512].rearrange("p (a g d) -> p g a d", a=4, g=2)[:, u]

        def norm_of(step, t):
            if step == "hg_norm":
                return hgO[:, t], SC[:, 0], HEADS, HD
            if step == "c_norm":
                w, at = ((QR, 0), (KVR, QR))[t]
                return CM[:, :, at:at + w], sc[:, 0:NT * w], NT, w
            if step == "up":
                return qk_tile[t % 2], sc[:, 0:1536], 2 * HEADS, QKD
            if step == "dif_norm":
                return DQK[:, t], sc[:, 0:1024], 16, HD
            if step == "swa_norm":
                return SQKV[:, t, 0:640], swa_sq, 10, HD
            return y_tok["diff"][:, t], SC[:, 0], DH, DV

        @block.sync
        def _(eng):
            p = Program(eng, "sp", rate)

            def alone():
                eng.sem_inc(waited["sp"], 1)

            xd = a["x"].rearrange("b (t p) d -> p (b t) d", p=P)
            for t in range(NT):
                eng.dma_start(xin[:, t], xd[:, t]).then_inc(x_loaded, p.gives(x_loaded, 16))
            eng.dma_start(rw[:, :, :], a["router_w"].rearrange("(k p) e -> p k e", p=P)).then_inc(
                router_loaded, p.gives(router_loaded, 16))
            pos = [0]

            def load(parts):
                j = pos[0] % RING
                pos[0] += 1
                eng.wait_ge(slot_used[j], p.so_far(slot_used[j]))
                alone()
                for dst, src in parts(j):
                    eng.dma_start(dst, src).then_inc(slot_loaded[j], p.gives(slot_loaded[j], 16))
                p.mark(slot_used[j])

            def layer(name, i):
                ap = a[name][bass.ds(i, 1)]
                return ap.rearrange("a b c -> (a b) c") if len(ap.shape) == 3 else ap

            def cols(w, c0, n):
                def parts(j):
                    src = w.rearrange("(k p) n -> p k n", p=P)
                    dst = ring[:, j, 0:NC * n].rearrange("p (k n) -> p k n", k=NC)
                    for h in range(4):
                        yield dst[:, 2 * h:2 * h + 2], src[:, 2 * h:2 * h + 2, bass.ds(c0, n)]
                return parts

            def uq(w):
                def parts(j):
                    for h in range(4):
                        k, c = h // 2, (h % 2) * 384
                        yield ring[:, j, k * 768 + c:k * 768 + c + 384], w[k * P:(k + 1) * P, c:c + 384]
                return parts

            def ukv(w):
                def parts(j):
                    for h in range(4):
                        yield ring[:, j, h * 256:(h + 1) * 256], w[:, h * 256:(h + 1) * 256]
                return parts

            with p.loop("layer", DEPTH) as l:
                eng.wait_ge(params_used, p.so_far(params_used))
                p.mark(params_used)
                for name, w in ROWS:
                    src = a[name][bass.ds(l, 1)]
                    if len(src.shape) == 3:
                        src = src.rearrange("a b c -> a (b c)")
                    eng.dma_start(row(name), src.partition_broadcast(P).rearrange("p a w -> p (a w)")).then_inc(
                        rows_loaded, p.gives(rows_loaded, 16))
                for lo, name, n in ((0, "ada_b", 48), (48, "norm_mix", NC), (56, "norm_ffn", NC)):
                    eng.dma_start(pcols[lo:lo + n, :],
                                         a[name][bass.ds(l, 1)].rearrange("a (k p) -> (a k) p", p=P)).then_inc(
                        cols_loaded, p.gives(cols_loaded, 16))
                w_in = layer("w_in", l)
                with p.loop("ada", 6) as s:
                    for u in range(4):
                        load(cols(layer("ada_w", l), s * 1024 + u * 256, 256))
                for c in ("hf", "hq", "hi", "hg"):
                    for u in range(2):
                        load(cols(w_in, COL[c] + u * 256, 256))
                load(cols(w_in, COL["cq"], 256))
                load(cols(w_in, COL["ckv"], KVR + ROPE))
                for u in range(3):
                    load(cols(w_in, COL["dq"] + u * 256, 256))
                load(uq(layer("mla_w_uq", l)))
                load(ukv(layer("mla_w_ukv", l)))
                for u in range(3, 6):
                    load(cols(w_in, COL["dq"] + u * 256, 256))
                for u in range(3):
                    load(cols(w_in, COL["sq"] + u * 256, 256))
                with p.loop("merge", 2) as g:
                    for b in range(NB):
                        for u in range(2):
                            load(cols(w_in, g * 512 + (COL["gate"] + b * D + u * 256), 256))

                        def branch(j, b=b):
                            src = a["w_branch"][bass.ds(l, 1), b].rearrange("a (k p) n -> p (a k) n", p=P)
                            for h in range(4):
                                yield ring[:, j, h * 512:(h + 1) * 512], src[:, h, bass.ds(g * 512, 512)]
                        load(branch)
                for u in range(4):
                    load(cols(layer("w_out", l), u * 256, 256))
                with p.loop("moe", NG) as g:
                    for e in range(4):
                        for name in ("moe_w_gate", "moe_w_up"):
                            w = a[name].rearrange("l e k n -> (l e) k n")[bass.ds(l * NE + g * 4 + e, 1)]
                            load(cols(w.rearrange("a k n -> (a k) n"), 0, FF))
                    wd = a["moe_w_down"].rearrange("l e (j p) n -> (l e) p j n", p=P)
                    for u in range(4):
                        def down(j, u=u):
                            dst = ring[:, j].rearrange("p (e j n) -> p e j n", e=4, j=2)
                            for e in range(4):
                                src = wd[bass.ds(l * NE + g * 4 + e, 1)].rearrange("a p j n -> p (a j) n")
                                yield dst[:, e], src[:, :, u * 256:(u + 1) * 256]
                        load(down)
                pos[0] += (-pos[0]) % RING

        @block.tensor
        def _(eng):
            p = Program(eng, "pe", rate)
            for sem in (*slot_used, *sq_used, *qk_used, *attn_used, *tile_used):
                eng.sem_inc(sem, 1)

            def alone():
                eng.sem_inc(waited["pe"], 1)

            owed = []
            pos = [0]

            def later(sem):
                owed.append(sem)

            def free(b):
                eng.wait_ge(emptied[b], p.so_far(emptied[b]))
                eng.wait_ge(handed[b], p.so_far(handed[b]))

            def mm(o, lhsT, rhs, start=True, stop=True, last=False, transpose=False):
                if transpose:
                    ins = nc.tensor.transpose(o, lhsT, rhs)
                else:
                    ins = nc.tensor.matmul(o, lhsT, rhs, start=start, stop=stop)
                if owed and not last:
                    ins.then_inc(owed[0], p.gives(owed.pop(0)))
                return ins

            def turn(o, src, k=P, last=False):
                return mm(o, src, ident[0:k, 0:k], last=last, transpose=True)

            @contextmanager
            def loop(name, n):
                def settle():
                    while owed:
                        turn(ps[0:32, 7, 0:32], ident[0:32, 0:32], k=32)

                free(7)
                alone()
                settle()
                with p.loop(name, n) as i:
                    yield i
                    settle()

            def slot():
                j = pos[0] % RING
                pos[0] += 1
                eng.wait_ge(slot_loaded[j], p.next(slot_loaded[j], 64))
                return j

            def w3(j, n):
                return ring[:, j, 0:NC * n].rearrange("p (k n) -> p k n", k=NC)

            def tokens(n, banks, bys):
                j = slot()
                w = w3(j, n)
                for t in range(NT):
                    b = banks[t]
                    free(b)
                    for k in range(NC):
                        last = k == NC - 1
                        ins = mm(bank(b, n), H[:, k, tt(t)], w[:, k], k == 0, k == NC - 1, last=last)
                        if last:
                            ins.then_inc(filled[b], p.gives(filled[b]))
                            p.mark(bys[t][b])
                later(slot_used[j])

            def features(banks, bys=None):
                j = slot()
                w = w3(j, 256)
                for m in range(2):
                    b = banks[m]
                    free(b)
                    for k in range(NC):
                        last = k == NC - 1
                        ins = mm(bank(b), w[:, k, tt(m)], H[:, k], k == 0, k == NC - 1, last=last)
                        if last:
                            ins.then_inc(filled[b], p.gives(filled[b]))
                            p.mark((bys or (emptied,) * 2)[m][b])
                later(slot_used[j])

            eng.wait_ge(constants_ready, p.next(constants_ready))
            eng.wait_ge(x_loaded, p.next(x_loaded, 64))
            for c in range(NC):
                free(c % 2)
                for t in range(NT):
                    last = t == NT - 1
                    ins = turn(ps[:, c % 2, tt(t)], xin[:, t, tt(c)], last=last)
                    if last:
                        ins.then_inc(filled[c % 2], p.gives(filled[c % 2]))
                        p.mark((handed if c == NC - 1 else emptied)[c % 2])
            eng.wait_ge(router_loaded, p.next(router_loaded, 16))
            eng.wait_ge(cact_ready, p.next(cact_ready))

            def feature_norm():
                free(2)
                for c in range(NC):
                    eng.wait_ge(sq_ready[c % 2], p.next(sq_ready[c % 2]))
                    last = c == NC - 1
                    ins = mm(bank(2), ones[:, :], SC[:, c % 2], c == 0, c == NC - 1, last=last)
                    if last:
                        ins.then_inc(filled[2], p.gives(filled[2]))
                        p.mark(handed[2])
                    later(sq_used[c % 2])

            def y_turn(src, br):
                for t in range(NT):
                    b = 2 + t % 2
                    free(b)
                    if br in (0, 2):
                        eng.wait_ge(gained, p.next(gained))
                    else:
                        eng.wait_ge(emptied[t % 2], p.so_far(emptied[t % 2]))
                    for k in range(4):
                        last = k == 3
                        ins = turn(ps[:, b, tt(k)], src[:, t, tt(k)], last=last)
                        if last:
                            ins.then_inc(filled[b], p.gives(filled[b]))
                            p.mark(emptied[b])

            def levels(pr):
                i = (9 * pr) % 2
                eng.wait_ge(ks_ready[i], p.next(ks_ready[i]))
                free(2)
                for c in range(NT):
                    last = c == 3
                    ins = turn(ps[:, 2, tt(c)], hgKs[i][:, tt(c)], last=last)
                    if last:
                        ins.then_inc(filled[2], p.gives(filled[2]))
                        p.mark(emptied[2])
                later(qk_used[i])
                for lv in range(LEVELS + 1):
                    if lv:
                        i = (9 * pr + lv) % 2
                        eng.wait_ge(qs_ready[i], p.next(qs_ready[i]))
                        eng.wait_ge(ks_ready[i], p.next(ks_ready[i]))
                        q, k = hgQs[i], hgKs[i]
                    else:
                        q, k = hgQ[:, pr], hgK[:, pr]
                    for hp in range(2):
                        b = (lv % 2) * 4 + hp
                        free(b)
                        for c in range(NT):
                            r = slice(hp * HD, (hp + 1) * HD)
                            last = c == 3
                            ins = mm(ps[:, b, tt(c)], k[r, tt(c)], q[r, tt(c)], last=last)
                            if last:
                                ins.then_inc(filled[b], p.gives(filled[b]))
                                p.mark(emptied[b])
                    if lv:
                        later(qk_used[i])
                    if lv == 4:
                        eng.wait_ge(emptied[2], p.so_far(emptied[2]))
                        free(0)
                        for c in range(3):
                            last = c == 2
                            ins = mm(ps[:, 0, tt(c)], KdT[pr % 2][:, c], TM[:, c, tt(pr)], last=last)
                            if last:
                                ins.then_inc(filled[0], p.gives(filled[0]))
                                p.mark(emptied[0])

            def chunk_outputs(pr):
                for b in (0, 1, 4, 5):
                    eng.wait_ge(emptied[b], p.so_far(emptied[b]))
                eng.wait_ge(qin_ready, p.next(qin_ready))
                b = 6 + pr % 2
                free(b)
                for c in range(NT):
                    o = ps[:, b, tt(c)]
                    if c:
                        mm(o, hgQin[pr % 2][:, tt(c)], state[pr % 2][:, c], True, False)
                    for h in range(2):
                        last = c == 3 and h == 1
                        ins = mm(o[:, h * HD:(h + 1) * HD], attnT[pr % 2][h][:, c], TM[:, c, pr * P + h * HD:pr * P + (h + 1) * HD], c == 0, c == 0 or h == 1, last=last)
                        if last:
                            ins.then_inc(filled[b], p.gives(filled[b]))
                            p.mark(emptied[b])
                later(attn_used[pr % 2])

            held = {}

            def up(t):
                if t == 0:
                    held["uq"], held["ukv"] = slot(), slot()
                wq = ring[:, held["uq"], 0:1536].rearrange("p (k n) -> p k n", k=2)
                wkv = ring[:, held["ukv"], 0:1024]
                for f in range(2):
                    free(f)
                    for k in range(2):
                        last = k == 1
                        ins = mm(bank(f, 384), cT[:, k, tt(t)], wq[:, k, f * 384:(f + 1) * 384], k == 0, k == 1, last=last)
                        if last:
                            ins.then_inc(filled[f], p.gives(filled[f]))
                            p.mark((emptied, handed)[f][f])
                for f in range(2):
                    free(6 + f)
                    mm(bank(6 + f), cT[:, 2, tt(t)], wkv[:, f * 512:(f + 1) * 512], last=True).then_inc(
                        filled[6 + f], p.gives(filled[6 + f]))
                    p.mark(emptied[6 + f])
                if t == 3:
                    later(slot_used[held['uq']])
                    later(slot_used[held['ukv']])

            def mla_turn(t):
                qk = heads(qk_tile[t % 2], 2 * HEADS)
                eng.wait_ge(gained, p.next(gained))
                for f in range(4):
                    b = 2 + f % 2
                    free(b)
                    for h in range(4):
                        last = h == 3
                        ins = turn(ps[0:QKD, b, tt(h)], qk[:, 4 * f + h], last=last)
                        if last:
                            ins.then_inc(filled[b], p.gives(filled[b]))
                            p.mark(emptied[b])
                later(tile_used[t % 2])

            def scores(s, n):
                t, h, kt = s.tile(n), s.head(n), s.blocks(n)
                keys = slice(kt[0] * P, (t + 1) * P)
                w = len(kt) * P
                if s.kind == "mla":
                    parts = [(mlaQ[0:QKD, h, tt(t)], mlaK[0:QKD, h, keys])]
                elif s.kind == "diff":
                    parts = [(difQ[r, h, tt(t)], difK[r, h, keys]) for r in (slice(0, HD), slice(HD, P))]
                else:
                    r = slice((h // 4) * HD, (h // 4 + 1) * HD)
                    parts = [(swaQ[r, h % 4, tt(t)], swaK[r, keys])]
                for b, (q, k) in zip(s.banks(n), parts):
                    free(b)
                    mm(bank(b, w), q, k, last=True).then_inc(filled[b], p.gives(filled[b]))
                    p.mark((handed if s.kind == "diff" else emptied)[b])

            def turn_probs(s, n):
                if s.kind == "diff":
                    eng.wait_ge(probs_ready, p.next(probs_ready))
                else:
                    eng.wait_ge(emptied[s.banks(n)[0]], p.so_far(emptied[s.banks(n)[0]]))
                b = 2 + n % 2
                free(b)
                kt = s.blocks(n)
                for i in range(len(kt)):
                    last = i == len(kt) - 1
                    ins = turn(ps[:, b, tt(i)], probs[n % 2][0][:, tt(i)], last=last)
                    if last:
                        ins.then_inc(filled[b], p.gives(filled[b]))
                        p.mark(emptied[b])

            def values(s, n):
                t, h, kt = s.tile(n), s.head(n), s.blocks(n)
                eng.wait_ge(emptied[2 + n % 2], p.so_far(emptied[2 + n % 2]))
                b = t % 2
                if s.first(n):
                    free(b)
                d = DV if s.kind == "diff" else HD
                for i, k in enumerate(kt):
                    v = {"mla": lambda: mlaV[:, k, h * d:(h + 1) * d],
                         "diff": lambda: DVt[:, k, h * d:(h + 1) * d],
                         "swa": lambda: SQKV[:, k, 640 + (h // 4) * d:640 + (h // 4 + 1) * d]}[s.kind]()
                    end = i == len(kt) - 1
                    last = end and s.last(n)
                    ins = mm(ps[:, b, h * d:(h + 1) * d], probsT[n % 2][:, i], v, i == 0, end, last=last)
                    if last:
                        ins.then_inc(filled[b], p.gives(filled[b]))
                        p.mark((handed if s.kind == "diff" else emptied)[b])

            def sweep(s):
                for n in range(s.units + 2):
                    if n < s.units:
                        scores(s, n)
                    if 1 <= n <= s.units:
                        turn_probs(s, n - 1)
                    if n >= 2:
                        values(s, n - 2)

            half = (emptied,) * 4

            def do(step, i):
                if step in ("c", "d"):
                    tokens(256, (0, 2, 1, 3), half)
                elif step == "hg_y":
                    y_turn(hgO, 0)
                elif step == "c_turn":
                    eng.wait_ge(gained, p.next(gained, 2))
                    for t in range(NT):
                        b = 2 + t % 2
                        free(b)
                        for k in range(3):
                            last = k == 2
                            ins = turn(ps[:, b, tt(k)], CM[:, t, tt(k)], last=last)
                            if last:
                                ins.then_inc(filled[b], p.gives(filled[b]))
                                p.mark(emptied[b])
                elif step == "up":
                    up(i)
                elif step == "turn":
                    mla_turn(i)
                elif step == "mla_y":
                    y_turn(y_tok["mla"], 1)
                elif step == "dif_turn":
                    eng.wait_ge(gained, p.next(gained, 4))
                    for t in range(NT):
                        for f in range(2):
                            free(2 + f)
                            for k in range(4):
                                last = k == 3
                                ins = turn(ps[:, 2 + f, tt(k)], DQK[:, t, f * 512 + k * P:f * 512 + (k + 1) * P], last=last)
                                if last:
                                    ins.then_inc(filled[2 + f], p.gives(filled[2 + f]))
                                    p.mark(emptied[2 + f])
                elif step == "swa_turn":
                    eng.wait_ge(gained, p.next(gained, 4))
                    for t in range(NT):
                        free(2)
                        for k in range(4):
                            last = k == 3
                            ins = turn(ps[:, 2, tt(k)], SQKV[:, t, tt(k)], last=last)
                            if last:
                                ins.then_inc(filled[2], p.gives(filled[2]))
                                p.mark(emptied[2])
                        free(3)
                        turn(ps[:, 3, 0:P], SQKV[:, t, 512:640], last=True).then_inc(
                            filled[3], p.gives(filled[3]))
                        p.mark(emptied[3])
                elif step == "sweep":
                    sweep(i)
                elif step == "dif_y":
                    y_turn(y_tok["diff"], 2)
                elif step == "swa_y":
                    y_turn(y_tok["swa"], 3)

            with loop("layer", DEPTH):
                free(0)
                eng.wait_ge(cols_loaded, p.next(cols_loaded, 48))
                alone()
                turn(ps[:, 0, 0:NCOLP], pcols[0:NCOLP, :], k=NCOLP, last=True).then_inc(
                    filled[0], p.gives(filled[0]))
                p.mark(emptied[0])
                feature_norm()
                with loop("ada", 6):
                    free(1)
                    for u in range(4):
                        j = slot()
                        w = w3(j, 256)
                        for m in range(2):
                            for k in range(NC):
                                last = (u, m, k) == (3, 1, NC - 1)
                                ins = mm(ps[:, 1, 2 * u + m:2 * u + m + 1], w[:, k, tt(m)], cact[:, k:k + 1], k == 0, k == NC - 1, last=last)
                                if last:
                                    ins.then_inc(filled[1], p.gives(filled[1]))
                                    p.mark(emptied[1])
                        later(slot_used[j])
                eng.wait_ge(h_ready, p.next(h_ready, NC))
                for u in range(2):
                    features((0, 1), (emptied, emptied))
                for u in range(2):
                    features((2, 3))
                for u in range(2):
                    tokens(256, (0, 2, 1, 3), half)
                for u in range(2):
                    tokens(256, (2, 3, 2, 3), half)
                for n in (256, KVR + ROPE):
                    tokens(n, (0, 2, 1, 3), half)
                eng.wait_ge(k_ready, p.next(k_ready))
                for pr in range(4):
                    levels(pr)
                    chunk_outputs(pr)
                for step, i in SCHEDULE:
                    do(step, i)
                for b in (2, 3):
                    eng.wait_ge(emptied[b], p.so_far(emptied[b]))
                    alone()
                with loop("merge", 2):
                    for br in range(NB):
                        jg = [slot(), slot()]
                        jb = slot()
                        wb = ring[:, jb].rearrange("p (k n) -> p k n", k=4)
                        for j in range(4):
                            free(2 + j % 2)
                            w = w3(jg[j // 2], 256)
                            for k in range(NC):
                                last = k == NC - 1
                                ins = mm(bank(2 + j % 2), w[:, k, tt(j % 2)], H[:, k], k == 0, k == NC - 1, last=last)
                                if last:
                                    ins.then_inc(filled[2 + j % 2], p.gives(filled[2 + j % 2]))
                                    p.mark(handed[2 + j % 2])
                            if j % 2:
                                later(slot_used[jg[j // 2]])
                            free(j % 2)
                            for k in range(4):
                                last = k == 3
                                ins = mm(bank(j % 2), wb[:, k, tt(j)], Y[:, br, k], k == 0, k == 3, last=last)
                                if last:
                                    ins.then_inc(filled[j % 2], p.gives(filled[j % 2]))
                                    p.mark((handed if br else emptied)[j % 2])
                            if br:
                                p.mark(added[j % 2])
                        later(slot_used[jb])
                eng.wait_ge(added[0], p.so_far(added[0]))
                eng.wait_ge(added[1], p.so_far(added[1]))
                for u in range(4):
                    j = slot()
                    w = w3(j, 256)
                    for m in range(2):
                        free(m)
                        for k in range(NC):
                            last = k == NC - 1
                            ins = mm(bank(m), w[:, k, tt(m)], merged[:, k], k == 0, k == NC - 1, last=last)
                            if last:
                                ins.then_inc(filled[m], p.gives(filled[m]))
                                p.mark((handed if (u, m) == (3, 1) else emptied)[m])
                    later(slot_used[j])
                feature_norm()
                eng.wait_ge(h_ready, p.next(h_ready, NC))
                free(6)
                for t in range(NT):
                    for k in range(NC):
                        last = (t, k) == (NT - 1, NC - 1)
                        ins = mm(ps[:, 6, t * NE:(t + 1) * NE], H[:, k, tt(t)], rw[:, k], k == 0, k == NC - 1, last=last)
                        if last:
                            ins.then_inc(filled[6], p.gives(filled[6]))
                            p.mark(handed[6])
                eng.wait_ge(comb_ready, p.next(comb_ready))
                free(7)
                for t in range(NT):
                    last = t == NT - 1
                    ins = turn(ps[0:NE, 7, tt(t)], rt[:, 4, t * NE:(t + 1) * NE], last=last)
                    if last:
                        ins.then_inc(filled[7], p.gives(filled[7]))
                        p.mark(emptied[7])
                with loop("moe", NG):
                    for e in range(4):
                        js = [slot(), slot()]
                        for m in range(2):
                            for which in range(2):
                                b = (2 if which == 0 else 0) + m
                                free(b)
                                for k in range(NC):
                                    last = k == NC - 1
                                    ins = mm(bank(b), w3(js[which], 256)[:, k, tt(m)], H[:, k], k == 0, k == NC - 1, last=last)
                                    if last:
                                        ins.then_inc(filled[b], p.gives(filled[b]))
                                        p.mark((handed, emptied)[which][b])
                        for j in js:
                            later(slot_used[j])
                    for b in (0, 1):
                        eng.wait_ge(emptied[b], p.so_far(emptied[b]))
                    for u in range(4):
                        j = slot()
                        w = w3(j, 256)
                        for m in range(2):
                            free(4 + m)
                            for k in range(NC):
                                last = k == NC - 1
                                ins = mm(bank(4 + m), w[:, k, tt(m)], hid[:, k], k == 0, k == NC - 1, last=last)
                                if last:
                                    ins.then_inc(filled[4 + m], p.gives(filled[4 + m]))
                                    p.mark((handed if (u, m) == (3, 1) else emptied)[4 + m])
                        later(slot_used[j])
                pos[0] += (-pos[0]) % RING
            for b in (4, 5):
                free(b)
            for t in range(NT):
                for f in range(2):
                    free(f)
                    for k in range(4):
                        last = k == 3
                        ins = turn(ps[:, f, tt(k)], X[:, 4 * f + k, tt(t)], last=last)
                        if last:
                            ins.then_inc(filled[f], p.gives(filled[f]))
                            p.mark((emptied, handed)[f][f])

        @block.scalar
        def _(eng):
            p = Program(eng, "act", rate)
            for b in (2, 3, 6, 7):
                eng.sem_inc(emptied[b], 1)
                eng.sem_inc(handed[b], 1)
            eng.sem_inc(comb_loaded, 1)
            act = nc.scalar.activation




            with nc.allow_non_contiguous_dma(reason="a few hundred parameters, once"):
                eng.dma_start(cact[:, :], a["c"].rearrange("b (k p) -> p (b k)", p=P)).then_inc(
                    c_loaded, p.gives(c_loaded, 16))
                eng.dma_start(posi[:, :], a["positions"].rearrange("b (t p) -> p (b t)", p=P)).then_inc(
                    positions_loaded, p.gives(positions_loaded, 16))
                for i in range(2):
                    eng.dma_start(lbz[:, i], a["hg_lb_logits"][i].rearrange("(c p) -> p c", p=P)).then_inc(
                        lb_loaded, p.gives(lb_loaded, 16))
            eng.dma_start(bias_row[:, :], a["router_bias"].rearrange("(a e) -> a e", a=1)
                                 .partition_broadcast(P).rearrange("p a e -> p (a e)")).then_inc(
                bias_loaded, p.gives(bias_loaded, 16))
            eng.wait_ge(constants_ready, p.next(constants_ready))
            eng.wait_ge(c_loaded, p.next(c_loaded, 16))
            act(cact[:, :], cact[:, :], ACT.Silu).then_inc(cact_ready, p.gives(cact_ready))
            eng.wait_ge(lbdiff_ready, p.next(lbdiff_ready))
            act(lbw[:, 1], lbw[:, 1], ACT.Exp, scale=-1.0).then_inc(scalar_step, p.gives(scalar_step))
            eng.wait_ge(scalar_step, p.given(scalar_step))
            act(lbw[:, 1], lbw[:, 1], ACT.Ln, bias=consts[:, 1:2]).then_inc(lbln_ready, p.gives(lbln_ready))
            eng.wait_ge(angles_ready, p.next(angles_ready))
            act(sinT[:, :, :], angk[:, 0], ACT.Sin).then_inc(rope_ready, p.gives(rope_ready))
            act(cosT[:, :, :], angk[:, 1], ACT.Sin).then_inc(rope_ready, p.gives(rope_ready))
            eng.wait_ge(handed[1], p.next(handed[1]))

            def feature_norm():
                for c in range(NC):
                    i = c % 2
                    eng.wait_ge(sq_used[i], p.so_far(sq_used[i]))
                    p.mark(sq_used[i])
                    act(SC[:, i], X[:, c], ACT.Square).then_inc(sq_ready[i], p.gives(sq_ready[i]))
                eng.wait_ge(filled[2], p.next(filled[2]))
                act(SC[:, 2], bank(2), ACT.Ln, scale=1.0 / D, bias=consts[:, 0:1]).then_inc(
                    scalar_step, p.gives(scalar_step))
                eng.wait_ge(scalar_step, p.given(scalar_step))
                act(SC[:, 2], SC[:, 2], ACT.Exp, scale=-0.5).then_inc(handed[2], p.gives(handed[2]))

            def head_norm(x, tmp, n, d):
                act(tmp, x, ACT.Square).then_inc(squares_ready, p.gives(squares_ready))
                eng.wait_ge(sums_ready, p.next(sums_ready))
                act(rsq[:, 0:n], ssq[:, 0:n], ACT.Ln, scale=1.0 / d, bias=consts[:, 0:1]).then_inc(
                    scalar_step, p.gives(scalar_step))
                eng.wait_ge(scalar_step, p.given(scalar_step))
                act(rsq[:, 0:n], rsq[:, 0:n], ACT.Exp, scale=-0.5).then_inc(rms_ready, p.gives(rms_ready))

            def odd_tiles(dst, n=256):
                for t in (1, 3):
                    b = 2 + t // 2
                    eng.wait_ge(filled[b], p.next(filled[b]))
                    to = dst(t)
                    act(to, bank(b, n) if len(to.shape) == 2 else bank3(b, 4, HD), ACT.Copy).then_inc(
                        emptied[b], p.gives(emptied[b]))

            def y_copy(br):
                for t in range(NT):
                    b = 2 + t % 2
                    eng.wait_ge(filled[b], p.next(filled[b]))
                    act(Y[:, br, :, tt(t)], bank3(b, 4, P), ACT.Copy).then_inc(emptied[b], p.gives(emptied[b]))

            def exps(s, n):
                t, h, w = s.tile(n), s.head(n), len(s.blocks(n)) * P
                eng.wait_ge(rowmax_ready, p.next(rowmax_ready))
                for i, b in enumerate(s.banks(n)):
                    eng.wait_ge(filled[b], p.next(filled[b]))
                    if s.kind == "swa":
                        act(esink[:, t % 2, h:h + 1], row("swa_sinks", h, 1), ACT.Exp,
                                   bias=nmax[:, n % 2, 0:1]).then_inc(scalar_step, p.gives(scalar_step))
                    total = dl[:, n % 2, i:i + 1] if s.kind == "diff" else lsum[:, t % 2, h:h + 1]
                    act(probs[n % 2][i][:, 0:w], bank(b, w), ACT.Exp, bias=nmax[:, n % 2, i:i + 1],
                                  accum_out=total).then_inc(
                        (handed if s.kind == "diff" else emptied)[b], p.gives((handed if s.kind == "diff" else emptied)[b]))

            def sweep(s):
                for n in range(s.units + 1):
                    if n < s.units:
                        exps(s, n)
                    if n >= 1:
                        b, k = 2 + (n - 1) % 2, len(s.blocks(n - 1))
                        eng.wait_ge(filled[b], p.next(filled[b]))
                        act(probsT[(n - 1) % 2][:, 0:k], bank3(b, k, P), ACT.Copy).then_inc(
                            emptied[b], p.gives(emptied[b]))

            def do(step_, i):
                if step_ == "c":
                    odd_tiles(lambda t: DQK[:, t, i * 256:(i + 1) * 256] if i < 4
                              else DVt[:, t, (i - 4) * 256:(i - 3) * 256])
                elif step_ == "d":
                    odd_tiles(lambda t: swa_cols(t, i))
                elif step_ in ("hg_norm", "dif_post"):
                    for t in range(NT):
                        if step_ == "dif_post":
                            eng.wait_ge(handed[t % 2], p.next(handed[t % 2]))
                        head_norm(*norm_of(step_, t))
                elif step_ == "c_norm":
                    for t in range(2):
                        head_norm(*norm_of(step_, t))
                elif step_ in ("dif_norm", "swa_norm"):
                    if (step_, i) == ("dif_norm", 0):
                        for b in (2, 3):
                            eng.wait_ge(emptied[b], p.given(emptied[b]))
                    head_norm(*norm_of(step_, i))
                elif step_ in ("hg_y", "mla_y", "dif_y", "swa_y"):
                    y_copy(("hg_y", "mla_y", "dif_y", "swa_y").index(step_))
                elif step_ == "c_turn":
                    for t in range(NT):
                        b = 2 + t % 2
                        eng.wait_ge(filled[b], p.next(filled[b]))
                        act(cT[:, 0:3, tt(t)], bank3(b, 3, P), ACT.Copy).then_inc(
                            emptied[b], p.gives(emptied[b]))
                elif step_ == "up":
                    qk = heads(qk_tile[i % 2], 2 * HEADS)
                    eng.wait_ge(tile_used[i % 2], p.so_far(tile_used[i % 2]))
                    p.mark(tile_used[i % 2])
                    for f in range(2):
                        eng.wait_ge(filled[6 + f], p.next(filled[6 + f]))
                        kv = bank3(6 + f, 4, P)
                        act(qk[:, HEADS + 4 * f:HEADS + 4 * f + 4, 0:NOPE], kv[:, :, 0:NOPE], ACT.Copy).then_inc(
                            scalar_step, p.gives(scalar_step))
                        eng.wait_ge(scalar_step, p.given(scalar_step))
                        act(heads(mlaV[:, i, f * 256:(f + 1) * 256], 4), kv[:, :, NOPE:], ACT.Copy).then_inc(
                            emptied[6 + f], p.gives(emptied[6 + f]))
                    eng.wait_ge(handed[1], p.next(handed[1]))
                    head_norm(*norm_of("up", i))
                elif step_ == "turn":
                    for f in range(4):
                        b = 2 + f % 2
                        eng.wait_ge(filled[b], p.next(filled[b]))
                        dst = (mlaQ, mlaK)[f // 2][0:QKD, 4 * (f % 2):4 * (f % 2) + 4, tt(i)]
                        act(dst, bank3(b, 4, P)[0:QKD], ACT.Copy).then_inc(emptied[b], p.gives(emptied[b]))
                elif step_ == "dif_turn":
                    for t in range(NT):
                        for f in range(2):
                            eng.wait_ge(filled[2 + f], p.next(filled[2 + f]))
                            act((difQ, difK)[f][:, :, tt(t)], bank3(2 + f, 4, P), ACT.Copy).then_inc(
                                emptied[2 + f], p.gives(emptied[2 + f]))
                elif step_ == "swa_turn":
                    for t in range(NT):
                        eng.wait_ge(filled[2], p.next(filled[2]))
                        act(swaQ[:, :, tt(t)], bank3(2, 4, P), ACT.Copy).then_inc(
                            emptied[2], p.gives(emptied[2]))
                        eng.wait_ge(filled[3], p.next(filled[3]))
                        act(swaK[:, tt(t)], bank(3, P), ACT.Copy).then_inc(emptied[3], p.gives(emptied[3]))
                elif step_ == "sweep":
                    sweep(i)

            with p.loop("layer", DEPTH):
                eng.wait_ge(handed[5], p.so_far(handed[5]))
                feature_norm()
                eng.wait_ge(lamsum_ready, p.next(lamsum_ready))
                act(lams[:, 2:4], lams[:, 0:2], ACT.Exp).then_inc(lamexp_ready, p.gives(lamexp_ready))
                L, fb, kf = flat(hgO), flat(hgB), flat(hgK)
                eng.wait_ge(f_ready, p.next(f_ready))
                act(L, fb, ACT.Abs).then_inc(scalar_step, p.gives(scalar_step))
                eng.wait_ge(scalar_step, p.given(scalar_step))
                act(L, L, ACT.Exp, scale=-1.0).then_inc(scalar_step, p.gives(scalar_step))
                eng.wait_ge(scalar_step, p.given(scalar_step))
                act(L, L, ACT.Ln, bias=consts[:, 1:2]).then_inc(ln_ready, p.gives(ln_ready))
                eng.wait_ge(logk_ready, p.next(logk_ready))
                act(kf, kf, ACT.Exp).then_inc(k_ready, p.gives(k_ready))
                eng.wait_ge(logt_ready, p.next(logt_ready))
                act(L, L, ACT.Abs).then_inc(scalar_step, p.gives(scalar_step))
                eng.wait_ge(scalar_step, p.given(scalar_step))
                act(L, L, ACT.Exp, scale=-1.0).then_inc(scalar_step, p.gives(scalar_step))
                eng.wait_ge(scalar_step, p.given(scalar_step))
                act(L, L, ACT.Ln, bias=consts[:, 1:2]).then_inc(logaddexp_ready, p.gives(logaddexp_ready))
                for c in range(4):
                    eng.wait_ge(filled[2 + c % 2], p.next(filled[2 + c % 2]))
                    act(hgQ[:, c], bank(2 + c % 2), ACT.Silu).then_inc(
                        emptied[2 + c % 2], p.gives(emptied[2 + c % 2]))
                for u in range(2):
                    odd_tiles(lambda t: TM[:, t, u * 256:(u + 1) * 256])
                for u in range(2):
                    for t in range(NT):
                        b = 2 + t % 2
                        eng.wait_ge(filled[b], p.next(filled[b]))
                        act(TM[:, t, 512 + u * 256:512 + (u + 1) * 256], bank(b, 256), ACT.Silu).then_inc(
                            emptied[b], p.gives(emptied[b]))
                for at, n in ((0, 256), (256, KVR + ROPE)):
                    odd_tiles(lambda t: CM[:, t, at:at + n], n)
                eng.wait_ge(b_ready, p.next(b_ready))
                eng.wait_ge(emptied[2], p.given(emptied[2]))
                for pr in range(4):
                    for j in range(9):
                        i = (9 * pr + j) % 2
                        if j < 8:
                            eng.wait_ge(d_ready[i], p.next(d_ready[i]))
                            if j > 0:
                                act(hgE[i], hgE[i], ACT.Abs).then_inc(scalar_step, p.gives(scalar_step))
                                eng.wait_ge(scalar_step, p.given(scalar_step))
                            act(hgE[i], hgE[i], ACT.Exp, scale=-1.0).then_inc(e_ready[i], p.gives(e_ready[i]))
                            p.mark(ks_ready[i])
                            if j:
                                p.mark(qs_ready[i])
                        else:
                            eng.wait_ge(ks_ready[i], p.so_far(ks_ready[i]))
                            eng.wait_ge(qs_ready[i], p.so_far(qs_ready[i]))
                            act(hgE[i], hgB[:, pr], ACT.Exp).then_inc(e_ready[i], p.gives(e_ready[i]))
                        if j == 3:
                            ends = heads(hgB[:, pr], NT)[:, :, P - 1]
                            act(edec[:, :], ends, ACT.Exp).then_inc(edec_ready, p.gives(edec_ready))
                            eng.wait_ge(filled[2], p.next(filled[2]))
                            act(KdT[pr % 2], bank3(2, 4, P), ACT.Copy).then_inc(emptied[2], p.gives(emptied[2]))
                    if pr:
                        eng.wait_ge(filled[6 + (pr - 1) % 2], p.next(filled[6 + (pr - 1) % 2]))
                        act(hgO[:, :, tt(pr - 1)], bank3(6 + (pr - 1) % 2, 4, P), ACT.Copy).then_inc(
                            emptied[6 + (pr - 1) % 2], p.gives(emptied[6 + (pr - 1) % 2]))
                eng.wait_ge(filled[7], p.next(filled[7]))
                act(hgO[:, :, tt(3)], bank3(7, 4, P), ACT.Copy).then_inc(emptied[7], p.gives(emptied[7]))
                eng.wait_ge(emptied[7], p.given(emptied[7]))
                for st, i in SCHEDULE:
                    do(st, i)
                with p.loop("merge", 2):
                    for br in range(NB):
                        for j in range(4):
                            eng.wait_ge(filled[2 + j % 2], p.next(filled[2 + j % 2]))
                            act(SC[:, j], bank(2 + j % 2), ACT.Sigmoid).then_inc(
                                handed[2 + j % 2], p.gives(handed[2 + j % 2]))
                            if br:
                                p.mark(handed[j % 2])
                eng.wait_ge(handed[1], p.next(handed[1]))
                feature_norm()
                eng.wait_ge(filled[6], p.next(filled[6]))
                act(rt[:, 0], bank(6, NT * NE), ACT.Sigmoid).then_inc(handed[6], p.gives(handed[6]))
                eng.wait_ge(filled[7], p.next(filled[7]))
                act(combT, ps[0:NE, 7], ACT.Copy).then_inc(emptied[7], p.gives(emptied[7]))
                eng.wait_ge(emptied[7], p.given(emptied[7]))
                eng.wait_ge(comb_loaded, p.so_far(comb_loaded))
                eng.dma_start(scratch, combT).then_inc(comb_stored, p.gives(comb_stored, 16))
                eng.wait_ge(comb_stored, p.given(comb_stored))
                eng.dma_start(comb, scratch.partition_broadcast(P)).then_inc(
                    comb_loaded, p.gives(comb_loaded, 16))
                p.mark(comb_loaded, 16)
                with p.loop("moe", NG):
                    for e in range(4):
                        for m in range(2):
                            eng.wait_ge(filled[2 + m], p.next(filled[2 + m]))
                            act(SC[:, 2 * (e % 2) + m], bank(2 + m), ACT.Silu).then_inc(
                                handed[2 + m], p.gives(handed[2 + m]))
                    p.mark(handed[5])
            for t in range(NT):
                eng.wait_ge(handed[1], p.next(handed[1]))
                eng.dma_start(out.rearrange("b (t p) d -> p (b t) d", p=P)[:, t], xin[:, t]).then_inc(
                    out_stored, p.gives(out_stored, 16))
            eng.wait_ge(out_stored, p.given(out_stored))

        @block.vector
        def _(eng):
            p = Program(eng, "dve", rate)
            for b in (0, 1, 4, 5):
                eng.sem_inc(emptied[b], 1)
                eng.sem_inc(handed[b], 1)
            eng.sem_inc(params_used, 1)

            def alone():
                eng.sem_inc(waited["dve"], 1)

            v = nc.vector




            eng.wait_ge(lb_loaded, p.next(lb_loaded, 32))
            eng.wait_ge(constants_ready, p.next(constants_ready))
            v.tensor_tensor(lbw[:, 0], lbz[:, 0], lbz[:, 1], ALU.subtract).then_inc(
                vector_step, p.gives(vector_step))
            eng.wait_ge(vector_step, p.given(vector_step))
            v.scalar_tensor_tensor(out=lbw[:, 1], in0=lbw[:, 0], scalar=-1.0, in1=lbw[:, 0],
                                          op0=ALU.mult, op1=ALU.max).then_inc(
                lbdiff_ready, p.gives(lbdiff_ready))
            eng.wait_ge(positions_loaded, p.next(positions_loaded, 16))
            v.tensor_copy(posf[:, :], posi[:, :]).then_inc(vector_step, p.gives(vector_step))
            eng.wait_ge(vector_step, p.given(vector_step))
            for t in range(NT):
                v.tensor_scalar(ang[:, t], ifr[:, :], posf[:, t:t + 1], None, ALU.mult).then_inc(
                    vector_step, p.gives(vector_step))
                eng.wait_ge(vector_step, p.given(vector_step))
            c1 = 6.28125
            c2 = float((np.array(2 * math.pi - c1, np.float32).view(np.uint32) & np.uint32(0xFFFFF000)).view(np.float32))
            c3 = 2 * math.pi - c1 - c2
            big = 1.5 * 2 ** 23
            for i in range(2):
                tmp = posf
                v.tensor_scalar(angk[:, i], ang[:, :, :], 1.0 / (2 * math.pi), 0.25 * i, ALU.mult, ALU.add).then_inc(
                    vector_step, p.gives(vector_step))
                eng.wait_ge(vector_step, p.given(vector_step))
                v.tensor_scalar(angk[:, i], angk[:, i], big, None, ALU.add).then_inc(
                    vector_step, p.gives(vector_step))
                eng.wait_ge(vector_step, p.given(vector_step))
                v.tensor_scalar(angk[:, i], angk[:, i], big, None, ALU.subtract).then_inc(
                    vector_step, p.gives(vector_step))
                eng.wait_ge(vector_step, p.given(vector_step))
            r = [sb(f"rope_r{i}", NT, HALF) for i in range(2)]
            for i in range(2):
                a0 = ang[:, :, :]
                for k, c in enumerate((c1, c2, c3)):
                    v.scalar_tensor_tensor(out=r[i][:, :, :], in0=angk[:, i], scalar=-c,
                                                in1=a0 if k == 0 else r[i][:, :, :], op0=ALU.mult, op1=ALU.add).then_inc(
                        vector_step, p.gives(vector_step))
                    eng.wait_ge(vector_step, p.given(vector_step))
                v.tensor_scalar(r[i][:, :, :], r[i][:, :, :], 0.5 * math.pi * i, 3.1415925, ALU.add, ALU.min).then_inc(
                    vector_step, p.gives(vector_step))
                eng.wait_ge(vector_step, p.given(vector_step))
            v.tensor_scalar(angk[:, 0], r[0][:, :, :], -3.1415925, None, ALU.max).then_inc(
                vector_step, p.gives(vector_step))
            eng.wait_ge(vector_step, p.given(vector_step))
            v.tensor_scalar(angk[:, 1], r[1][:, :, :], -3.1415925, None, ALU.max).then_inc(
                angles_ready, p.gives(angles_ready))
            eng.wait_ge(lbln_ready, p.next(lbln_ready))
            for i, sign in ((0, 1.0), (1, -1.0)):
                dst = lbt[:, 1, i * NT:(i + 1) * NT]
                v.tensor_scalar(dst, lbw[:, 0], sign, 0.0, ALU.mult, ALU.max).then_inc(
                    vector_step, p.gives(vector_step))
                eng.wait_ge(vector_step, p.given(vector_step))
                v.scalar_tensor_tensor(out=dst, in0=dst, scalar=-1.0, in1=lbw[:, 1],
                                            op0=ALU.mult, op1=ALU.subtract).then_inc(
                    vector_step, p.gives(vector_step))
                eng.wait_ge(vector_step, p.given(vector_step))
            for c in range(NC):
                eng.wait_ge(filled[c % 2], p.next(filled[c % 2]))
                v.tensor_copy(X[:, c], bank(c % 2)).then_inc(
                    (handed if c == NC - 1 else emptied)[c % 2], p.gives((handed if c == NC - 1 else emptied)[c % 2]))
            eng.wait_ge(bias_loaded, p.next(bias_loaded, 16))

            def feature_norm(scale_at, norm_at, shift_at):
                v.scalar_tensor_tensor(out=gain[:, :], in0=mod[:, scale_at:scale_at + NC], scalar=1.0,
                                            in1=colT[:, norm_at:norm_at + NC], op0=ALU.add, op1=ALU.mult).then_inc(
                    vector_step, p.gives(vector_step))
                eng.wait_ge(vector_step, p.given(vector_step))
                for c in range(NC):
                    v.scalar_tensor_tensor(out=H[:, c], in0=X[:, c], scalar=gain[:, c:c + 1],
                                                  in1=SC[:, 2], op0=ALU.mult, op1=ALU.mult).then_inc(
                        vector_step, p.gives(vector_step))
                eng.wait_ge(vector_step, p.given(vector_step))
                for c in range(NC):
                    v.tensor_scalar(H[:, c], H[:, c], mod[:, shift_at + c:shift_at + c + 1], None,
                                           ALU.add).then_inc(h_ready, p.gives(h_ready))

            def head_norm(x, tmp, n, d):
                x = x if len(x.shape) == 3 else heads(x, n)
                eng.wait_ge(squares_ready, p.next(squares_ready))
                tmp = tmp if len(tmp.shape) == 3 else heads(tmp, n)
                v.tensor_reduce(ssq[:, 0:n], tmp, AX, ALU.add).then_inc(sums_ready, p.gives(sums_ready))
                eng.wait_ge(rms_ready, p.next(rms_ready))
                v.tensor_tensor(x, x, spread(rsq[:, 0:n], d), ALU.mult).then_inc(normed, p.gives(normed))

            def even_tiles(dst, n=256):
                for t in (0, 2):
                    eng.wait_ge(filled[t // 2], p.next(filled[t // 2]))
                    to = dst(t)
                    v.tensor_copy(to, bank(t // 2, n) if len(to.shape) == 2 else bank3(t // 2, 4, HD)).then_inc(
                        emptied[t // 2], p.gives(emptied[t // 2]))

            def rowmax(s, n):
                t, h, w = s.tile(n), s.head(n), len(s.blocks(n)) * P
                bs = s.banks(n)
                for i, b in enumerate(bs):
                    eng.wait_ge(filled[b], p.next(filled[b]))
                    if s.kind == "swa":
                        m = swmask[:, 2 * P - w:2 * P]
                        v.tensor_tensor(bank(b, w), bank(b, w), m, ALU.add).then_inc(
                            vector_step, p.gives(vector_step))
                        eng.wait_ge(vector_step, p.given(vector_step))
                    else:
                        v.tensor_tensor(ps[:, b, tt(t)], ps[:, b, tt(t)], cmask[:, :], ALU.add).then_inc(
                            vector_step, p.gives(vector_step))
                        eng.wait_ge(vector_step, p.given(vector_step))
                    red = v.tensor_reduce(nmax[:, n % 2, i:i + 1], bank(b, w), AX, ALU.max, negate=True)
                    if s.kind == "swa":
                        red.then_inc(vector_step, p.gives(vector_step))
                        eng.wait_ge(vector_step, p.given(vector_step))
                        red = v.tensor_tensor(nmax[:, n % 2, 0:1], nmax[:, n % 2, 0:1], nsink[:, h:h + 1], ALU.min)
                    red.then_inc(
                        (rowmax_ready if i == len(bs) - 1 else vector_step), p.gives((rowmax_ready if i == len(bs) - 1 else vector_step)))

            def combine(n):
                w = len(DIFF.blocks(n)) * P
                eng.wait_ge(handed[6], p.next(handed[6]))
                eng.wait_ge(handed[7], p.next(handed[7]))
                p1, p2 = (probs[n % 2][i][:, 0:w] for i in range(2))
                if n:
                    eng.wait_ge(probs_ready, p.given(probs_ready))
                v.reciprocal(dr[:, :], dl[:, n % 2]).then_inc(vector_step, p.gives(vector_step))
                eng.wait_ge(vector_step, p.given(vector_step))
                v.tensor_tensor(dr[:, 1:2], dr[:, 1:2], neglam[:, :], ALU.mult).then_inc(
                    vector_step, p.gives(vector_step))
                eng.wait_ge(vector_step, p.given(vector_step))
                v.tensor_scalar(p1, p1, dr[:, 0:1], None, ALU.mult).then_inc(vector_step, p.gives(vector_step))
                eng.wait_ge(vector_step, p.given(vector_step))
                v.scalar_tensor_tensor(out=p1, in0=p2, scalar=dr[:, 1:2], in1=p1,
                                              op0=ALU.mult, op1=ALU.add).then_inc(
                    probs_ready, p.gives(probs_ready))

            def tile_out(s, t):
                b = t % 2
                eng.wait_ge(filled[b], p.next(filled[b]))
                dst = y_tok[s.kind][:, t]
                if s.kind == "diff":
                    v.tensor_copy(dst, bank(b)).then_inc(handed[b], p.gives(handed[b]))
                    return
                if s.kind == "swa":
                    v.tensor_tensor(lrec[:, :], lsum[:, t % 2], esink[:, t % 2], ALU.add).then_inc(
                        vector_step, p.gives(vector_step))
                    eng.wait_ge(vector_step, p.given(vector_step))
                    v.reciprocal(lrec[:, :], lrec[:, :]).then_inc(vector_step, p.gives(vector_step))
                    eng.wait_ge(vector_step, p.given(vector_step))
                else:
                    v.reciprocal(lrec[:, :], lsum[:, t % 2]).then_inc(vector_step, p.gives(vector_step))
                    eng.wait_ge(vector_step, p.given(vector_step))
                v.tensor_tensor(heads(dst, HEADS), bank3(b, HEADS, HD), spread(lrec[:, :], HD), ALU.mult).then_inc(
                    emptied[b], p.gives(emptied[b]))

            def sweep(s):
                for n in range(s.units + 2):
                    if n < s.units:
                        rowmax(s, n)
                    if s.kind == "diff" and 1 <= n <= s.units:
                        combine(n - 1)
                    if n >= 2 and s.last(n - 2):
                        tile_out(s, s.tile(n - 2))

            def do(step_, i):
                if step_ == "c":
                    even_tiles(lambda t: DQK[:, t, i * 256:(i + 1) * 256] if i < 4
                               else DVt[:, t, (i - 4) * 256:(i - 3) * 256])
                elif step_ == "d":
                    even_tiles(lambda t: swa_cols(t, i))
                elif step_ in ("hg_norm", "dif_post"):
                    for t in range(NT):
                        head_norm(*norm_of(step_, t))
                elif step_ == "c_norm":
                    for t in range(2):
                        head_norm(*norm_of(step_, t))
                elif step_ in ("dif_norm", "swa_norm"):
                    head_norm(*norm_of(step_, i))
                elif step_ == "up":
                    qk = heads(qk_tile[i % 2], 2 * HEADS)
                    eng.wait_ge(tile_used[i % 2], p.so_far(tile_used[i % 2]))
                    p.mark(tile_used[i % 2])
                    p.mark(filled[6])
                    p.mark(filled[7])
                    v.tensor_copy(qk[:, HEADS:, NOPE:], repeat(CM[:, i, QR + KVR:], HEADS)).then_inc(
                        vector_step, p.gives(vector_step))
                    for f in range(2):
                        eng.wait_ge(filled[f], p.next(filled[f]))
                        v.tensor_copy(qk_tile[i % 2][:, f * 384:(f + 1) * 384], bank(f, 384)).then_inc(
                            (emptied, handed)[f][f], p.gives((emptied, handed)[f][f]))
                    head_norm(*norm_of("up", i))
                elif step_ == "sweep":
                    sweep(i)

            with p.loop("layer", DEPTH) as l:
                eng.wait_ge(filled[0], p.next(filled[0]))
                v.tensor_copy(colT[:, :], bank(0, NCOLP)).then_inc(emptied[0], p.gives(emptied[0]))
                eng.wait_ge(emptied[0], p.given(emptied[0]))
                eng.wait_ge(rows_loaded, p.next(rows_loaded, 16 * len(ROWS)))
                v.tensor_copy(lic[:, :], pick(litab[:, :, :], l)).then_inc(vector_step, p.gives(vector_step))
                eng.wait_ge(vector_step, p.given(vector_step))
                v.tensor_copy(lbc[:, :], pick(lbt[:, :, :], l)).then_inc(vector_step, p.gives(vector_step))
                eng.wait_ge(vector_step, p.given(vector_step))
                for name, n, s in (("mla_qk_norm", QKD, QKD ** -0.5), ("diff_qk_norm", HD, HD ** -0.5),
                                   ("swa_qk_norm", HD, HD ** -0.5)):
                    v.tensor_scalar(row(name, 0, n), row(name, 0, n), s, None, ALU.mult).then_inc(
                        vector_step, p.gives(vector_step))
                    eng.wait_ge(vector_step, p.given(vector_step))
                v.tensor_scalar(nsink[:, :], row("swa_sinks"), -1.0, None, ALU.mult).then_inc(
                    vector_step, p.gives(vector_step))
                eng.wait_ge(vector_step, p.given(vector_step))
                lp = heads(row("diff_lam"), 4)
                for i in range(2):
                    v.tensor_tensor(lamp[:, i], lp[:, 2 * i], lp[:, 2 * i + 1], ALU.mult).then_inc(
                        vector_step, p.gives(vector_step))
                    eng.wait_ge(vector_step, p.given(vector_step))
                v.tensor_reduce(lams[:, 0:2], lamp[:, :, :], AX, ALU.add).then_inc(
                    lamsum_ready, p.gives(lamsum_ready))
                v.tensor_scalar(row("diff_onorm"), row("diff_onorm"), lic[:, 1:2], None, ALU.mult).then_inc(
                    rows_ready, p.gives(rows_ready))
                eng.wait_ge(lamexp_ready, p.next(lamexp_ready))
                v.tensor_tensor(neglam[:, :], lams[:, 3:4], lams[:, 2:3], ALU.subtract).then_inc(
                    vector_step, p.gives(vector_step))
                eng.wait_ge(vector_step, p.given(vector_step))
                v.tensor_tensor(neglam[:, :], neglam[:, :], lic[:, 0:1], ALU.subtract).then_inc(
                    vector_step, p.gives(vector_step))
                eng.wait_ge(vector_step, p.given(vector_step))
                alone()
                with p.loop("ada", 6) as s:
                    eng.wait_ge(filled[1], p.next(filled[1]))
                    v.tensor_tensor(mod[:, bass.ds(s * NC, NC)], bank(1, NC),
                                              colT[:, bass.ds(s * NC, NC)], ALU.add).then_inc(
                        emptied[1], p.gives(emptied[1]))
                eng.wait_ge(emptied[1], p.given(emptied[1]))
                eng.wait_ge(handed[2], p.next(handed[2]))
                feature_norm(NC, 48, 0)

                fb = hgB
                for c in range(4):
                    eng.wait_ge(filled[c % 2], p.next(filled[c % 2]))
                    v.tensor_copy(fb[:, c], bank(c % 2)).then_inc(emptied[c % 2], p.gives(emptied[c % 2]))
                eng.wait_ge(emptied[0], p.given(emptied[0]))
                eng.wait_ge(emptied[1], p.given(emptied[1]))
                v.tensor_scalar(flat(hgK), flat(fb), -1.0, 0.0, ALU.mult, ALU.min).then_inc(
                    f_ready, p.gives(f_ready))
                eng.wait_ge(ln_ready, p.next(ln_ready))
                for c in range(4):
                    v.scalar_tensor_tensor(out=hgK[:, c], in0=hgK[:, c], scalar=lbc[:, NT + c:NT + c + 1],
                                                  in1=hgO[:, c], op0=ALU.add, op1=ALU.subtract).then_inc(
                        (logk_ready if c == 3 else vector_step), p.gives((logk_ready if c == 3 else vector_step)))
                for c in range(4):
                    v.tensor_scalar(fb[:, c], fb[:, c], 0.0, lbc[:, NT + c:NT + c + 1], ALU.min, ALU.add).then_inc(
                        vector_step, p.gives(vector_step))
                eng.wait_ge(vector_step, p.given(vector_step))
                v.tensor_tensor(flat(fb), flat(fb), flat(hgO), ALU.subtract).then_inc(
                    vector_step, p.gives(vector_step))
                eng.wait_ge(vector_step, p.given(vector_step))
                for c in range(4):
                    v.tensor_scalar(hgO[:, c], fb[:, c], -1.0, lbc[:, c:c + 1], ALU.mult, ALU.add).then_inc(
                        (logt_ready if c == 3 else vector_step), p.gives((logt_ready if c == 3 else vector_step)))
                v.memset(flat(DQK[:, 0:2]), 0.0).then_inc(vector_step, p.gives(vector_step))
                v.memset(DQK[:, 3], 0.0).then_inc(vector_step, p.gives(vector_step))
                eng.wait_ge(logaddexp_ready, p.next(logaddexp_ready))
                for c in range(4):
                    v.scalar_tensor_tensor(out=fb[:, c], in0=fb[:, c], scalar=lbc[:, c:c + 1],
                                                  in1=hgO[:, c], op0=ALU.max, op1=ALU.add).then_inc(
                        vector_step, p.gives(vector_step))
                eng.wait_ge(vector_step, p.given(vector_step))
                for c in range(4):
                    for t in range(NT):
                        v.tensor_tensor_scan(out=fb[:, c, tt(t)], data0=ones[:, :], data1=fb[:, c, tt(t)],
                                                    initial=0.0, op0=ALU.mult, op1=ALU.add).then_inc(
                            (b_ready if (c, t) == (3, 3) else vector_step), p.gives((b_ready if (c, t) == (3, 3) else vector_step)))
                eng.wait_ge(b_ready, p.given(b_ready))
                for u in range(2):
                    even_tiles(lambda t: TM[:, t, u * 256:(u + 1) * 256])
                for at, n in ((0, 256), (256, KVR + ROPE)):
                    even_tiles(lambda t: CM[:, t, at:at + n], n)
                eng.wait_ge(k_ready, p.next(k_ready))

                def decay(g):
                    pr, j = divmod(g, 9)
                    i = g % 2
                    if j == 8 or g == 36:
                        return
                    if g >= 2:
                        eng.wait_ge((qin_ready if (g - 2) % 9 == 8 else qs_ready[i]), p.so_far((qin_ready if (g - 2) % 9 == 8 else qs_ready[i])))
                        eng.wait_ge(ks_ready[i], p.given(ks_ready[i]))
                    size = P if j == 0 else 1 << j
                    blocks = hgB[:, pr].rearrange("p (n s) -> p n s", s=size)
                    mid = size - 1 if j == 0 else size // 2 - 1
                    ref = blocks[:, :, mid:mid + 1].to_broadcast([P, S // size, size])
                    v.tensor_tensor(hgE[i].rearrange("p (n s) -> p n s", s=size), blocks, ref,
                                           ALU.subtract).then_inc(d_ready[i], p.gives(d_ready[i]))

                def keep(pr, lv):
                    if lv == 0:
                        eng.wait_ge(attn_used[pr % 2], p.so_far(attn_used[pr % 2]))
                        alone()
                        p.mark(attn_used[pr % 2])
                    mask = (ident[:, :] if lv == 0 else lmask[:, lv - 1]).bitcast(I32)
                    for hp in range(2):
                        b = (lv % 2) * 4 + hp
                        eng.wait_ge(filled[b], p.next(filled[b]))
                        alone()
                        if lv:
                            eng.wait_ge(emptied[4 - lv % 2 * 4 + hp], p.given(emptied[4 - lv % 2 * 4 + hp]))
                            alone()
                        v.copy_predicated(attnT[pr % 2][hp], repeat(mask, NT), bank3(b, NT, P)).then_inc(
                            emptied[b], p.gives(emptied[b]))

                decay(0)
                for pr in range(4):
                    for j in range(9):
                        g = 9 * pr + j
                        i = g % 2
                        if j < 8:
                            decay(g + 1)
                            eng.wait_ge(e_ready[i], p.next(e_ready[i]))
                            eng.wait_ge(qk_used[i], p.so_far(qk_used[i]))
                            p.mark(qk_used[i])
                            v.tensor_tensor(hgKs[i], hgK[:, pr], hgE[i], ALU.mult).then_inc(
                                ks_ready[i], p.gives(ks_ready[i]))
                            if j:
                                p.mark(qs_ready[i])
                        else:
                            p.mark(e_ready[i])
                            p.mark(qin_ready)
                            decay(g + 1)
                        if j:
                            keep(pr, j - 1)
                        if j == 5:
                            eng.wait_ge(edec_ready, p.next(edec_ready))
                            eng.wait_ge(filled[0], p.next(filled[0]))
                            for c in range(3):
                                for h in range(2):
                                    r = slice(h * HD, (h + 1) * HD)
                                    new, add = state[pr % 2][r, c + 1, r], ps[r, 0, c * P + h * HD:c * P + (h + 1) * HD]
                                    if c == 0:
                                        ins = v.tensor_copy(new, add)
                                    else:
                                        ins = v.scalar_tensor_tensor(out=new, in0=state[pr % 2][r, c, r],
                                                                     scalar=edec[r, c:c + 1], in1=add,
                                                                     op0=ALU.mult, op1=ALU.add)
                                    if (c, h) == (2, 1):
                                        ins.then_inc(emptied[0], p.gives(emptied[0]))
                                    else:
                                        ins.then_inc(vector_step, p.gives(vector_step))
                                if c < 2:
                                    eng.wait_ge(vector_step, p.given(vector_step))
                    p.mark(filled[6 + pr % 2])
                for st, i in SCHEDULE:
                    do(st, i)

                with p.loop("merge", 2) as g:
                    for br in range(NB):
                        for j in range(4):
                            i = j % 2
                            eng.wait_ge(handed[2 + i], p.next(handed[2 + i]))
                            eng.wait_ge(filled[i], p.next(filled[i]))
                            if br == 0:
                                v.tensor_tensor(pick(merged, g * 4 + j), bank(i), SC[:, j], ALU.mult).then_inc(
                                    emptied[i], p.gives(emptied[i]))
                            else:
                                eng.wait_ge(added[i], p.so_far(added[i]))
                                p.mark(added[i])
                                v.tensor_tensor(SC[:, 4 + i], bank(i), SC[:, j], ALU.mult).then_inc(
                                    handed[i], p.gives(handed[i]))
                for c in range(NC):
                    i = c % 2
                    eng.wait_ge(filled[i], p.next(filled[i]))
                    if c == 0:
                        ins = None
                    v.scalar_tensor_tensor(out=X[:, c], in0=bank(i), scalar=mod[:, 2 * NC + c:2 * NC + c + 1],
                                                     in1=X[:, c], op0=ALU.mult, op1=ALU.add).then_inc(
                        (handed if c == NC - 1 else emptied)[i], p.gives((handed if c == NC - 1 else emptied)[i]))
                eng.wait_ge(handed[2], p.next(handed[2]))
                eng.wait_ge(handed[1], p.given(handed[1]))
                feature_norm(4 * NC, 56, 3 * NC)
                p.mark(filled[6])
                p.mark(filled[7])
                eng.wait_ge(handed[6], p.next(handed[6]))
                r16 = [heads(rt[:, k], NT) for k in range(6)]
                w16 = repeat(wexp[:, :], NT)
                v.tensor_tensor(r16[1], r16[0], repeat(bias_row[:, :], NT), ALU.add).then_inc(
                    vector_step, p.gives(vector_step))
                eng.wait_ge(vector_step, p.given(vector_step))
                q = rt[:, 1].rearrange("p (g e) -> p g e", e=PER)
                for k in range(2):
                    v.tensor_tensor(rg[:, k], q[:, :, 2 * k], q[:, :, 2 * k + 1], ALU.max).then_inc(
                        vector_step, p.gives(vector_step))
                    eng.wait_ge(vector_step, p.given(vector_step))
                    v.tensor_tensor(rg[:, 2 + k], q[:, :, 2 * k], q[:, :, 2 * k + 1], ALU.min).then_inc(
                        vector_step, p.gives(vector_step))
                    eng.wait_ge(vector_step, p.given(vector_step))
                v.tensor_tensor(rg[:, 4], rg[:, 0], rg[:, 1], ALU.max).then_inc(
                    vector_step, p.gives(vector_step))
                eng.wait_ge(vector_step, p.given(vector_step))
                v.tensor_tensor(rg[:, 5], rg[:, 0], rg[:, 1], ALU.min).then_inc(
                    vector_step, p.gives(vector_step))
                eng.wait_ge(vector_step, p.given(vector_step))
                v.tensor_tensor(rg[:, 2], rg[:, 2], rg[:, 3], ALU.max).then_inc(
                    vector_step, p.gives(vector_step))
                eng.wait_ge(vector_step, p.given(vector_step))
                v.tensor_tensor(rg[:, 5], rg[:, 5], rg[:, 2], ALU.max).then_inc(
                    vector_step, p.gives(vector_step))
                eng.wait_ge(vector_step, p.given(vector_step))
                v.tensor_tensor(rg[:, 4], rg[:, 4], rg[:, 5], ALU.add).then_inc(
                    vector_step, p.gives(vector_step))
                eng.wait_ge(vector_step, p.given(vector_step))

                def first_max(x, w, n, top, hit, dst):
                    v.tensor_reduce(top, x, AX, ALU.max).then_inc(vector_step, p.gives(vector_step))
                    eng.wait_ge(vector_step, p.given(vector_step))
                    v.tensor_tensor(hit, x, spread(top, n), ALU.is_equal).then_inc(
                        vector_step, p.gives(vector_step))
                    eng.wait_ge(vector_step, p.given(vector_step))
                    v.tensor_tensor(hit, hit, w, ALU.mult).then_inc(vector_step, p.gives(vector_step))
                    eng.wait_ge(vector_step, p.given(vector_step))
                    v.tensor_reduce(top, hit, AX, ALU.max).then_inc(vector_step, p.gives(vector_step))
                    eng.wait_ge(vector_step, p.given(vector_step))
                    v.tensor_tensor(dst, hit, spread(top, n), ALU.is_equal).then_inc(
                        vector_step, p.gives(vector_step))
                    eng.wait_ge(vector_step, p.given(vector_step))

                g3 = [heads(rg[:, k], NT) for k in range(6)]
                first_max(g3[4], repeat(wgrp[:, :], NT), NG, ssq[:, 0:NT], g3[0], g3[1])
                v.tensor_scalar(rg[:, 1], rg[:, 1], -NEG, NEG, ALU.mult, ALU.add).then_inc(
                    vector_step, p.gives(vector_step))
                eng.wait_ge(vector_step, p.given(vector_step))
                v.tensor_tensor(q, q, rg[:, 1].unsqueeze(2).to_broadcast([P, NT * NG, PER]), ALU.add).then_inc(
                    vector_step, p.gives(vector_step))
                eng.wait_ge(vector_step, p.given(vector_step))
                first_max(r16[1], w16, NE, ssq[:, 0:NT], r16[2], r16[3])
                v.scalar_tensor_tensor(out=rt[:, 1], in0=rt[:, 3], scalar=2 * NEG, in1=rt[:, 1],
                                            op0=ALU.mult, op1=ALU.add).then_inc(
                    vector_step, p.gives(vector_step))
                eng.wait_ge(vector_step, p.given(vector_step))
                first_max(r16[1], w16, NE, ssq[:, 0:NT], r16[2], r16[5])
                v.tensor_tensor(rt[:, 3], rt[:, 3], rt[:, 5], ALU.add).then_inc(
                    vector_step, p.gives(vector_step))
                eng.wait_ge(vector_step, p.given(vector_step))
                v.tensor_tensor(rt[:, 3], rt[:, 3], rt[:, 0], ALU.mult).then_inc(
                    vector_step, p.gives(vector_step))
                eng.wait_ge(vector_step, p.given(vector_step))
                v.tensor_reduce(ssq[:, 0:NT], r16[3], AX, ALU.add).then_inc(vector_step, p.gives(vector_step))
                eng.wait_ge(vector_step, p.given(vector_step))
                v.reciprocal(ssq[:, NT:2 * NT], ssq[:, 0:NT]).then_inc(vector_step, p.gives(vector_step))
                eng.wait_ge(vector_step, p.given(vector_step))
                v.tensor_tensor(r16[4], r16[3], spread(ssq[:, NT:2 * NT], NE), ALU.mult).then_inc(
                    comb_ready, p.gives(comb_ready))
                with p.loop("moe", NG):
                    for e in range(4):
                        for m in range(2):
                            eng.wait_ge(weighted, p.next(weighted))
                            p.mark(handed[2 + m])
                            eng.wait_ge(filled[m], p.next(filled[m]))
                            v.tensor_tensor(hid[:, 2 * e + m], bank(m), SC[:, 2 * (e % 2) + m], ALU.mult).then_inc(
                                emptied[m], p.gives(emptied[m]))
                    for c in range(NC):
                        b = 4 + c % 2
                        eng.wait_ge(filled[b], p.next(filled[b]))
                        v.scalar_tensor_tensor(out=X[:, c], in0=bank(b), scalar=mod[:, 5 * NC + c:5 * NC + c + 1],
                                                         in1=X[:, c], op0=ALU.mult, op1=ALU.add).then_inc(
                            (handed if c == NC - 1 else emptied)[b], p.gives((handed if c == NC - 1 else emptied)[b]))
                eng.wait_ge(emptied[4], p.given(emptied[4]))
                eng.wait_ge(handed[5], p.given(handed[5]))
                v.memset(lams[:, 0:1], 0.0).then_inc(params_used, p.gives(params_used))
            for t in range(NT):
                for f in range(2):
                    eng.wait_ge(filled[f], p.next(filled[f]))
                    v.tensor_copy(xin[:, t, f * 512:(f + 1) * 512], bank(f)).then_inc(
                        (emptied, handed)[f][f], p.gives((emptied, handed)[f][f]))

        @block.gpsimd
        def _(eng):
            p = Program(eng, "pool", rate)
            for sem in (*added, *qs_ready):
                eng.sem_inc(sem, 1)

            def alone():
                eng.sem_inc(waited["pool"], 1)



            def select(ap, op, fill, base, pattern, channel):
                eng.affine_select(out=ap, in_=ap, compare_op=op, fill=fill, base=base, pattern=pattern,
                                       channel_multiplier=channel).then_inc(pool_step, p.gives(pool_step))
                eng.wait_ge(pool_step, p.given(pool_step))

            eng.memset(ident[:, :], 0.0).then_inc(pool_step, p.gives(pool_step))
            eng.wait_ge(pool_step, p.given(pool_step))
            select(ident[:, :], ALU.not_equal, 1.0, 0, [[-1, P]], 1)
            eng.memset(ones[:, :], 1.0).then_inc(pool_step, p.gives(pool_step))
            eng.wait_ge(pool_step, p.given(pool_step))
            eng.memset(cmask[:, :], 0.0).then_inc(pool_step, p.gives(pool_step))
            eng.wait_ge(pool_step, p.given(pool_step))
            select(cmask[:, :], ALU.is_ge, NEG, 0, [[-1, P]], 1)
            eng.memset(swmask[:, :], 0.0).then_inc(pool_step, p.gives(pool_step))
            eng.wait_ge(pool_step, p.given(pool_step))
            select(swmask[:, 0:P], ALU.is_gt, NEG, 0, [[1, P]], -1)
            select(swmask[:, P:], ALU.is_ge, NEG, 0, [[-1, P]], 1)
            eng.memset(lmask[:, :, :], 0.0).then_inc(pool_step, p.gives(pool_step))
            eng.wait_ge(pool_step, p.given(pool_step))
            for lv in range(LEVELS):
                h = 1 << lv
                n = P // (2 * h)
                up = lmask[:, lv].rearrange("p (n a h) -> p n a h", n=n, a=2)[:, :, 1]
                eng.memset(up, 1.0).then_inc(pool_step, p.gives(pool_step))
                eng.wait_ge(pool_step, p.given(pool_step))
                select(up, ALU.is_ge, 0.0, 0, [[-2 * h, n], [0, h]], 1)
                select(up, ALU.is_ge, 0.0, h - 1, [[2 * h, n], [0, h]], -1)
            freq = np.float32(10000.0) ** (-np.arange(0, ROPE, 2, dtype=np.float32) / np.float32(ROPE))
            for i in range(HALF):
                eng.memset(ifr[:, i:i + 1], float(freq[i]))
            for l in range(DEPTH):
                li = 0.8 - 0.6 * math.exp(-0.3 * l)
                eng.memset(litab[:, l, 0:1], li)
                eng.memset(litab[:, l, 1:2], 1.0 - li)
            eng.memset(consts[:, 0:1], EPS)
            eng.memset(consts[:, 1:2], 1.0)
            eng.memset(lbt[:, 0, 0:NT], LN0)
            eng.memset(lbt[:, 0, NT:], 0.0)
            for e in range(NE):
                eng.memset(wexp[:, e:e + 1], float(NE - e))
            for g in range(NG):
                ins = eng.memset(wgrp[:, g:g + 1], float(NG - g))
            ins.then_inc(constants_ready, p.gives(constants_ready))
            eng.wait_ge(constants_ready, p.given(constants_ready))

            def gains(parts, after=None):
                eng.wait_ge(normed, p.next(normed))
                for k, (x, g) in enumerate(parts):
                    ins = eng.tensor_tensor(x, x, g, ALU.mult)
                    if after is None and k == len(parts) - 1:
                        ins.then_inc(gained, p.gives(gained))
                    else:
                        ins.then_inc(pool_step, p.gives(pool_step))
                        eng.wait_ge(pool_step, p.given(pool_step))
                if after is not None:
                    after()

            def rope(qk, t):
                tmp = [heads(sc[:, 1536 + 256 * k:1792 + 256 * k], 2 * HEADS) for k in range(4)]
                x1, x2 = qk[:, :, NOPE:NOPE + HALF], qk[:, :, NOPE + HALF:]
                c, s = repeat(cosT[:, t], 2 * HEADS), repeat(sinT[:, t], 2 * HEADS)
                for k, (x, y) in enumerate(((x1, c), (x2, s), (x1, s), (x2, c))):
                    eng.tensor_tensor(tmp[k], x, y, ALU.mult).then_inc(pool_step, p.gives(pool_step))
                    eng.wait_ge(pool_step, p.given(pool_step))
                eng.tensor_tensor(x1, tmp[0], tmp[1], ALU.subtract).then_inc(pool_step, p.gives(pool_step))
                eng.wait_ge(pool_step, p.given(pool_step))
                eng.tensor_tensor(x2, tmp[2], tmp[3], ALU.add).then_inc(gained, p.gives(gained))

            def do(step_, i):
                if step_ == "hg_norm":
                    for t in range(NT):
                        o = hgO[:, t]
                        gains([(heads(o, HEADS), repeat(row("hg_onorm"), HEADS))],
                              lambda: eng.tensor_tensor(o, o, TM[:, t, 512:1024], ALU.mult).then_inc(
                                  gained, p.gives(gained)))
                elif step_ == "c_norm":
                    gains([(CM[:, :, 0:QR], repeat(row("mla_q_norm"), NT))])
                    gains([(CM[:, :, QR:QR + KVR], repeat(row("mla_kv_norm"), NT))])
                elif step_ == "up":
                    qk = heads(qk_tile[i % 2], 2 * HEADS)
                    p.mark(handed[1])
                    gains([(qk[:, k * HEADS:(k + 1) * HEADS], repeat(row("mla_qk_norm", k * QKD, QKD), HEADS))
                           for k in range(2)], lambda: rope(qk, i))
                elif step_ == "dif_norm":
                    gains([(heads(DQK[:, i, k * 512:(k + 1) * 512], 8), repeat(row("diff_qk_norm", k * HD, HD), 8))
                           for k in range(2)])
                elif step_ == "swa_norm":
                    gains([(heads(SQKV[:, i, 0:512], 8), repeat(row("swa_qk_norm", 0, HD), 8)),
                           (heads(SQKV[:, i, 512:640], 2), repeat(row("swa_qk_norm", HD, HD), 2))])
                elif step_ == "dif_post":
                    for t in range(NT):
                        p.mark(handed[t % 2])
                        gains([(heads(y_tok["diff"][:, t], DH), repeat(row("diff_onorm"), DH))])

            eng.wait_ge(rope_ready, p.next(rope_ready, 2))
            p.mark(handed[1])
            with p.loop("layer", DEPTH):
                p.mark(handed[2])
                eng.wait_ge(rows_ready, p.next(rows_ready))
                alone()
                for pr in range(4):
                    for j in range(9):
                        i = (9 * pr + j) % 2
                        if j == 0:
                            p.mark(e_ready[i])
                            p.mark(qk_used[i])
                            continue
                        eng.wait_ge(e_ready[i], p.next(e_ready[i]))
                        if j < 8:
                            eng.wait_ge(qk_used[i], p.so_far(qk_used[i]))
                            p.mark(qk_used[i])
                            eng.tensor_tensor(hgQs[i], hgQ[:, pr], hgE[i], ALU.mult).then_inc(
                                qs_ready[i], p.gives(qs_ready[i]))
                        else:
                            eng.wait_ge(attn_used[pr % 2], p.so_far(attn_used[pr % 2]))
                            p.mark(attn_used[pr % 2])
                            eng.tensor_tensor(hgQin[pr % 2], hgQ[:, pr], hgE[i], ALU.mult).then_inc(
                                qin_ready, p.gives(qin_ready))
                for st, i in SCHEDULE:
                    do(st, i)
                with p.loop("merge", 2) as g:
                    for br in range(NB):
                        for j in range(4):
                            i = j % 2
                            p.mark(handed[2 + i])
                            if not br:
                                continue
                            eng.wait_ge(handed[i], p.next(handed[i]))
                            alone()
                            m = pick(merged, g * 4 + j)
                            eng.tensor_tensor(m, m, SC[:, 4 + i], ALU.add).then_inc(added[i], p.gives(added[i]))
                p.mark(handed[1])
                p.mark(handed[2])
                eng.wait_ge(comb_loaded, p.next(comb_loaded, 16))
                alone()
                with p.loop("moe", NG) as g:
                    for e in range(4):
                        for m in range(2):
                            eng.wait_ge(handed[2 + m], p.next(handed[2 + m]))
                            alone()
                            s = SC[:, 2 * (e % 2) + m]
                            eng.tensor_tensor(s, s, pick(comb, g * 4 + e), ALU.mult).then_inc(
                                weighted, p.gives(weighted))


_INS = ("x c positions ada_w ada_b norm_mix norm_ffn w_in hg_lb_logits hg_onorm mla_q_norm mla_kv_norm "
        "mla_w_uq mla_w_ukv mla_qk_norm diff_qk_norm diff_lam diff_onorm swa_qk_norm swa_sinks w_branch "
        "w_out router_w router_bias moe_w_gate moe_w_up moe_w_down").split()


def program(nc, inputs, rate):
    dts = {"float32": F32, "int32": I32}
    args = {n: nc.dram_tensor(f"in_{n}", inputs[n].shape, dts[str(inputs[n].dtype)], kind="ExternalInput").ap()
            for n in _INS}
    out = nc.dram_tensor("out_x", (1, S, D), F32, kind="ExternalOutput").ap()
    scratch = nc.dram_tensor("expert_weights", (NE, S), F32, kind="Internal").ap()
    build(nc, args, out, scratch, rate)


def kernel(**inputs):
    import numpy as _np
    import concourse.bacc as _bacc
    from concourse.bass_utils import run_bass_kernel_spmd as _run

    arrays = {n: _np.ascontiguousarray(inputs[n]) for n in _INS}
    rate = {}
    for _ in range(2):
        nc = _bacc.Bacc("TRN2", target_bir_lowering=False, num_devices=1)
        program(nc, arrays, rate)
    r = _run(nc, [{f"in_{n}": x for n, x in arrays.items()}], core_ids=[0])
    return r.results[0]["out_x"]
```

```python
import math
from contextlib import ExitStack, contextmanager

import numpy as np

import concourse.bass as bass
from concourse import mybir
from concourse.alu_op_type import AluOpType as ALU

F32, F32R, I32 = mybir.dt.float32, mybir.dt.float32r, mybir.dt.int32
ACT = mybir.ActivationFunctionType
AX = mybir.AxisListType.X

P = 128
D, S, DEPTH = 1024, 512, 2
NT, NC = S // P, D // P
EPS = 1e-6
HEADS, HD = 8, 64
QR, KVR, NOPE, ROPE = 256, 128, 64, 32
QKD = NOPE + ROPE
HALF = ROPE // 2
DH, DV = 4, 128
BW, NB = 512, 4
NE, NG, FF = 16, 4, 256
PER = NE // NG
SLOT = 2048
RING = 4
FRONT = 29
LEVELS = 7
NEG = -1e30
LN0 = -1e30

WIDTHS = (512, 512, 512, 512, QR, KVR, ROPE, 512, 512, 512, 512, 128, 128, NB * D)
COL = dict(zip("hq hf hi hg cq ckv kr dq dk dv sq sk sv gate".split(),
               (sum(WIDTHS[:i]) for i in range(len(WIDTHS)))))
N_IN = sum(WIDTHS)

ROWS = (("hg_onorm", 64), ("mla_q_norm", QR), ("mla_kv_norm", KVR), ("mla_qk_norm", 2 * QKD),
        ("diff_qk_norm", 128), ("diff_onorm", DV), ("swa_qk_norm", 128), ("swa_sinks", 8),
        ("diff_lam", 256))
ROW_AT = {}
for _n, _w in ROWS:
    ROW_AT[_n] = (sum(w for _, w in ROW_AT.values()), _w)
NROW = sum(w for _, w in ROWS)
NCOLP = 6 * NC + 2 * NC


PRIMED = ("emptied handed slot_used sq_used qk_used attn_used tile_used "
          "added params_used qs_ready split_used diag_used weights_used").split()


class Program:

    def __init__(self, eng, name, rate):
        self.eng, self.name, self.rate = eng, name, rate
        self.count, self.frames = {}, []

    def value(self, kind, sem, less=0):
        key = kind, sem.name
        v, fixed = None, self.count.get(key, 0) + (sem.name.rstrip("0123456789") in PRIMED) - less
        path = ()
        for loop, i, before in self.frames:
            path += (loop,)
            fixed += before.get(key, 0)
            r = self.rate.get((self.name, path, key), 0)
            if r:
                v = i * r if v is None else v + i * r
        if v is None:
            return fixed
        assert fixed > 0, key
        return v + fixed

    def mark(self, sem, n=1):
        key = "seen", sem.name
        self.count[key] = self.count.get(key, 0) + n

    def next(self, sem, n=1):
        self.mark(sem, n)
        return self.value("seen", sem)

    def so_far(self, sem):
        return self.value("seen", sem)

    def gives(self, sem, n=1):
        key = "sent", sem.name
        self.count[key] = self.count.get(key, 0) + n
        return n

    def given(self, sem, less=0):
        return self.value("sent", sem, less)

    @contextmanager
    def loop(self, name, n):
        with self.eng.Fori(0, n) as i:
            self.frames.append((name, i, self.count))
            self.count = {}
            yield i
            path = tuple(f[0] for f in self.frames)
            done, self.count = self.count, self.frames.pop()[2]
        for key, c in done.items():
            self.rate[self.name, path, key] = c
            self.count[key] = self.count.get(key, 0) + c * n


class Sweep:

    def __init__(self, kind, per_tile):
        self.kind, self.per_tile, self.units = kind, per_tile, NT * per_tile

    def tile(self, n):
        return n // self.per_tile

    def head(self, n):
        h = n % self.per_tile
        return (h % 2) * 4 + h // 2 if self.kind == "swa" else h

    def first(self, n):
        return n % self.per_tile == 0

    def last(self, n):
        return n % self.per_tile == self.per_tile - 1

    def banks(self, n):
        return (6, 7) if self.kind == "diff" else (6 + n % 2,)

    def blocks(self, n):
        t = self.tile(n)
        return list(range(max(t - 1, 0) if self.kind == "swa" else 0, t + 1))


MLA, DIFF, SWA = Sweep("mla", HEADS), Sweep("diff", DH), Sweep("swa", HEADS)

SCHEDULE = [("hg_norm", 0), ("c", 0), ("c", 1), ("hg_y", 0), ("c_norm", 0), ("c", 2), ("c_turn", 0),
            ("up", 0), ("c", 3), ("up", 1), ("turn", 0), ("c", 4), ("up", 2), ("turn", 1), ("up", 3),
            ("turn", 2), ("c", 5), ("turn", 3), ("sweep", MLA),
            ("dif_norm", 0), ("d", 0), ("dif_norm", 1), ("d", 1), ("dif_norm", 2), ("d", 2),
            ("dif_norm", 3), ("mla_y", 0), ("swa_norm", 0), ("swa_norm", 1), ("swa_norm", 2),
            ("swa_norm", 3), ("dif_turn", 0), ("swa_turn", 0), ("sweep", DIFF), ("dif_post", 0),
            ("sweep", SWA), ("dif_y", 0), ("swa_y", 0)]


def build(nc, a, out, rate):
    with ExitStack() as ctx:
        place = {}

        def sb(name, *shape, dt=F32):
            place[name] = -(-nc.sbuf_base // 32) * 32
            return ctx.enter_context(nc.sbuf_tensor(name, [P, *shape], dt))

        def rounded(name, lo, n):
            return nc.alloc_sbuf_tensor_at(f"{name}_{lo}_rounded", [P, n], F32R, offset=place[name] + 4 * lo)[:, :]

        ring = sb("ring", RING, SLOT)
        X = sb("X", NC, S)
        H = sb("H", NC, S)
        M16 = sb("M16", 4096)
        Y = sb("Y", NB, NT, S)
        TM = sb("TM", NT, 1024)
        CM = sb("CM", NT, 416)
        DQK = sb("DQK", NT, 1024)
        DVt = sb("DVt", NT, 512)
        SQKV = sb("SQKV", NT, 768)
        SC = sb("SC", 6, S)
        ident = sb("ident", P)
        ones = sb("ones", P)
        cmask = sb("cmask", P)
        swmask = sb("swmask", 2 * P)
        lmask = sb("lmask", LEVELS, P)
        rows = sb("rows", NROW)
        bias_row = sb("bias_row", NE)
        pcols = sb("pcols", P)
        colT = sb("colT", NCOLP)
        mod = sb("mod", 6 * NC)
        gain = sb("gain", NC)
        cact = sb("cact", NC)
        rw = sb("rw", NC, NE)
        cosT = sb("cosT", NT, HALF)
        sinT = sb("sinT", NT, HALF)
        ang = sb("ang", NT, HALF)
        angk = sb("angk", 2, NT, HALF)
        ifr = sb("ifr", HALF)
        posi = sb("posi", NT, dt=I32)
        posf = sb("posf", NT)
        lbz = sb("lbz", 2, NT)
        lbt = sb("lbt", DEPTH, 2 * NT)
        lbc = sb("lbc", 2 * NT)
        lbw = sb("lbw", 2, NT)
        litab = sb("litab", DEPTH, 2)
        lic = sb("lic", 2)
        lamp = sb("lamp", 2, HD)
        lams = sb("lams", 4)
        neglam = sb("neglam", 1)
        consts = sb("consts", 2)
        ssq = sb("ssq", 16)
        rsq = sb("rsq", 16)
        edec = sb("edec", NT)
        nmax = sb("nmax", 2, 2)
        lsum = sb("lsum", 2, HEADS)
        lrec = sb("lrec", HEADS)
        esink = sb("esink", 2, HEADS)
        nsink = sb("nsink", HEADS)
        dl = sb("dl", 2, 2)
        dr = sb("dr", 2)
        rt = sb("rt", 6, NT * NE)
        rg = sb("rg", 6, NT * NG)
        wexp = sb("wexp", NE)
        wgrp = sb("wgrp", NG)

        spare = sb("spare", 3 * S)

        ps = ctx.enter_context(nc.psum_tensor("ps", [P, 8, 512], F32))
        def signal(name):
            return ctx.enter_context(nc.semaphore(name))

        def signals(name, n=2):
            return [signal(f"{name}{i}") for i in range(n)]

        filled, emptied, handed = (signals(n, 8) for n in ("filled", "emptied", "handed"))
        slot_loaded, slot_used = (signals(n, RING) for n in ("slot_loaded", "slot_used"))
        (sq_ready, sq_used, d_ready, e_ready, qs_ready, ks_ready, qk_used, attn_used, tile_used,
         added, split_used, high_ready, diag_ready, diag_used, weights_used) = (signals(n) for n in (
             "sq_ready", "sq_used", "d_ready", "e_ready", "qs_ready", "ks_ready", "qk_used",
             "attn_used", "tile_used", "added", "split_used", "high_ready",
             "diag_ready", "diag_used", "weights_used"))
        (x_loaded, router_loaded, c_loaded, positions_loaded, lb_loaded, bias_loaded, rows_loaded,
         cols_loaded, out_stored) = (signal(n) for n in (
             "x_loaded", "router_loaded", "c_loaded", "positions_loaded", "lb_loaded", "bias_loaded",
             "rows_loaded", "cols_loaded", "out_stored"))
        vector_step, scalar_step, pool_step = (
            signal(n) for n in ("vector_step", "scalar_step", "pool_step"))
        (constants_ready, lbdiff_ready, lbln_ready, angles_ready, rope_ready, cact_ready,
         params_used, rows_ready, lamsum_ready, lamexp_ready, h_ready, f_ready, ln_ready, logk_ready,
         k_ready, logt_ready, logaddexp_ready, b_ready, qin_ready, edec_ready, squares_ready,
         sums_ready, rms_ready, normed, gained, rowmax_ready, probs_ready, comb_ready,
         scaled, summed, act_high, act_ready) = (signal(n) for n in (
             "constants_ready", "lbdiff_ready", "lbln_ready", "angles_ready", "rope_ready",
             "cact_ready", "params_used", "rows_ready", "lamsum_ready", "lamexp_ready", "h_ready",
             "f_ready", "ln_ready", "logk_ready", "k_ready", "logt_ready", "logaddexp_ready",
             "b_ready", "qin_ready", "edec_ready", "squares_ready", "sums_ready", "rms_ready",
             "normed", "gained", "rowmax_ready", "probs_ready", "comb_ready", "scaled",
             "summed", "act_high", "act_ready"))
        waited = {n: signal(f"waited_{n}") for n in ("sp", "pe", "dve", "pool")}

        block = ctx.enter_context(nc.Block())

        class Ring:

            def __init__(self, p):
                self.p, self.pos = p, 0

            def next(self, n=1):
                for _ in range(n):
                    j = self.pos % RING
                    self.pos += 1
                    self.p.mark(slot_loaded[j], 64)
                    self.p.mark(slot_used[j])
                return j

            def wrap(self):
                self.pos += (-self.pos) % RING

        def row(name, lo=0, n=None):
            at, w = ROW_AT[name]
            return rows[:, at + lo:at + lo + (w if n is None else n)]

        def bank(b, n=512):
            return ps[:, b, 0:n]

        def bank3(b, k, n):
            return ps[:, b, 0:k * n].rearrange("p (k n) -> p k n", k=k)

        def tt(t):
            return slice(t * P, (t + 1) * P)

        def heads(ap, n):
            return ap.rearrange("p (h d) -> p h d", h=n)

        def flat(ap):
            return ap.rearrange("p a b -> p (a b)")

        def spread(ap, n):
            return ap.unsqueeze(2).to_broadcast([P, ap.shape[1], n])

        def repeat(ap, n):
            return ap.unsqueeze(1).to_broadcast([P, n, ap.shape[1]])

        def pick(ap, i):
            return ap[:, bass.ds(i, 1)].rearrange("p a s -> p (a s)")

        M3 = M16[:, :].rearrange("p (c s) -> p c s", c=NC)
        xin = M16[:, :].rearrange("p (t d) -> p t d", t=NT)
        hgQ, hgB, hgK = M3[:, 0:4], M3[:, 4:8], Y[:, 2]
        hgO = Y[:, 3]
        hgE = [Y[:, 0, i] for i in range(2)]
        hgQs = [Y[:, 0, 2 + i] for i in range(2)]
        hgKs = [Y[:, 1, i] for i in range(2)]
        hgQin = [Y[:, 1, 2 + i] for i in range(2)]
        attnT = [[heads(DQK[:, i, h * S:(h + 1) * S], NT) for h in range(2)] for i in range(2)]
        KdT = [heads(DQK[:, 2, i * S:(i + 1) * S], NT) for i in range(2)]
        state = [heads(DQK[:, 3, i * S:(i + 1) * S], NT) for i in range(2)]
        cT = Y[:, 3]
        sqkv = flat(SQKV[:, :, :])
        qk_tile = [sqkv[:, i * 1536:(i + 1) * 1536] for i in range(2)]
        TM8 = flat(TM[:, :, :]).rearrange("p (h s) -> p h s", h=8)
        mlaQ, mlaK, mlaV = TM8, M3, Y[:, 2]
        difQ, difK = M3[:, 0:4], M3[:, 4:8]
        swaQ, swaK = TM8[:, 0:4], TM8[:, 4]
        swa_sq = flat(TM8[:, 5:7])[:, 0:640]
        sc = flat(SC[:, :, :])
        y_tok = {"mla": Y[:, 3], "diff": flat(DQK[:, 0:2]).rearrange("p (t s) -> p t s", t=NT),
                 "swa": flat(DQK[:, 2:4]).rearrange("p (t s) -> p t s", t=NT)}
        probs = [[SC[:, 2 * i + j] for j in range(2)] for i in range(2)]
        probsT = [heads(SC[:, 4 + i], NT) for i in range(2)]
        merged = M3
        scores_T = SC[0:NE, 3]
        chunks = lambda ap: [ap[:, k * S:(k + 1) * S] for k in range(ap.shape[1] // S)]
        split = [rounded(name, 0, 2 * SLOT) for name in ("TM", "DQK")]
        high = [ap[:, 0:SLOT] for ap in split]
        low = [ap[:, SLOT:2 * SLOT] for ap in split]
        Hc, Mc = ([x[:, k] for k in range(NC)] for x in (H, M3))
        H_lo, M_r = chunks(rounded("H", 0, NC * S)), chunks(rounded("M16", 0, NC * S))
        act_hi = chunks(rounded("SQKV", 0, 6 * S)) + chunks(rounded("DVt", 0, 2 * S))
        hid = chunks(flat(DVt[:, :, :]))[2:] + chunks(spare[:, :]) + chunks(flat(CM[:, :, :]))
        hid_lo = (chunks(rounded("DVt", 2 * S, 2 * S)) + chunks(rounded("spare", 0, 3 * S))
                  + chunks(rounded("CM", 0, 3 * S)))
        acc = spare[:, 0:D], sc[:, 4 * S:]

        def swa_cols(t, u):
            if u == 2:
                return SQKV[:, t, 512:768]
            return SQKV[:, t, 0:512].rearrange("p (a g d) -> p g a d", a=4, g=2)[:, u]

        def norm_of(step, t):
            if step == "hg_norm":
                return hgO[:, t], SC[:, 0], HEADS, HD
            if step == "c_norm":
                w, at = ((QR, 0), (KVR, QR))[t]
                return CM[:, :, at:at + w], sc[:, 0:NT * w], NT, w
            if step == "up":
                return qk_tile[t % 2], sc[:, 0:1536], 2 * HEADS, QKD
            if step == "dif_norm":
                return DQK[:, t], sc[:, 0:1024], 16, HD
            if step == "swa_norm":
                return SQKV[:, t, 0:640], swa_sq, 10, HD
            return y_tok["diff"][:, t], SC[:, 0], DH, DV

        @block.sync
        def _(eng):
            p = Program(eng, "sp", rate)

            def alone():
                eng.sem_inc(waited["sp"], 1)

            xd = a["x"].rearrange("b (t p) d -> p (b t) d", p=P)
            for t in range(NT):
                eng.dma_start(xin[:, t], xd[:, t]).then_inc(x_loaded, p.gives(x_loaded, 16))
            eng.dma_start(rw[:, :, :], a["router_w"].rearrange("(k p) e -> p k e", p=P)).then_inc(
                router_loaded, p.gives(router_loaded, 16))
            pos = [0]

            def load(parts):
                j = pos[0] % RING
                pos[0] += 1
                eng.wait_ge(slot_used[j], p.so_far(slot_used[j]))
                alone()
                for dst, src in parts(j):
                    eng.dma_start(dst, src).then_inc(slot_loaded[j], p.gives(slot_loaded[j], 16))
                p.mark(slot_used[j])

            def layer(name, i):
                ap = a[name][bass.ds(i, 1)]
                return ap.rearrange("a b c -> (a b) c") if len(ap.shape) == 3 else ap

            def cols(w, c0, n):
                def parts(j):
                    src = w.rearrange("(k p) n -> p k n", p=P)
                    dst = ring[:, j, 0:NC * n].rearrange("p (k n) -> p k n", k=NC)
                    for h in range(4):
                        yield dst[:, 2 * h:2 * h + 2], src[:, 2 * h:2 * h + 2, bass.ds(c0, n)]
                return parts

            def uq(w):
                def parts(j):
                    for h in range(4):
                        k, c = h // 2, (h % 2) * 384
                        yield ring[:, j, k * 768 + c:k * 768 + c + 384], w[k * P:(k + 1) * P, c:c + 384]
                return parts

            def ukv(w):
                def parts(j):
                    for h in range(4):
                        yield ring[:, j, h * 256:(h + 1) * 256], w[:, h * 256:(h + 1) * 256]
                return parts

            with p.loop("layer", DEPTH) as l:
                eng.wait_ge(params_used, p.so_far(params_used))
                p.mark(params_used)
                for name, w in ROWS:
                    src = a[name][bass.ds(l, 1)]
                    if len(src.shape) == 3:
                        src = src.rearrange("a b c -> a (b c)")
                    eng.dma_start(row(name), src.partition_broadcast(P).rearrange("p a w -> p (a w)")).then_inc(
                        rows_loaded, p.gives(rows_loaded, 16))
                for lo, name, n in ((0, "ada_b", 48), (48, "norm_mix", NC), (56, "norm_ffn", NC)):
                    eng.dma_start(pcols[lo:lo + n, :],
                                         a[name][bass.ds(l, 1)].rearrange("a (k p) -> (a k) p", p=P)).then_inc(
                        cols_loaded, p.gives(cols_loaded, 16))
                w_in = layer("w_in", l)
                with p.loop("ada", 2) as s:
                    for u in range(4):
                        load(cols(layer("ada_w", l), s * D + u * 256, 256))
                for c in ("hf", "hq", "hi", "hg"):
                    for u in range(2):
                        load(cols(w_in, COL[c] + u * 256, 256))
                load(cols(w_in, COL["cq"], 256))
                load(cols(w_in, COL["ckv"], KVR + ROPE))
                for u in range(3):
                    load(cols(w_in, COL["dq"] + u * 256, 256))
                load(uq(layer("mla_w_uq", l)))
                load(ukv(layer("mla_w_ukv", l)))
                for u in range(3, 6):
                    load(cols(w_in, COL["dq"] + u * 256, 256))
                for u in range(3):
                    load(cols(w_in, COL["sq"] + u * 256, 256))
                with p.loop("merge", 2) as g:
                    for b in range(NB):
                        def branch(j, b=b):
                            src = a["w_branch"][bass.ds(l, 1), b].rearrange("a (k p) n -> p (a k) n", p=P)
                            for h in range(4):
                                yield ring[:, j, h * 512:(h + 1) * 512], src[:, h, bass.ds(g * 512, 512)]
                        for u in range(2):
                            load(cols(w_in, g * 512 + (COL["gate"] + b * D + u * 256), 256))
                        load(branch)
                        for u in range(2):
                            load(cols(layer("ada_w", l), g * (2 * D) + ((2 + b // 2) * D + (b % 2 * 2 + u) * 256), 256))
                for u in range(4):
                    load(cols(layer("w_out", l), u * 256, 256))
                with p.loop("moe", NG) as g:
                    for e in range(4):
                        for name in ("moe_w_gate", "moe_w_up"):
                            w = a[name].rearrange("l e k n -> (l e) k n")[bass.ds(l * NE + g * 4 + e, 1)]
                            load(cols(w.rearrange("a k n -> (a k) n"), 0, FF))
                    wd = a["moe_w_down"].rearrange("l e (j p) n -> (l e) p j n", p=P)
                    for u in range(4):
                        def down(j, u=u):
                            dst = ring[:, j].rearrange("p (e j n) -> p e j n", e=4, j=2)
                            for e in range(4):
                                src = wd[bass.ds(l * NE + g * 4 + e, 1)].rearrange("a p j n -> p (a j) n")
                                yield dst[:, e], src[:, :, u * 256:(u + 1) * 256]
                        load(down)
                pos[0] += (-pos[0]) % RING

        @block.tensor
        def _(eng):
            p = Program(eng, "pe", rate)
            for sem in (*slot_used, *sq_used, *qk_used, *attn_used, *tile_used, *split_used, *diag_used):
                eng.sem_inc(sem, 1)

            def alone():
                eng.sem_inc(waited["pe"], 1)

            owed = []
            ring_at = Ring(p)

            def later(sem):
                owed.append(sem)

            def free(b):
                eng.wait_ge(emptied[b], p.so_far(emptied[b]))
                eng.wait_ge(handed[b], p.so_far(handed[b]))

            def mm(o, lhsT, rhs, start=True, stop=True, last=False, transpose=False):
                if transpose:
                    ins = nc.tensor.transpose(o, lhsT, rhs)
                else:
                    ins = nc.tensor.matmul(o, lhsT, rhs, start=start, stop=stop)
                if owed and not last:
                    ins.then_inc(owed[0], p.gives(owed.pop(0)))
                return ins

            def turn(o, src, k=P, last=False):
                return mm(o, src, ident[0:k, 0:k], last=last, transpose=True)

            @contextmanager
            def loop(name, n):
                def settle():
                    while owed:
                        turn(ps[0:32, 7, 0:32], ident[0:32, 0:32], k=32)

                free(7)
                alone()
                settle()
                with p.loop(name, n) as i:
                    yield i
                    settle()

            def slot():
                j = ring_at.next()
                eng.wait_ge(slot_loaded[j], p.so_far(slot_loaded[j]))
                return j

            def w3(j, n):
                return ring[:, j, 0:NC * n].rearrange("p (k n) -> p k n", k=NC)

            splits = [0]

            def parts():
                splits[0] += 1
                return (splits[0] - 1) % 2

            def product(b, i, m, hi, lo, ready=None):
                wh, wl = (heads(x[i], NC)[:, :, tt(m)] for x in (high, low))
                for k in range(NC):
                    if ready is not None:
                        eng.wait_ge(act_ready, ready[k])
                    xh, xl = hi[k], lo[k]
                    mm(bank(b), wh[:, k], xh, k == 0, False)
                    mm(bank(b), wh[:, k], xl, False, False)
                    ins = mm(bank(b), wl[:, k], xh, False, k == NC - 1, last=k == NC - 1)
                return ins

            def fresh():
                return [p.next(act_ready) for _ in range(NC)]

            def tokens(n, banks, bys):
                j = slot()
                w = w3(j, n)
                for t in range(NT):
                    b = banks[t]
                    free(b)
                    for k in range(NC):
                        last = k == NC - 1
                        ins = mm(bank(b, n), H[:, k, tt(t)], w[:, k], k == 0, k == NC - 1, last=last)
                        if last:
                            ins.then_inc(filled[b], p.gives(filled[b]))
                            p.mark(bys[t][b])
                later(slot_used[j])

            def features(banks, bys=None, ready=None):
                j = slot()
                w = w3(j, 256)
                for m in range(2):
                    b = banks[m]
                    free(b)
                    for k in range(NC):
                        if ready is not None and m == 0:
                            eng.wait_ge(h_ready, ready[k])
                        last = k == NC - 1
                        ins = mm(bank(b), w[:, k, tt(m)], H[:, k], k == 0, k == NC - 1, last=last)
                        if last:
                            ins.then_inc(filled[b], p.gives(filled[b]))
                            p.mark((bys or (emptied,) * 2)[m][b])
                later(slot_used[j])

            eng.wait_ge(constants_ready, p.next(constants_ready))
            eng.wait_ge(x_loaded, p.next(x_loaded, 64))
            for c in range(NC):
                free(c % 2)
                for t in range(NT):
                    last = t == NT - 1
                    ins = turn(ps[:, c % 2, tt(t)], xin[:, t, tt(c)], last=last)
                    if last:
                        ins.then_inc(filled[c % 2], p.gives(filled[c % 2]))
                        p.mark((handed if c == NC - 1 else emptied)[c % 2])
            eng.wait_ge(router_loaded, p.next(router_loaded, 16))
            eng.wait_ge(cact_ready, p.next(cact_ready))

            def square_sum(c):
                if c == 0:
                    free(2)
                eng.wait_ge(sq_ready[c % 2], p.next(sq_ready[c % 2]))
                ins = mm(bank(2), ones[:, :], SC[:, c % 2], c == 0, c == NC - 1, last=True)
                if c == NC - 1:
                    ins.then_inc(filled[2], p.gives(filled[2]))
                    p.mark(handed[2])
                    later(sq_used[c % 2])
                else:
                    ins.then_inc(sq_used[c % 2], p.gives(sq_used[c % 2]))

            def y_turn(src, br):
                for t in range(NT):
                    b = 2 + t % 2
                    free(b)
                    if br in (0, 2):
                        eng.wait_ge(gained, p.next(gained))
                    else:
                        eng.wait_ge(emptied[t % 2], p.so_far(emptied[t % 2]))
                    for k in range(4):
                        last = k == 3
                        ins = turn(ps[:, b, tt(k)], src[:, t, tt(k)], last=last)
                        if last:
                            ins.then_inc(filled[b], p.gives(filled[b]))
                            p.mark(emptied[b])

            def levels(pr):
                i = (9 * pr) % 2
                eng.wait_ge(ks_ready[i], p.next(ks_ready[i]))
                free(2)
                for c in range(NT):
                    last = c == 3
                    ins = turn(ps[:, 2, tt(c)], hgKs[i][:, tt(c)], last=last)
                    if last:
                        ins.then_inc(filled[2], p.gives(filled[2]))
                        p.mark(emptied[2])
                later(qk_used[i])
                for lv in range(LEVELS + 1):
                    if lv:
                        i = (9 * pr + lv) % 2
                        eng.wait_ge(qs_ready[i], p.next(qs_ready[i]))
                        eng.wait_ge(ks_ready[i], p.next(ks_ready[i]))
                        q, k = hgQs[i], hgKs[i]
                    else:
                        q, k = hgQ[:, pr], hgK[:, pr]
                    for hp in range(2):
                        b = (lv % 2) * 4 + hp
                        free(b)
                        for c in range(NT):
                            r = slice(hp * HD, (hp + 1) * HD)
                            last = c == 3
                            ins = mm(ps[:, b, tt(c)], k[r, tt(c)], q[r, tt(c)], last=last)
                            if last:
                                ins.then_inc(filled[b], p.gives(filled[b]))
                                p.mark(emptied[b])
                    if lv:
                        later(qk_used[i])
                    if lv == 4:
                        eng.wait_ge(emptied[2], p.so_far(emptied[2]))
                        free(0)
                        for c in range(3):
                            last = c == 2
                            ins = mm(ps[:, 0, tt(c)], KdT[pr % 2][:, c], TM[:, c, tt(pr)], last=last)
                            if last:
                                ins.then_inc(filled[0], p.gives(filled[0]))
                                p.mark(emptied[0])

            def chunk_outputs(pr):
                for b in (0, 1, 4, 5):
                    eng.wait_ge(emptied[b], p.so_far(emptied[b]))
                eng.wait_ge(qin_ready, p.next(qin_ready))
                b = 6 + pr % 2
                free(b)
                for c in range(NT):
                    o = ps[:, b, tt(c)]
                    if c:
                        mm(o, hgQin[pr % 2][:, tt(c)], state[pr % 2][:, c], True, False)
                    for h in range(2):
                        last = c == 3 and h == 1
                        ins = mm(o[:, h * HD:(h + 1) * HD], attnT[pr % 2][h][:, c], TM[:, c, pr * P + h * HD:pr * P + (h + 1) * HD], c == 0, c == 0 or h == 1, last=last)
                        if last:
                            ins.then_inc(filled[b], p.gives(filled[b]))
                            p.mark(emptied[b])
                later(attn_used[pr % 2])

            held = {}

            def up(t):
                if t == 0:
                    held["uq"], held["ukv"] = slot(), slot()
                wq = ring[:, held["uq"], 0:1536].rearrange("p (k n) -> p k n", k=2)
                wkv = ring[:, held["ukv"], 0:1024]
                for f in range(2):
                    free(f)
                    for k in range(2):
                        last = k == 1
                        ins = mm(bank(f, 384), cT[:, k, tt(t)], wq[:, k, f * 384:(f + 1) * 384], k == 0, k == 1, last=last)
                        if last:
                            ins.then_inc(filled[f], p.gives(filled[f]))
                            p.mark((emptied, handed)[f][f])
                for f in range(2):
                    free(6 + f)
                    mm(bank(6 + f), cT[:, 2, tt(t)], wkv[:, f * 512:(f + 1) * 512], last=True).then_inc(
                        filled[6 + f], p.gives(filled[6 + f]))
                    p.mark(emptied[6 + f])
                if t == 3:
                    later(slot_used[held['uq']])
                    later(slot_used[held['ukv']])

            def mla_turn(t):
                qk = heads(qk_tile[t % 2], 2 * HEADS)
                eng.wait_ge(gained, p.next(gained))
                for f in range(4):
                    b = 2 + f % 2
                    free(b)
                    for h in range(4):
                        last = h == 3
                        ins = turn(ps[0:QKD, b, tt(h)], qk[:, 4 * f + h], last=last)
                        if last:
                            ins.then_inc(filled[b], p.gives(filled[b]))
                            p.mark(emptied[b])
                later(tile_used[t % 2])

            def scores(s, n):
                t, h, kt = s.tile(n), s.head(n), s.blocks(n)
                keys = slice(kt[0] * P, (t + 1) * P)
                w = len(kt) * P
                if s.kind == "mla":
                    parts = [(mlaQ[0:QKD, h, tt(t)], mlaK[0:QKD, h, keys])]
                elif s.kind == "diff":
                    parts = [(difQ[r, h, tt(t)], difK[r, h, keys]) for r in (slice(0, HD), slice(HD, P))]
                else:
                    r = slice((h // 4) * HD, (h // 4 + 1) * HD)
                    parts = [(swaQ[r, h % 4, tt(t)], swaK[r, keys])]
                for b, (q, k) in zip(s.banks(n), parts):
                    free(b)
                    mm(bank(b, w), q, k, last=True).then_inc(filled[b], p.gives(filled[b]))
                    p.mark((handed if s.kind == "diff" else emptied)[b])

            def turn_probs(s, n):
                if s.kind == "diff":
                    eng.wait_ge(probs_ready, p.next(probs_ready))
                else:
                    eng.wait_ge(emptied[s.banks(n)[0]], p.so_far(emptied[s.banks(n)[0]]))
                b = 2 + n % 2
                free(b)
                kt = s.blocks(n)
                for i in range(len(kt)):
                    last = i == len(kt) - 1
                    ins = turn(ps[:, b, tt(i)], probs[n % 2][0][:, tt(i)], last=last)
                    if last:
                        ins.then_inc(filled[b], p.gives(filled[b]))
                        p.mark(emptied[b])

            def values(s, n):
                t, h, kt = s.tile(n), s.head(n), s.blocks(n)
                eng.wait_ge(emptied[2 + n % 2], p.so_far(emptied[2 + n % 2]))
                b = t % 2
                if s.first(n):
                    free(b)
                d = DV if s.kind == "diff" else HD
                for i, k in enumerate(kt):
                    v = {"mla": lambda: mlaV[:, k, h * d:(h + 1) * d],
                         "diff": lambda: DVt[:, k, h * d:(h + 1) * d],
                         "swa": lambda: SQKV[:, k, 640 + (h // 4) * d:640 + (h // 4 + 1) * d]}[s.kind]()
                    end = i == len(kt) - 1
                    last = end and s.last(n)
                    ins = mm(ps[:, b, h * d:(h + 1) * d], probsT[n % 2][:, i], v, i == 0, end, last=last)
                    if last:
                        ins.then_inc(filled[b], p.gives(filled[b]))
                        p.mark((handed if s.kind == "diff" else emptied)[b])

            def sweep(s):
                for n in range(s.units + 2):
                    if n < s.units:
                        scores(s, n)
                    if 1 <= n <= s.units:
                        turn_probs(s, n - 1)
                    if n >= 2:
                        values(s, n - 2)

            def section(b, s=0):
                free(b)
                eng.wait_ge(summed, p.next(summed))
                for m in range(NC):
                    last = m == NC - 1
                    ins = mm(ps[:, b, m:m + 1], acc[s][:, tt(m)], ones[:, 0:1], last=last)
                    if last:
                        ins.then_inc(filled[b], p.gives(filled[b]))
                        p.mark(emptied[b])

            all_emptied = (emptied,) * NT

            def do(step, i):
                if step in ("c", "d"):
                    tokens(256, (0, 2, 1, 3), all_emptied)
                elif step == "hg_y":
                    y_turn(hgO, 0)
                elif step == "c_turn":
                    eng.wait_ge(gained, p.next(gained, 2))
                    for t in range(NT):
                        b = 2 + t % 2
                        free(b)
                        for k in range(3):
                            last = k == 2
                            ins = turn(ps[:, b, tt(k)], CM[:, t, tt(k)], last=last)
                            if last:
                                ins.then_inc(filled[b], p.gives(filled[b]))
                                p.mark(emptied[b])
                elif step == "up":
                    up(i)
                elif step == "turn":
                    mla_turn(i)
                elif step == "mla_y":
                    y_turn(y_tok["mla"], 1)
                elif step == "dif_turn":
                    eng.wait_ge(gained, p.next(gained, 4))
                    for t in range(NT):
                        for f in range(2):
                            free(2 + f)
                            for k in range(4):
                                last = k == 3
                                ins = turn(ps[:, 2 + f, tt(k)], DQK[:, t, f * 512 + k * P:f * 512 + (k + 1) * P], last=last)
                                if last:
                                    ins.then_inc(filled[2 + f], p.gives(filled[2 + f]))
                                    p.mark(emptied[2 + f])
                elif step == "swa_turn":
                    eng.wait_ge(gained, p.next(gained, 4))
                    for t in range(NT):
                        free(2)
                        for k in range(4):
                            last = k == 3
                            ins = turn(ps[:, 2, tt(k)], SQKV[:, t, tt(k)], last=last)
                            if last:
                                ins.then_inc(filled[2], p.gives(filled[2]))
                                p.mark(emptied[2])
                        free(3)
                        turn(ps[:, 3, 0:P], SQKV[:, t, 512:640], last=True).then_inc(
                            filled[3], p.gives(filled[3]))
                        p.mark(emptied[3])
                elif step == "sweep":
                    sweep(i)
                elif step == "dif_y":
                    y_turn(y_tok["diff"], 2)
                elif step == "swa_y":
                    y_turn(y_tok["swa"], 3)

            with loop("layer", DEPTH):
                free(0)
                eng.wait_ge(cols_loaded, p.next(cols_loaded, 48))
                alone()
                turn(ps[:, 0, 0:NCOLP], pcols[0:NCOLP, :], k=NCOLP, last=True).then_inc(
                    filled[0], p.gives(filled[0]))
                p.mark(emptied[0])
                for c in range(NC):
                    square_sum(c)
                for s in range(2):
                    ring_at.next(4)
                    section(1, s)
                ready = [p.next(h_ready) for _ in range(NC)]
                for u in range(2):
                    features((0, 1), (emptied, emptied), ready if u == 0 else None)
                for u in range(2):
                    features((2, 3))
                for u in range(2):
                    tokens(256, (0, 2, 1, 3), all_emptied)
                for u in range(2):
                    tokens(256, (2, 3, 2, 3), all_emptied)
                for n in (256, KVR + ROPE):
                    tokens(n, (0, 2, 1, 3), all_emptied)
                eng.wait_ge(k_ready, p.next(k_ready))
                for pr in range(4):
                    levels(pr)
                    chunk_outputs(pr)
                for step, i in SCHEDULE:
                    do(step, i)
                for b in (2, 3):
                    eng.wait_ge(emptied[b], p.so_far(emptied[b]))
                    alone()
                ready = fresh()
                with loop("merge", 2):
                    for br in range(NB):
                        ja, jb, jw = ring_at.next(), ring_at.next(), ring_at.next()
                        wb = ring[:, jw].rearrange("p (k n) -> p k n", k=4)
                        for u, j in enumerate((ja, jb)):
                            eng.wait_ge(slot_used[j], p.so_far(slot_used[j]))
                            i = parts()
                            for m in range(2):
                                free(2 + m)
                                product(2 + m, i, m, act_hi, H_lo, ready if (br, u, m) == (0, 0, 0) else None).then_inc(
                                    filled[2 + m], p.gives(filled[2 + m]))
                                p.mark(handed[2 + m])
                            later(split_used[i])
                            if u == 0:
                                eng.wait_ge(slot_loaded[jw], p.so_far(slot_loaded[jw]))
                            for m in range(2):
                                free(m)
                                for k in range(4):
                                    ins = mm(bank(m), wb[:, k, tt(2 * u + m)], Y[:, br, k], k == 0, k == 3,
                                             last=k == 3)
                                ins.then_inc(filled[m], p.gives(filled[m]))
                                p.mark((handed if br else emptied)[m])
                                if br:
                                    p.mark(added[m])
                        later(slot_used[jw])
                        ring_at.next(2)
                        if br % 2:
                            section(4)
                ready = fresh()
                for u in range(4):
                    j, i = ring_at.next(), parts()
                    eng.wait_ge(slot_used[j], p.so_far(slot_used[j]))
                    for m in range(2):
                        free(m)
                        product(m, i, m, act_hi, M_r, ready if (u, m) == (0, 0) else None).then_inc(
                            filled[m], p.gives(filled[m]))
                        p.mark(handed[m])
                        if u:
                            square_sum(2 * u + m - 2)
                    later(split_used[i])
                for c in (NC - 2, NC - 1):
                    square_sum(c)
                free(6)
                for k in range(NC):
                    eng.wait_ge(h_ready, p.next(h_ready))
                    ins = mm(ps[0:NE, 6], rw[:, k], H[:, k], k == 0, k == NC - 1, last=k == NC - 1)
                ins.then_inc(filled[6], p.gives(filled[6]))
                p.mark(emptied[6])
                free(6)
                free(7)
                alone()
                for t in range(NT):
                    ins = turn(ps[:, 7, t * NE:(t + 1) * NE], scores_T[:, tt(t)], k=NE, last=t == NT - 1)
                ins.then_inc(filled[7], p.gives(filled[7]))
                p.mark(handed[7])
                ready = fresh()
                with loop("moe", NG):
                    for e in range(4):
                        for b in (2, 0):
                            j, i = ring_at.next(), parts()
                            eng.wait_ge(slot_used[j], p.so_far(slot_used[j]))
                            for m in range(2):
                                free(b + m)
                                product(b + m, i, m, act_hi, H_lo, ready if (e, b, m) == (0, 2, 0) else None).then_inc(
                                    filled[b + m], p.gives(filled[b + m]))
                                p.mark(handed[b + m])
                            later(split_used[i])
                        d = e % 2
                        eng.wait_ge(diag_ready[d], p.next(diag_ready[d]))
                        free(6 + d)
                        eng.wait_ge(weights_used[d], p.so_far(weights_used[d]))
                        mm(bank(6 + d), ones[:, :], SC[:, 4 + d], last=True).then_inc(
                            filled[6 + d], p.gives(filled[6 + d]))
                        p.mark(weights_used[d])
                        later(diag_used[d])
                    done = fresh()
                    for u in range(4):
                        j, i = ring_at.next(), parts()
                        eng.wait_ge(slot_used[j], p.so_far(slot_used[j]))
                        for m in range(2):
                            free(4 + m)
                            product(4 + m, i, m, M_r, hid_lo, done if (u, m) == (0, 0) else None).then_inc(
                                filled[4 + m], p.gives(filled[4 + m]))
                            p.mark((handed if (u, m) == (3, 1) else emptied)[4 + m])
                        later(split_used[i])
                ring_at.wrap()
            for b in (4, 5):
                free(b)
            for t in range(NT):
                for f in range(2):
                    free(f)
                    for k in range(4):
                        last = k == 3
                        ins = turn(ps[:, f, tt(k)], X[:, 4 * f + k, tt(t)], last=last)
                        if last:
                            ins.then_inc(filled[f], p.gives(filled[f]))
                            p.mark((emptied, handed)[f][f])

        @block.scalar
        def _(eng):
            p = Program(eng, "act", rate)
            ring_at = Ring(p)
            splits = [0]

            def split_high():
                j, i = ring_at.next(), splits[0] % 2
                splits[0] += 1
                eng.wait_ge(slot_loaded[j], p.so_far(slot_loaded[j]))
                eng.wait_ge(split_used[i], p.so_far(split_used[i]))
                p.mark(split_used[i])
                act(high[i], ring[:, j], ACT.Copy).then_inc(high_ready[i], p.gives(high_ready[i]))

            def acts_high(src, dst, after=None):
                for x, y in zip(src, dst):
                    if after is not None:
                        eng.wait_ge(after, p.next(after))
                    act(y, x, ACT.Copy).then_inc(act_high, p.gives(act_high))

            for b in (2, 3, 6, 7):
                eng.sem_inc(emptied[b], 1)
                eng.sem_inc(handed[b], 1)
            act = nc.scalar.activation




            with nc.allow_non_contiguous_dma(reason="a few hundred parameters, once"):
                eng.dma_start(cact[:, :], a["c"].rearrange("b (k p) -> p (b k)", p=P)).then_inc(
                    c_loaded, p.gives(c_loaded, 16))
                eng.dma_start(posi[:, :], a["positions"].rearrange("b (t p) -> p (b t)", p=P)).then_inc(
                    positions_loaded, p.gives(positions_loaded, 16))
                for i in range(2):
                    eng.dma_start(lbz[:, i], a["hg_lb_logits"][i].rearrange("(c p) -> p c", p=P)).then_inc(
                        lb_loaded, p.gives(lb_loaded, 16))
            eng.dma_start(bias_row[:, :], a["router_bias"].rearrange("(a e) -> a e", a=1)
                                 .partition_broadcast(P).rearrange("p a e -> p (a e)")).then_inc(
                bias_loaded, p.gives(bias_loaded, 16))
            eng.wait_ge(constants_ready, p.next(constants_ready))
            eng.wait_ge(c_loaded, p.next(c_loaded, 16))
            act(cact[:, :], cact[:, :], ACT.Silu).then_inc(cact_ready, p.gives(cact_ready))
            eng.wait_ge(lbdiff_ready, p.next(lbdiff_ready))
            act(lbw[:, 1], lbw[:, 1], ACT.Exp, scale=-1.0).then_inc(scalar_step, p.gives(scalar_step))
            eng.wait_ge(scalar_step, p.given(scalar_step))
            act(lbw[:, 1], lbw[:, 1], ACT.Ln, bias=consts[:, 1:2]).then_inc(lbln_ready, p.gives(lbln_ready))
            eng.wait_ge(angles_ready, p.next(angles_ready))
            act(sinT[:, :, :], angk[:, 0], ACT.Sin).then_inc(rope_ready, p.gives(rope_ready))
            act(cosT[:, :, :], angk[:, 1], ACT.Sin).then_inc(rope_ready, p.gives(rope_ready))
            eng.wait_ge(handed[1], p.next(handed[1]))

            def exp_and_ln():
                nc.scalar.preload_act_table_set("natural_log_exp_and_others")

            def feature_norm(ready=False):
                for c in range(NC):
                    i = c % 2
                    if ready:
                        if c == 2:
                            split_high()
                        eng.wait_ge(handed[i], p.next(handed[i]))
                    eng.wait_ge(sq_used[i], p.so_far(sq_used[i]))
                    p.mark(sq_used[i])
                    act(SC[:, i], X[:, c], ACT.Square).then_inc(sq_ready[i], p.gives(sq_ready[i]))
                eng.wait_ge(filled[2], p.next(filled[2]))
                act(SC[:, 2], bank(2), ACT.Ln, scale=1.0 / D, bias=consts[:, 0:1]).then_inc(
                    scalar_step, p.gives(scalar_step))
                eng.wait_ge(scalar_step, p.given(scalar_step))
                act(SC[:, 2], SC[:, 2], ACT.Exp, scale=-0.5).then_inc(handed[2], p.gives(handed[2]))

            def shift(at):
                for c in range(NC):
                    eng.wait_ge(scaled, p.next(scaled))
                    act(H[:, c], H[:, c], ACT.Identity, bias=mod[:, at + c:at + c + 1]).then_inc(
                        h_ready, p.gives(h_ready))

            def head_norm(x, tmp, n, d):
                act(tmp, x, ACT.Square).then_inc(squares_ready, p.gives(squares_ready))
                eng.wait_ge(sums_ready, p.next(sums_ready))
                act(rsq[:, 0:n], ssq[:, 0:n], ACT.Ln, scale=1.0 / d, bias=consts[:, 0:1]).then_inc(
                    scalar_step, p.gives(scalar_step))
                eng.wait_ge(scalar_step, p.given(scalar_step))
                act(rsq[:, 0:n], rsq[:, 0:n], ACT.Exp, scale=-0.5).then_inc(rms_ready, p.gives(rms_ready))

            def odd_tiles(dst, n=256):
                for t in (1, 3):
                    b = 2 + t // 2
                    eng.wait_ge(filled[b], p.next(filled[b]))
                    to = dst(t)
                    act(to, bank(b, n) if len(to.shape) == 2 else bank3(b, 4, HD), ACT.Copy).then_inc(
                        emptied[b], p.gives(emptied[b]))

            def y_copy(br):
                for t in range(NT):
                    b = 2 + t % 2
                    eng.wait_ge(filled[b], p.next(filled[b]))
                    act(Y[:, br, :, tt(t)], bank3(b, 4, P), ACT.Copy).then_inc(emptied[b], p.gives(emptied[b]))

            def exps(s, n):
                t, h, w = s.tile(n), s.head(n), len(s.blocks(n)) * P
                eng.wait_ge(rowmax_ready, p.next(rowmax_ready))
                for i, b in enumerate(s.banks(n)):
                    eng.wait_ge(filled[b], p.next(filled[b]))
                    if s.kind == "swa":
                        act(esink[:, t % 2, h:h + 1], row("swa_sinks", h, 1), ACT.Exp,
                                   bias=nmax[:, n % 2, 0:1]).then_inc(scalar_step, p.gives(scalar_step))
                    total = dl[:, n % 2, i:i + 1] if s.kind == "diff" else lsum[:, t % 2, h:h + 1]
                    act(probs[n % 2][i][:, 0:w], bank(b, w), ACT.Exp, bias=nmax[:, n % 2, i:i + 1],
                                  accum_out=total).then_inc(
                        (handed if s.kind == "diff" else emptied)[b], p.gives((handed if s.kind == "diff" else emptied)[b]))

            def sweep(s):
                for n in range(s.units + 1):
                    if n < s.units:
                        exps(s, n)
                    if n >= 1:
                        b, k = 2 + (n - 1) % 2, len(s.blocks(n - 1))
                        eng.wait_ge(filled[b], p.next(filled[b]))
                        act(probsT[(n - 1) % 2][:, 0:k], bank3(b, k, P), ACT.Copy).then_inc(
                            emptied[b], p.gives(emptied[b]))

            def do(step_, i):
                if step_ == "c":
                    odd_tiles(lambda t: DQK[:, t, i * 256:(i + 1) * 256] if i < 4
                              else DVt[:, t, (i - 4) * 256:(i - 3) * 256])
                elif step_ == "d":
                    odd_tiles(lambda t: swa_cols(t, i))
                elif step_ in ("hg_norm", "dif_post"):
                    for t in range(NT):
                        if step_ == "dif_post":
                            eng.wait_ge(handed[t % 2], p.next(handed[t % 2]))
                        head_norm(*norm_of(step_, t))
                elif step_ == "c_norm":
                    for t in range(2):
                        head_norm(*norm_of(step_, t))
                elif step_ in ("dif_norm", "swa_norm"):
                    if (step_, i) == ("dif_norm", 0):
                        for b in (2, 3):
                            eng.wait_ge(emptied[b], p.given(emptied[b]))
                    head_norm(*norm_of(step_, i))
                elif step_ in ("hg_y", "mla_y", "dif_y", "swa_y"):
                    y_copy(("hg_y", "mla_y", "dif_y", "swa_y").index(step_))
                elif step_ == "c_turn":
                    for t in range(NT):
                        b = 2 + t % 2
                        eng.wait_ge(filled[b], p.next(filled[b]))
                        act(cT[:, 0:3, tt(t)], bank3(b, 3, P), ACT.Copy).then_inc(
                            emptied[b], p.gives(emptied[b]))
                elif step_ == "up":
                    qk = heads(qk_tile[i % 2], 2 * HEADS)
                    eng.wait_ge(tile_used[i % 2], p.so_far(tile_used[i % 2]))
                    p.mark(tile_used[i % 2])
                    for f in range(2):
                        eng.wait_ge(filled[6 + f], p.next(filled[6 + f]))
                        kv = bank3(6 + f, 4, P)
                        act(qk[:, HEADS + 4 * f:HEADS + 4 * f + 4, 0:NOPE], kv[:, :, 0:NOPE], ACT.Copy).then_inc(
                            scalar_step, p.gives(scalar_step))
                        eng.wait_ge(scalar_step, p.given(scalar_step))
                        act(heads(mlaV[:, i, f * 256:(f + 1) * 256], 4), kv[:, :, NOPE:], ACT.Copy).then_inc(
                            emptied[6 + f], p.gives(emptied[6 + f]))
                    eng.wait_ge(handed[1], p.next(handed[1]))
                    head_norm(*norm_of("up", i))
                elif step_ == "turn":
                    for f in range(4):
                        b = 2 + f % 2
                        eng.wait_ge(filled[b], p.next(filled[b]))
                        dst = (mlaQ, mlaK)[f // 2][0:QKD, 4 * (f % 2):4 * (f % 2) + 4, tt(i)]
                        act(dst, bank3(b, 4, P)[0:QKD], ACT.Copy).then_inc(emptied[b], p.gives(emptied[b]))
                elif step_ == "dif_turn":
                    for t in range(NT):
                        for f in range(2):
                            eng.wait_ge(filled[2 + f], p.next(filled[2 + f]))
                            act((difQ, difK)[f][:, :, tt(t)], bank3(2 + f, 4, P), ACT.Copy).then_inc(
                                emptied[2 + f], p.gives(emptied[2 + f]))
                elif step_ == "swa_turn":
                    for t in range(NT):
                        eng.wait_ge(filled[2], p.next(filled[2]))
                        act(swaQ[:, :, tt(t)], bank3(2, 4, P), ACT.Copy).then_inc(
                            emptied[2], p.gives(emptied[2]))
                        eng.wait_ge(filled[3], p.next(filled[3]))
                        act(swaK[:, tt(t)], bank(3, P), ACT.Copy).then_inc(emptied[3], p.gives(emptied[3]))
                elif step_ == "sweep":
                    sweep(i)

            with p.loop("layer", DEPTH):
                exp_and_ln()
                eng.wait_ge(handed[5], p.so_far(handed[5]))
                feature_norm()
                eng.wait_ge(lamsum_ready, p.next(lamsum_ready))
                act(lams[:, 2:4], lams[:, 0:2], ACT.Exp).then_inc(lamexp_ready, p.gives(lamexp_ready))
                shift(0)
                L, fb, kf = flat(hgO), flat(hgB), flat(hgK)
                eng.wait_ge(f_ready, p.next(f_ready))
                act(L, fb, ACT.Abs).then_inc(scalar_step, p.gives(scalar_step))
                eng.wait_ge(scalar_step, p.given(scalar_step))
                act(L, L, ACT.Exp, scale=-1.0).then_inc(scalar_step, p.gives(scalar_step))
                eng.wait_ge(scalar_step, p.given(scalar_step))
                act(L, L, ACT.Ln, bias=consts[:, 1:2]).then_inc(ln_ready, p.gives(ln_ready))
                eng.wait_ge(logk_ready, p.next(logk_ready))
                act(kf, kf, ACT.Exp).then_inc(k_ready, p.gives(k_ready))
                eng.wait_ge(logt_ready, p.next(logt_ready))
                act(L, L, ACT.Abs).then_inc(scalar_step, p.gives(scalar_step))
                eng.wait_ge(scalar_step, p.given(scalar_step))
                act(L, L, ACT.Exp, scale=-1.0).then_inc(scalar_step, p.gives(scalar_step))
                eng.wait_ge(scalar_step, p.given(scalar_step))
                act(L, L, ACT.Ln, bias=consts[:, 1:2]).then_inc(logaddexp_ready, p.gives(logaddexp_ready))
                for c in range(4):
                    eng.wait_ge(filled[2 + c % 2], p.next(filled[2 + c % 2]))
                    act(hgQ[:, c], bank(2 + c % 2), ACT.Silu).then_inc(
                        emptied[2 + c % 2], p.gives(emptied[2 + c % 2]))
                for u in range(2):
                    odd_tiles(lambda t: TM[:, t, u * 256:(u + 1) * 256])
                for u in range(2):
                    for t in range(NT):
                        b = 2 + t % 2
                        eng.wait_ge(filled[b], p.next(filled[b]))
                        act(TM[:, t, 512 + u * 256:512 + (u + 1) * 256], bank(b, 256), ACT.Silu).then_inc(
                            emptied[b], p.gives(emptied[b]))
                for at, n in ((0, 256), (256, KVR + ROPE)):
                    odd_tiles(lambda t: CM[:, t, at:at + n], n)
                exp_and_ln()
                eng.wait_ge(b_ready, p.next(b_ready))
                eng.wait_ge(emptied[2], p.given(emptied[2]))
                for pr in range(4):
                    for j in range(9):
                        i = (9 * pr + j) % 2
                        if j < 8:
                            eng.wait_ge(d_ready[i], p.next(d_ready[i]))
                            if j > 0:
                                act(hgE[i], hgE[i], ACT.Abs).then_inc(scalar_step, p.gives(scalar_step))
                                eng.wait_ge(scalar_step, p.given(scalar_step))
                            act(hgE[i], hgE[i], ACT.Exp, scale=-1.0).then_inc(e_ready[i], p.gives(e_ready[i]))
                            p.mark(ks_ready[i])
                            if j:
                                p.mark(qs_ready[i])
                        else:
                            eng.wait_ge(ks_ready[i], p.so_far(ks_ready[i]))
                            eng.wait_ge(qs_ready[i], p.so_far(qs_ready[i]))
                            act(hgE[i], hgB[:, pr], ACT.Exp).then_inc(e_ready[i], p.gives(e_ready[i]))
                        if j == 3:
                            ends = heads(hgB[:, pr], NT)[:, :, P - 1]
                            act(edec[:, :], ends, ACT.Exp).then_inc(edec_ready, p.gives(edec_ready))
                            eng.wait_ge(filled[2], p.next(filled[2]))
                            act(KdT[pr % 2], bank3(2, 4, P), ACT.Copy).then_inc(emptied[2], p.gives(emptied[2]))
                    if pr:
                        eng.wait_ge(filled[6 + (pr - 1) % 2], p.next(filled[6 + (pr - 1) % 2]))
                        act(hgO[:, :, tt(pr - 1)], bank3(6 + (pr - 1) % 2, 4, P), ACT.Copy).then_inc(
                            emptied[6 + (pr - 1) % 2], p.gives(emptied[6 + (pr - 1) % 2]))
                eng.wait_ge(filled[7], p.next(filled[7]))
                act(hgO[:, :, tt(3)], bank3(7, 4, P), ACT.Copy).then_inc(emptied[7], p.gives(emptied[7]))
                eng.wait_ge(emptied[7], p.given(emptied[7]))
                for st, i in SCHEDULE:
                    do(st, i)
                ring_at.next(FRONT)
                acts_high(Hc, act_hi)
                with p.loop("merge", 2):
                    split_high()
                    split_high()
                    for br in range(NB):
                        for j in range(4):
                            m = j % 2
                            eng.wait_ge(filled[2 + m], p.next(filled[2 + m]))
                            act(SC[:, j], bank(2 + m), ACT.Sigmoid).then_inc(handed[2 + m], p.gives(handed[2 + m]))
                            if br:
                                p.mark(handed[m])
                            if j == 1:
                                ring_at.next(3)
                            if br < NB - 1 and m:
                                split_high()
                split_high()
                split_high()
                for m in range(2):
                    p.mark(added[m], 12)
                    eng.wait_ge(added[m], p.so_far(added[m]))
                acts_high(Mc, act_hi)
                exp_and_ln()
                split_high()
                feature_norm(ready=True)
                shift(3 * NC)
                eng.wait_ge(h_ready, p.given(h_ready))
                eng.wait_ge(filled[6], p.next(filled[6]))
                act(scores_T, ps[0:NE, 6], ACT.Sigmoid).then_inc(emptied[6], p.gives(emptied[6]))
                acts_high(Hc, act_hi)
                eng.wait_ge(filled[7], p.next(filled[7]))
                act(rt[:, 0], bank(7, NT * NE), ACT.Copy).then_inc(handed[7], p.gives(handed[7]))
                with p.loop("moe", NG):
                    split_high()
                    split_high()
                    for e in range(4):
                        for m in range(2):
                            eng.wait_ge(filled[2 + m], p.next(filled[2 + m]))
                            act(SC[:, 2 * (e % 2) + m], bank(2 + m), ACT.Silu).then_inc(
                                handed[2 + m], p.gives(handed[2 + m]))
                        split_high()
                        p.mark(filled[6 + e % 2])
                        for m in range(2):
                            acts_high([hid[2 * e + m]], [M_r[2 * e + m]], handed[m])
                        split_high()
                    split_high()
                    split_high()
                    p.mark(handed[5])
                ring_at.wrap()
            for t in range(NT):
                eng.wait_ge(handed[1], p.next(handed[1]))
                eng.dma_start(out.rearrange("b (t p) d -> p (b t) d", p=P)[:, t], xin[:, t]).then_inc(
                    out_stored, p.gives(out_stored, 16))
            eng.wait_ge(out_stored, p.given(out_stored))

        @block.vector
        def _(eng):
            p = Program(eng, "dve", rate)
            ring_at = Ring(p)

            def acts_low(src, dst, hi):
                for x, y, h in zip(src, dst, hi):
                    eng.wait_ge(act_high, p.next(act_high))
                    v.tensor_tensor(y, x, h.bitcast(F32), ALU.subtract).then_inc(act_ready, p.gives(act_ready))

            def ada(u, s=0):
                js = [ring_at.next(), ring_at.next()]
                w = [ring[:, j].rearrange("p (k n) -> p k n", k=NC) for j in js]
                part = [acc[s][:, (u + i) * 256:(u + i + 1) * 256] for i in range(2)]
                for j in js:
                    eng.wait_ge(slot_loaded[j], p.so_far(slot_loaded[j]))
                for k in range(NC):
                    for i in range(2):
                        if k:
                            eng.wait_ge(vector_step, p.given(vector_step, less=1 if k < NC - 1 else 1 - i))
                            ins = v.scalar_tensor_tensor(out=part[i], in0=w[i][:, k], scalar=cact[:, k:k + 1],
                                                         in1=part[i], op0=ALU.mult, op1=ALU.add)
                        else:
                            ins = v.tensor_scalar(part[i], w[i][:, 0], cact[:, 0:1], None, ALU.mult)
                        if k < NC - 1:
                            ins.then_inc(vector_step, p.gives(vector_step))
                        else:
                            ins.then_inc(slot_used[js[i]], p.gives(slot_used[js[i]]))
                if u == 2:
                    for j in js:
                        eng.wait_ge(slot_used[j], p.so_far(slot_used[j]))
                    v.tensor_copy(ssq[:, s:s + 1], part[0][:, 0:1]).then_inc(summed, p.gives(summed))

            def section(b, s):
                eng.wait_ge(filled[b], p.next(filled[b]))
                v.tensor_tensor(mod[:, bass.ds(s, NC)], bank(b, NC), colT[:, bass.ds(s, NC)], ALU.add).then_inc(
                    emptied[b], p.gives(emptied[b]))

            for b in (0, 1, 4, 5):
                eng.sem_inc(emptied[b], 1)
                eng.sem_inc(handed[b], 1)
            for sem in (params_used, *weights_used):
                eng.sem_inc(sem, 1)

            def alone():
                eng.sem_inc(waited["dve"], 1)

            v = nc.vector




            eng.wait_ge(lb_loaded, p.next(lb_loaded, 32))
            eng.wait_ge(constants_ready, p.next(constants_ready))
            v.tensor_tensor(lbw[:, 0], lbz[:, 0], lbz[:, 1], ALU.subtract).then_inc(
                vector_step, p.gives(vector_step))
            eng.wait_ge(vector_step, p.given(vector_step))
            v.scalar_tensor_tensor(out=lbw[:, 1], in0=lbw[:, 0], scalar=-1.0, in1=lbw[:, 0],
                                          op0=ALU.mult, op1=ALU.max).then_inc(
                lbdiff_ready, p.gives(lbdiff_ready))
            eng.wait_ge(positions_loaded, p.next(positions_loaded, 16))
            v.tensor_copy(posf[:, :], posi[:, :]).then_inc(vector_step, p.gives(vector_step))
            eng.wait_ge(vector_step, p.given(vector_step))
            for t in range(NT):
                v.tensor_scalar(ang[:, t], ifr[:, :], posf[:, t:t + 1], None, ALU.mult).then_inc(
                    vector_step, p.gives(vector_step))
                eng.wait_ge(vector_step, p.given(vector_step))
            c1 = 6.28125
            c2 = float((np.array(2 * math.pi - c1, np.float32).view(np.uint32) & np.uint32(0xFFFFF000)).view(np.float32))
            c3 = 2 * math.pi - c1 - c2
            big = 1.5 * 2 ** 23
            for i in range(2):
                v.tensor_scalar(angk[:, i], ang[:, :, :], 1.0 / (2 * math.pi), 0.25 * i, ALU.mult, ALU.add).then_inc(
                    vector_step, p.gives(vector_step))
                eng.wait_ge(vector_step, p.given(vector_step))
                v.tensor_scalar(angk[:, i], angk[:, i], big, None, ALU.add).then_inc(
                    vector_step, p.gives(vector_step))
                eng.wait_ge(vector_step, p.given(vector_step))
                v.tensor_scalar(angk[:, i], angk[:, i], big, None, ALU.subtract).then_inc(
                    vector_step, p.gives(vector_step))
                eng.wait_ge(vector_step, p.given(vector_step))
            r = [sb(f"rope_r{i}", NT, HALF) for i in range(2)]
            for i in range(2):
                a0 = ang[:, :, :]
                for k, c in enumerate((c1, c2, c3)):
                    v.scalar_tensor_tensor(out=r[i][:, :, :], in0=angk[:, i], scalar=-c,
                                                in1=a0 if k == 0 else r[i][:, :, :], op0=ALU.mult, op1=ALU.add).then_inc(
                        vector_step, p.gives(vector_step))
                    eng.wait_ge(vector_step, p.given(vector_step))
                v.tensor_scalar(r[i][:, :, :], r[i][:, :, :], 0.5 * math.pi * i, 3.1415925, ALU.add, ALU.min).then_inc(
                    vector_step, p.gives(vector_step))
                eng.wait_ge(vector_step, p.given(vector_step))
            v.tensor_scalar(angk[:, 0], r[0][:, :, :], -3.1415925, None, ALU.max).then_inc(
                vector_step, p.gives(vector_step))
            eng.wait_ge(vector_step, p.given(vector_step))
            v.tensor_scalar(angk[:, 1], r[1][:, :, :], -3.1415925, None, ALU.max).then_inc(
                angles_ready, p.gives(angles_ready))
            eng.wait_ge(lbln_ready, p.next(lbln_ready))
            for i, sign in ((0, 1.0), (1, -1.0)):
                dst = lbt[:, 1, i * NT:(i + 1) * NT]
                v.tensor_scalar(dst, lbw[:, 0], sign, 0.0, ALU.mult, ALU.max).then_inc(
                    vector_step, p.gives(vector_step))
                eng.wait_ge(vector_step, p.given(vector_step))
                v.scalar_tensor_tensor(out=dst, in0=dst, scalar=-1.0, in1=lbw[:, 1],
                                            op0=ALU.mult, op1=ALU.subtract).then_inc(
                    vector_step, p.gives(vector_step))
                eng.wait_ge(vector_step, p.given(vector_step))
            for c in range(NC):
                eng.wait_ge(filled[c % 2], p.next(filled[c % 2]))
                v.tensor_copy(X[:, c], bank(c % 2)).then_inc(
                    (handed if c == NC - 1 else emptied)[c % 2], p.gives((handed if c == NC - 1 else emptied)[c % 2]))
            eng.wait_ge(bias_loaded, p.next(bias_loaded, 16))

            def feature_norm(scale_at, norm_at):
                v.scalar_tensor_tensor(out=gain[:, :], in0=mod[:, scale_at:scale_at + NC], scalar=1.0,
                                            in1=colT[:, norm_at:norm_at + NC], op0=ALU.add, op1=ALU.mult).then_inc(
                    vector_step, p.gives(vector_step))
                eng.wait_ge(vector_step, p.given(vector_step))
                for c in range(NC):
                    v.scalar_tensor_tensor(out=H[:, c], in0=X[:, c], scalar=gain[:, c:c + 1], in1=SC[:, 2],
                                           op0=ALU.mult, op1=ALU.mult).then_inc(scaled, p.gives(scaled))

            def head_norm(x, tmp, n, d):
                x = x if len(x.shape) == 3 else heads(x, n)
                eng.wait_ge(squares_ready, p.next(squares_ready))
                tmp = tmp if len(tmp.shape) == 3 else heads(tmp, n)
                v.tensor_reduce(ssq[:, 0:n], tmp, AX, ALU.add).then_inc(sums_ready, p.gives(sums_ready))
                eng.wait_ge(rms_ready, p.next(rms_ready))
                v.tensor_tensor(x, x, spread(rsq[:, 0:n], d), ALU.mult).then_inc(normed, p.gives(normed))

            def even_tiles(dst, n=256):
                for t in (0, 2):
                    eng.wait_ge(filled[t // 2], p.next(filled[t // 2]))
                    to = dst(t)
                    v.tensor_copy(to, bank(t // 2, n) if len(to.shape) == 2 else bank3(t // 2, 4, HD)).then_inc(
                        emptied[t // 2], p.gives(emptied[t // 2]))

            def rowmax(s, n):
                t, h, w = s.tile(n), s.head(n), len(s.blocks(n)) * P
                bs = s.banks(n)
                for i, b in enumerate(bs):
                    eng.wait_ge(filled[b], p.next(filled[b]))
                    if s.kind == "swa":
                        m = swmask[:, 2 * P - w:2 * P]
                        v.tensor_tensor(bank(b, w), bank(b, w), m, ALU.add).then_inc(
                            vector_step, p.gives(vector_step))
                        eng.wait_ge(vector_step, p.given(vector_step))
                    else:
                        v.tensor_tensor(ps[:, b, tt(t)], ps[:, b, tt(t)], cmask[:, :], ALU.add).then_inc(
                            vector_step, p.gives(vector_step))
                        eng.wait_ge(vector_step, p.given(vector_step))
                    red = v.tensor_reduce(nmax[:, n % 2, i:i + 1], bank(b, w), AX, ALU.max, negate=True)
                    if s.kind == "swa":
                        red.then_inc(vector_step, p.gives(vector_step))
                        eng.wait_ge(vector_step, p.given(vector_step))
                        red = v.tensor_tensor(nmax[:, n % 2, 0:1], nmax[:, n % 2, 0:1], nsink[:, h:h + 1], ALU.min)
                    red.then_inc(
                        (rowmax_ready if i == len(bs) - 1 else vector_step), p.gives((rowmax_ready if i == len(bs) - 1 else vector_step)))

            def combine(n):
                w = len(DIFF.blocks(n)) * P
                eng.wait_ge(handed[6], p.next(handed[6]))
                eng.wait_ge(handed[7], p.next(handed[7]))
                p1, p2 = (probs[n % 2][i][:, 0:w] for i in range(2))
                if n:
                    eng.wait_ge(probs_ready, p.given(probs_ready))
                v.reciprocal(dr[:, :], dl[:, n % 2]).then_inc(vector_step, p.gives(vector_step))
                eng.wait_ge(vector_step, p.given(vector_step))
                v.tensor_tensor(dr[:, 1:2], dr[:, 1:2], neglam[:, :], ALU.mult).then_inc(
                    vector_step, p.gives(vector_step))
                eng.wait_ge(vector_step, p.given(vector_step))
                v.tensor_scalar(p1, p1, dr[:, 0:1], None, ALU.mult).then_inc(vector_step, p.gives(vector_step))
                eng.wait_ge(vector_step, p.given(vector_step))
                v.scalar_tensor_tensor(out=p1, in0=p2, scalar=dr[:, 1:2], in1=p1,
                                              op0=ALU.mult, op1=ALU.add).then_inc(
                    probs_ready, p.gives(probs_ready))

            def tile_out(s, t):
                b = t % 2
                eng.wait_ge(filled[b], p.next(filled[b]))
                dst = y_tok[s.kind][:, t]
                if s.kind == "diff":
                    v.tensor_copy(dst, bank(b)).then_inc(handed[b], p.gives(handed[b]))
                    return
                if s.kind == "swa":
                    v.tensor_tensor(lrec[:, :], lsum[:, t % 2], esink[:, t % 2], ALU.add).then_inc(
                        vector_step, p.gives(vector_step))
                    eng.wait_ge(vector_step, p.given(vector_step))
                    v.reciprocal(lrec[:, :], lrec[:, :]).then_inc(vector_step, p.gives(vector_step))
                    eng.wait_ge(vector_step, p.given(vector_step))
                else:
                    v.reciprocal(lrec[:, :], lsum[:, t % 2]).then_inc(vector_step, p.gives(vector_step))
                    eng.wait_ge(vector_step, p.given(vector_step))
                v.tensor_tensor(heads(dst, HEADS), bank3(b, HEADS, HD), spread(lrec[:, :], HD), ALU.mult).then_inc(
                    emptied[b], p.gives(emptied[b]))

            def sweep(s):
                for n in range(s.units + 2):
                    if n < s.units:
                        rowmax(s, n)
                    if s.kind == "diff" and 1 <= n <= s.units:
                        combine(n - 1)
                    if n >= 2 and s.last(n - 2):
                        tile_out(s, s.tile(n - 2))

            def do(step_, i):
                if step_ == "c":
                    even_tiles(lambda t: DQK[:, t, i * 256:(i + 1) * 256] if i < 4
                               else DVt[:, t, (i - 4) * 256:(i - 3) * 256])
                elif step_ == "d":
                    even_tiles(lambda t: swa_cols(t, i))
                elif step_ in ("hg_norm", "dif_post"):
                    for t in range(NT):
                        head_norm(*norm_of(step_, t))
                elif step_ == "c_norm":
                    for t in range(2):
                        head_norm(*norm_of(step_, t))
                elif step_ in ("dif_norm", "swa_norm"):
                    head_norm(*norm_of(step_, i))
                elif step_ == "up":
                    qk = heads(qk_tile[i % 2], 2 * HEADS)
                    eng.wait_ge(tile_used[i % 2], p.so_far(tile_used[i % 2]))
                    p.mark(tile_used[i % 2])
                    p.mark(filled[6])
                    p.mark(filled[7])
                    v.tensor_copy(qk[:, HEADS:, NOPE:], repeat(CM[:, i, QR + KVR:], HEADS)).then_inc(
                        vector_step, p.gives(vector_step))
                    for f in range(2):
                        eng.wait_ge(filled[f], p.next(filled[f]))
                        v.tensor_copy(qk_tile[i % 2][:, f * 384:(f + 1) * 384], bank(f, 384)).then_inc(
                            (emptied, handed)[f][f], p.gives((emptied, handed)[f][f]))
                    head_norm(*norm_of("up", i))
                elif step_ == "sweep":
                    sweep(i)

            with p.loop("layer", DEPTH) as l:
                eng.wait_ge(filled[0], p.next(filled[0]))
                v.tensor_copy(colT[:, :], bank(0, NCOLP)).then_inc(emptied[0], p.gives(emptied[0]))
                eng.wait_ge(emptied[0], p.given(emptied[0]))
                eng.wait_ge(rows_loaded, p.next(rows_loaded, 16 * len(ROWS)))
                v.tensor_copy(lic[:, :], pick(litab[:, :, :], l)).then_inc(vector_step, p.gives(vector_step))
                eng.wait_ge(vector_step, p.given(vector_step))
                v.tensor_copy(lbc[:, :], pick(lbt[:, :, :], l)).then_inc(vector_step, p.gives(vector_step))
                eng.wait_ge(vector_step, p.given(vector_step))
                for name, n, s in (("mla_qk_norm", QKD, QKD ** -0.5), ("diff_qk_norm", HD, HD ** -0.5),
                                   ("swa_qk_norm", HD, HD ** -0.5)):
                    v.tensor_scalar(row(name, 0, n), row(name, 0, n), s, None, ALU.mult).then_inc(
                        vector_step, p.gives(vector_step))
                    eng.wait_ge(vector_step, p.given(vector_step))
                v.tensor_scalar(nsink[:, :], row("swa_sinks"), -1.0, None, ALU.mult).then_inc(
                    vector_step, p.gives(vector_step))
                eng.wait_ge(vector_step, p.given(vector_step))
                lp = heads(row("diff_lam"), 4)
                for i in range(2):
                    v.tensor_tensor(lamp[:, i], lp[:, 2 * i], lp[:, 2 * i + 1], ALU.mult).then_inc(
                        vector_step, p.gives(vector_step))
                    eng.wait_ge(vector_step, p.given(vector_step))
                v.tensor_reduce(lams[:, 0:2], lamp[:, :, :], AX, ALU.add).then_inc(
                    lamsum_ready, p.gives(lamsum_ready))
                v.tensor_scalar(row("diff_onorm"), row("diff_onorm"), lic[:, 1:2], None, ALU.mult).then_inc(
                    rows_ready, p.gives(rows_ready))
                for s in range(2):
                    ada(0, s)
                    ada(2, s)
                eng.wait_ge(lamexp_ready, p.next(lamexp_ready))
                v.tensor_tensor(neglam[:, :], lams[:, 3:4], lams[:, 2:3], ALU.subtract).then_inc(
                    vector_step, p.gives(vector_step))
                eng.wait_ge(vector_step, p.given(vector_step))
                v.tensor_tensor(neglam[:, :], neglam[:, :], lic[:, 0:1], ALU.subtract).then_inc(
                    vector_step, p.gives(vector_step))
                eng.wait_ge(vector_step, p.given(vector_step))
                alone()
                for s in range(2):
                    section(1, s * NC)
                ring_at.next(FRONT - 2 * 4)
                eng.wait_ge(emptied[1], p.given(emptied[1]))
                eng.wait_ge(handed[2], p.next(handed[2]))
                feature_norm(NC, 48)

                fb = hgB
                for c in range(4):
                    eng.wait_ge(filled[c % 2], p.next(filled[c % 2]))
                    v.tensor_copy(fb[:, c], bank(c % 2)).then_inc(emptied[c % 2], p.gives(emptied[c % 2]))
                eng.wait_ge(emptied[0], p.given(emptied[0]))
                eng.wait_ge(emptied[1], p.given(emptied[1]))
                v.tensor_scalar(flat(hgK), flat(fb), -1.0, 0.0, ALU.mult, ALU.min).then_inc(
                    f_ready, p.gives(f_ready))
                eng.wait_ge(ln_ready, p.next(ln_ready))
                for c in range(4):
                    v.scalar_tensor_tensor(out=hgK[:, c], in0=hgK[:, c], scalar=lbc[:, NT + c:NT + c + 1],
                                                  in1=hgO[:, c], op0=ALU.add, op1=ALU.subtract).then_inc(
                        (logk_ready if c == 3 else vector_step), p.gives((logk_ready if c == 3 else vector_step)))
                for c in range(4):
                    v.tensor_scalar(fb[:, c], fb[:, c], 0.0, lbc[:, NT + c:NT + c + 1], ALU.min, ALU.add).then_inc(
                        vector_step, p.gives(vector_step))
                eng.wait_ge(vector_step, p.given(vector_step))
                v.tensor_tensor(flat(fb), flat(fb), flat(hgO), ALU.subtract).then_inc(
                    vector_step, p.gives(vector_step))
                eng.wait_ge(vector_step, p.given(vector_step))
                for c in range(4):
                    v.tensor_scalar(hgO[:, c], fb[:, c], -1.0, lbc[:, c:c + 1], ALU.mult, ALU.add).then_inc(
                        (logt_ready if c == 3 else vector_step), p.gives((logt_ready if c == 3 else vector_step)))
                v.memset(flat(DQK[:, 0:2]), 0.0).then_inc(vector_step, p.gives(vector_step))
                v.memset(DQK[:, 3], 0.0).then_inc(vector_step, p.gives(vector_step))
                eng.wait_ge(logaddexp_ready, p.next(logaddexp_ready))
                for c in range(4):
                    v.scalar_tensor_tensor(out=fb[:, c], in0=fb[:, c], scalar=lbc[:, c:c + 1],
                                                  in1=hgO[:, c], op0=ALU.max, op1=ALU.add).then_inc(
                        vector_step, p.gives(vector_step))
                eng.wait_ge(vector_step, p.given(vector_step))
                for c in range(4):
                    for t in range(NT):
                        v.tensor_tensor_scan(out=fb[:, c, tt(t)], data0=ones[:, :], data1=fb[:, c, tt(t)],
                                                    initial=0.0, op0=ALU.mult, op1=ALU.add).then_inc(
                            (b_ready if (c, t) == (3, 3) else vector_step), p.gives((b_ready if (c, t) == (3, 3) else vector_step)))
                eng.wait_ge(b_ready, p.given(b_ready))
                for u in range(2):
                    even_tiles(lambda t: TM[:, t, u * 256:(u + 1) * 256])
                for at, n in ((0, 256), (256, KVR + ROPE)):
                    even_tiles(lambda t: CM[:, t, at:at + n], n)
                eng.wait_ge(k_ready, p.next(k_ready))

                def decay(g):
                    pr, j = divmod(g, 9)
                    i = g % 2
                    if j == 8 or g == 36:
                        return
                    if g >= 2:
                        eng.wait_ge((qin_ready if (g - 2) % 9 == 8 else qs_ready[i]), p.so_far((qin_ready if (g - 2) % 9 == 8 else qs_ready[i])))
                        eng.wait_ge(ks_ready[i], p.given(ks_ready[i]))
                    size = P if j == 0 else 1 << j
                    blocks = hgB[:, pr].rearrange("p (n s) -> p n s", s=size)
                    mid = size - 1 if j == 0 else size // 2 - 1
                    ref = blocks[:, :, mid:mid + 1].to_broadcast([P, S // size, size])
                    v.tensor_tensor(hgE[i].rearrange("p (n s) -> p n s", s=size), blocks, ref,
                                           ALU.subtract).then_inc(d_ready[i], p.gives(d_ready[i]))

                def keep(pr, lv):
                    if lv == 0:
                        eng.wait_ge(attn_used[pr % 2], p.so_far(attn_used[pr % 2]))
                        alone()
                        p.mark(attn_used[pr % 2])
                    mask = (ident[:, :] if lv == 0 else lmask[:, lv - 1]).bitcast(I32)
                    for hp in range(2):
                        b = (lv % 2) * 4 + hp
                        eng.wait_ge(filled[b], p.next(filled[b]))
                        alone()
                        if lv:
                            eng.wait_ge(emptied[4 - lv % 2 * 4 + hp], p.given(emptied[4 - lv % 2 * 4 + hp]))
                            alone()
                        v.copy_predicated(attnT[pr % 2][hp], repeat(mask, NT), bank3(b, NT, P)).then_inc(
                            emptied[b], p.gives(emptied[b]))

                decay(0)
                for pr in range(4):
                    for j in range(9):
                        g = 9 * pr + j
                        i = g % 2
                        if j < 8:
                            decay(g + 1)
                            eng.wait_ge(e_ready[i], p.next(e_ready[i]))
                            eng.wait_ge(qk_used[i], p.so_far(qk_used[i]))
                            p.mark(qk_used[i])
                            v.tensor_tensor(hgKs[i], hgK[:, pr], hgE[i], ALU.mult).then_inc(
                                ks_ready[i], p.gives(ks_ready[i]))
                            if j:
                                p.mark(qs_ready[i])
                        else:
                            p.mark(e_ready[i])
                            p.mark(qin_ready)
                            decay(g + 1)
                        if j:
                            keep(pr, j - 1)
                        if j == 5:
                            eng.wait_ge(edec_ready, p.next(edec_ready))
                            eng.wait_ge(filled[0], p.next(filled[0]))
                            for c in range(3):
                                for h in range(2):
                                    r = slice(h * HD, (h + 1) * HD)
                                    new, add = state[pr % 2][r, c + 1, r], ps[r, 0, c * P + h * HD:c * P + (h + 1) * HD]
                                    if c == 0:
                                        ins = v.tensor_copy(new, add)
                                    else:
                                        ins = v.scalar_tensor_tensor(out=new, in0=state[pr % 2][r, c, r],
                                                                     scalar=edec[r, c:c + 1], in1=add,
                                                                     op0=ALU.mult, op1=ALU.add)
                                    if (c, h) == (2, 1):
                                        ins.then_inc(emptied[0], p.gives(emptied[0]))
                                    else:
                                        ins.then_inc(vector_step, p.gives(vector_step))
                                if c < 2:
                                    eng.wait_ge(vector_step, p.given(vector_step))
                    p.mark(filled[6 + pr % 2])
                for st, i in SCHEDULE:
                    do(st, i)

                acts_low(Hc, H_lo, act_hi)
                eng.wait_ge(act_ready, p.given(act_ready))
                v.memset(lams[:, 0:1], 0.0).then_inc(params_used, p.gives(params_used))
                with p.loop("merge", 2) as g:
                    for br in range(NB):
                        ring_at.next(3)
                        ada(br % 2 * 2)
                        for j in range(4):
                            i = j % 2
                            eng.wait_ge(handed[2 + i], p.next(handed[2 + i]))
                            eng.wait_ge(filled[i], p.next(filled[i]))
                            if br == 0:
                                v.tensor_tensor(pick(merged, g * 4 + j), bank(i), SC[:, j], ALU.mult).then_inc(
                                    emptied[i], p.gives(emptied[i]))
                            else:
                                eng.wait_ge(added[i], p.so_far(added[i]))
                                p.mark(added[i])
                                v.tensor_tensor(SC[:, 4 + i], bank(i), SC[:, j], ALU.mult).then_inc(
                                    handed[i], p.gives(handed[i]))
                        if br % 2:
                            section(4, g * (2 * NC) + (2 + br // 2) * NC)
                ring_at.next(4)
                acts_low(Mc, M_r, act_hi)
                for c in range(NC):
                    i = c % 2
                    eng.wait_ge(filled[i], p.next(filled[i]))
                    v.scalar_tensor_tensor(out=X[:, c], in0=bank(i), scalar=mod[:, 2 * NC + c:2 * NC + c + 1],
                                                     in1=X[:, c], op0=ALU.mult, op1=ALU.add).then_inc(
                        handed[i], p.gives(handed[i]))
                eng.wait_ge(handed[2], p.next(handed[2]))
                eng.wait_ge(handed[1], p.given(handed[1]))
                eng.wait_ge(emptied[4], p.given(emptied[4]))
                feature_norm(4 * NC, 56)
                eng.wait_ge(filled[6], p.next(filled[6]))
                acts_low(Hc, H_lo, act_hi)
                p.mark(filled[7])
                eng.wait_ge(handed[7], p.next(handed[7]))
                r16 = [heads(rt[:, k], NT) for k in range(6)]
                w16 = repeat(wexp[:, :], NT)
                v.tensor_tensor(r16[1], r16[0], repeat(bias_row[:, :], NT), ALU.add).then_inc(
                    vector_step, p.gives(vector_step))
                eng.wait_ge(vector_step, p.given(vector_step))
                q = rt[:, 1].rearrange("p (g e) -> p g e", e=PER)
                for k in range(2):
                    v.tensor_tensor(rg[:, k], q[:, :, 2 * k], q[:, :, 2 * k + 1], ALU.max).then_inc(
                        vector_step, p.gives(vector_step))
                    eng.wait_ge(vector_step, p.given(vector_step))
                    v.tensor_tensor(rg[:, 2 + k], q[:, :, 2 * k], q[:, :, 2 * k + 1], ALU.min).then_inc(
                        vector_step, p.gives(vector_step))
                    eng.wait_ge(vector_step, p.given(vector_step))
                v.tensor_tensor(rg[:, 4], rg[:, 0], rg[:, 1], ALU.max).then_inc(
                    vector_step, p.gives(vector_step))
                eng.wait_ge(vector_step, p.given(vector_step))
                v.tensor_tensor(rg[:, 5], rg[:, 0], rg[:, 1], ALU.min).then_inc(
                    vector_step, p.gives(vector_step))
                eng.wait_ge(vector_step, p.given(vector_step))
                v.tensor_tensor(rg[:, 2], rg[:, 2], rg[:, 3], ALU.max).then_inc(
                    vector_step, p.gives(vector_step))
                eng.wait_ge(vector_step, p.given(vector_step))
                v.tensor_tensor(rg[:, 5], rg[:, 5], rg[:, 2], ALU.max).then_inc(
                    vector_step, p.gives(vector_step))
                eng.wait_ge(vector_step, p.given(vector_step))
                v.tensor_tensor(rg[:, 4], rg[:, 4], rg[:, 5], ALU.add).then_inc(
                    vector_step, p.gives(vector_step))
                eng.wait_ge(vector_step, p.given(vector_step))

                def first_max(x, w, n, top, hit, dst):
                    v.tensor_reduce(top, x, AX, ALU.max).then_inc(vector_step, p.gives(vector_step))
                    eng.wait_ge(vector_step, p.given(vector_step))
                    v.tensor_tensor(hit, x, spread(top, n), ALU.is_equal).then_inc(
                        vector_step, p.gives(vector_step))
                    eng.wait_ge(vector_step, p.given(vector_step))
                    v.tensor_tensor(hit, hit, w, ALU.mult).then_inc(vector_step, p.gives(vector_step))
                    eng.wait_ge(vector_step, p.given(vector_step))
                    v.tensor_reduce(top, hit, AX, ALU.max).then_inc(vector_step, p.gives(vector_step))
                    eng.wait_ge(vector_step, p.given(vector_step))
                    v.tensor_tensor(dst, hit, spread(top, n), ALU.is_equal).then_inc(
                        vector_step, p.gives(vector_step))
                    eng.wait_ge(vector_step, p.given(vector_step))

                g3 = [heads(rg[:, k], NT) for k in range(6)]
                first_max(g3[4], repeat(wgrp[:, :], NT), NG, ssq[:, 0:NT], g3[0], g3[1])
                v.tensor_scalar(rg[:, 1], rg[:, 1], -NEG, NEG, ALU.mult, ALU.add).then_inc(
                    vector_step, p.gives(vector_step))
                eng.wait_ge(vector_step, p.given(vector_step))
                v.tensor_tensor(q, q, rg[:, 1].unsqueeze(2).to_broadcast([P, NT * NG, PER]), ALU.add).then_inc(
                    vector_step, p.gives(vector_step))
                eng.wait_ge(vector_step, p.given(vector_step))
                first_max(r16[1], w16, NE, ssq[:, 0:NT], r16[2], r16[3])
                v.scalar_tensor_tensor(out=rt[:, 1], in0=rt[:, 3], scalar=2 * NEG, in1=rt[:, 1],
                                            op0=ALU.mult, op1=ALU.add).then_inc(
                    vector_step, p.gives(vector_step))
                eng.wait_ge(vector_step, p.given(vector_step))
                first_max(r16[1], w16, NE, ssq[:, 0:NT], r16[2], r16[5])
                v.tensor_tensor(rt[:, 3], rt[:, 3], rt[:, 5], ALU.add).then_inc(
                    vector_step, p.gives(vector_step))
                eng.wait_ge(vector_step, p.given(vector_step))
                v.tensor_tensor(rt[:, 3], rt[:, 3], rt[:, 0], ALU.mult).then_inc(
                    vector_step, p.gives(vector_step))
                eng.wait_ge(vector_step, p.given(vector_step))
                v.tensor_reduce(ssq[:, 0:NT], r16[3], AX, ALU.add).then_inc(vector_step, p.gives(vector_step))
                eng.wait_ge(vector_step, p.given(vector_step))
                v.reciprocal(ssq[:, NT:2 * NT], ssq[:, 0:NT]).then_inc(vector_step, p.gives(vector_step))
                eng.wait_ge(vector_step, p.given(vector_step))
                v.tensor_tensor(r16[4], r16[3], spread(ssq[:, NT:2 * NT], NE), ALU.mult).then_inc(
                    comb_ready, p.gives(comb_ready))
                with p.loop("moe", NG):
                    ring_at.next(12)
                    for e in range(4):
                        d = e % 2
                        silu = SC[:, 2 * d:2 * d + 2]
                        eng.wait_ge(handed[2], p.next(handed[2]))
                        eng.wait_ge(handed[3], p.next(handed[3]))
                        eng.wait_ge(filled[6 + d], p.next(filled[6 + d]))
                        v.tensor_tensor(silu, silu, repeat(bank(6 + d), 2), ALU.mult).then_inc(
                            weights_used[d], p.gives(weights_used[d]))
                        eng.wait_ge(weights_used[d], p.given(weights_used[d]))
                        for m in range(2):
                            eng.wait_ge(filled[m], p.next(filled[m]))
                            v.tensor_tensor(hid[2 * e + m], bank(m), silu[:, m], ALU.mult).then_inc(
                                handed[m], p.gives(handed[m]))
                        part = slice(2 * e, 2 * e + 2)
                        acts_low(hid[part], hid_lo[part], M_r[part])
                    for c in range(NC):
                        b = 4 + c % 2
                        eng.wait_ge(filled[b], p.next(filled[b]))
                        v.scalar_tensor_tensor(out=X[:, c], in0=bank(b), scalar=mod[:, 5 * NC + c:5 * NC + c + 1],
                                                         in1=X[:, c], op0=ALU.mult, op1=ALU.add).then_inc(
                            (handed if c == NC - 1 else emptied)[b], p.gives((handed if c == NC - 1 else emptied)[b]))
                ring_at.wrap()
                eng.wait_ge(emptied[4], p.given(emptied[4]))
                eng.wait_ge(handed[5], p.given(handed[5]))
            for t in range(NT):
                for f in range(2):
                    eng.wait_ge(filled[f], p.next(filled[f]))
                    v.tensor_copy(xin[:, t, f * 512:(f + 1) * 512], bank(f)).then_inc(
                        (emptied, handed)[f][f], p.gives((emptied, handed)[f][f]))

        @block.gpsimd
        def _(eng):
            p = Program(eng, "pool", rate)
            ring_at = Ring(p)
            splits = [0]

            def split_low():
                j, i = ring_at.next(), splits[0] % 2
                splits[0] += 1
                eng.wait_ge(high_ready[i], p.next(high_ready[i]))
                eng.tensor_tensor(low[i], ring[:, j], high[i].bitcast(F32), ALU.subtract).then_inc(
                    slot_used[j], p.gives(slot_used[j]))

            for sem in (*added, *qs_ready):
                eng.sem_inc(sem, 1)

            def alone():
                eng.sem_inc(waited["pool"], 1)



            def select(ap, op, fill, base, pattern, channel):
                eng.affine_select(out=ap, in_=ap, compare_op=op, fill=fill, base=base, pattern=pattern,
                                       channel_multiplier=channel).then_inc(pool_step, p.gives(pool_step))
                eng.wait_ge(pool_step, p.given(pool_step))

            eng.memset(ident[:, :], 0.0).then_inc(pool_step, p.gives(pool_step))
            eng.wait_ge(pool_step, p.given(pool_step))
            select(ident[:, :], ALU.not_equal, 1.0, 0, [[-1, P]], 1)
            eng.memset(ones[:, :], 1.0).then_inc(pool_step, p.gives(pool_step))
            eng.wait_ge(pool_step, p.given(pool_step))
            eng.memset(cmask[:, :], 0.0).then_inc(pool_step, p.gives(pool_step))
            eng.wait_ge(pool_step, p.given(pool_step))
            select(cmask[:, :], ALU.is_ge, NEG, 0, [[-1, P]], 1)
            eng.memset(swmask[:, :], 0.0).then_inc(pool_step, p.gives(pool_step))
            eng.wait_ge(pool_step, p.given(pool_step))
            select(swmask[:, 0:P], ALU.is_gt, NEG, 0, [[1, P]], -1)
            select(swmask[:, P:], ALU.is_ge, NEG, 0, [[-1, P]], 1)
            eng.memset(lmask[:, :, :], 0.0).then_inc(pool_step, p.gives(pool_step))
            eng.wait_ge(pool_step, p.given(pool_step))
            for lv in range(LEVELS):
                h = 1 << lv
                n = P // (2 * h)
                up = lmask[:, lv].rearrange("p (n a h) -> p n a h", n=n, a=2)[:, :, 1]
                eng.memset(up, 1.0).then_inc(pool_step, p.gives(pool_step))
                eng.wait_ge(pool_step, p.given(pool_step))
                select(up, ALU.is_ge, 0.0, 0, [[-2 * h, n], [0, h]], 1)
                select(up, ALU.is_ge, 0.0, h - 1, [[2 * h, n], [0, h]], -1)
            freq = np.float32(10000.0) ** (-np.arange(0, ROPE, 2, dtype=np.float32) / np.float32(ROPE))
            for i in range(HALF):
                eng.memset(ifr[:, i:i + 1], float(freq[i]))
            for l in range(DEPTH):
                li = 0.8 - 0.6 * math.exp(-0.3 * l)
                eng.memset(litab[:, l, 0:1], li)
                eng.memset(litab[:, l, 1:2], 1.0 - li)
            eng.memset(consts[:, 0:1], EPS)
            eng.memset(consts[:, 1:2], 1.0)
            eng.memset(lbt[:, 0, 0:NT], LN0)
            eng.memset(lbt[:, 0, NT:], 0.0)
            for e in range(NE):
                eng.memset(wexp[:, e:e + 1], float(NE - e))
            for g in range(NG):
                ins = eng.memset(wgrp[:, g:g + 1], float(NG - g))
            ins.then_inc(constants_ready, p.gives(constants_ready))
            eng.wait_ge(constants_ready, p.given(constants_ready))

            def gains(parts, after=None):
                eng.wait_ge(normed, p.next(normed))
                for k, (x, g) in enumerate(parts):
                    ins = eng.tensor_tensor(x, x, g, ALU.mult)
                    if after is None and k == len(parts) - 1:
                        ins.then_inc(gained, p.gives(gained))
                    else:
                        ins.then_inc(pool_step, p.gives(pool_step))
                        eng.wait_ge(pool_step, p.given(pool_step))
                if after is not None:
                    after()

            def rope(qk, t):
                tmp = [heads(sc[:, 1536 + 256 * k:1792 + 256 * k], 2 * HEADS) for k in range(4)]
                x1, x2 = qk[:, :, NOPE:NOPE + HALF], qk[:, :, NOPE + HALF:]
                c, s = repeat(cosT[:, t], 2 * HEADS), repeat(sinT[:, t], 2 * HEADS)
                for k, (x, y) in enumerate(((x1, c), (x2, s), (x1, s), (x2, c))):
                    eng.tensor_tensor(tmp[k], x, y, ALU.mult).then_inc(pool_step, p.gives(pool_step))
                    eng.wait_ge(pool_step, p.given(pool_step))
                eng.tensor_tensor(x1, tmp[0], tmp[1], ALU.subtract).then_inc(pool_step, p.gives(pool_step))
                eng.wait_ge(pool_step, p.given(pool_step))
                eng.tensor_tensor(x2, tmp[2], tmp[3], ALU.add).then_inc(gained, p.gives(gained))

            def do(step_, i):
                if step_ == "hg_norm":
                    for t in range(NT):
                        o = hgO[:, t]
                        gains([(heads(o, HEADS), repeat(row("hg_onorm"), HEADS))],
                              lambda: eng.tensor_tensor(o, o, TM[:, t, 512:1024], ALU.mult).then_inc(
                                  gained, p.gives(gained)))
                elif step_ == "c_norm":
                    gains([(CM[:, :, 0:QR], repeat(row("mla_q_norm"), NT))])
                    gains([(CM[:, :, QR:QR + KVR], repeat(row("mla_kv_norm"), NT))])
                elif step_ == "up":
                    qk = heads(qk_tile[i % 2], 2 * HEADS)
                    p.mark(handed[1])
                    gains([(qk[:, k * HEADS:(k + 1) * HEADS], repeat(row("mla_qk_norm", k * QKD, QKD), HEADS))
                           for k in range(2)], lambda: rope(qk, i))
                elif step_ == "dif_norm":
                    gains([(heads(DQK[:, i, k * 512:(k + 1) * 512], 8), repeat(row("diff_qk_norm", k * HD, HD), 8))
                           for k in range(2)])
                elif step_ == "swa_norm":
                    gains([(heads(SQKV[:, i, 0:512], 8), repeat(row("swa_qk_norm", 0, HD), 8)),
                           (heads(SQKV[:, i, 512:640], 2), repeat(row("swa_qk_norm", HD, HD), 2))])
                elif step_ == "dif_post":
                    for t in range(NT):
                        p.mark(handed[t % 2])
                        gains([(heads(y_tok["diff"][:, t], DH), repeat(row("diff_onorm"), DH))])

            eng.wait_ge(rope_ready, p.next(rope_ready, 2))
            p.mark(handed[1])
            with p.loop("layer", DEPTH):
                p.mark(handed[2])
                eng.wait_ge(rows_ready, p.next(rows_ready))
                alone()
                for pr in range(4):
                    for j in range(9):
                        i = (9 * pr + j) % 2
                        if j == 0:
                            p.mark(e_ready[i])
                            p.mark(qk_used[i])
                            continue
                        eng.wait_ge(e_ready[i], p.next(e_ready[i]))
                        if j < 8:
                            eng.wait_ge(qk_used[i], p.so_far(qk_used[i]))
                            p.mark(qk_used[i])
                            eng.tensor_tensor(hgQs[i], hgQ[:, pr], hgE[i], ALU.mult).then_inc(
                                qs_ready[i], p.gives(qs_ready[i]))
                        else:
                            eng.wait_ge(attn_used[pr % 2], p.so_far(attn_used[pr % 2]))
                            p.mark(attn_used[pr % 2])
                            eng.tensor_tensor(hgQin[pr % 2], hgQ[:, pr], hgE[i], ALU.mult).then_inc(
                                qin_ready, p.gives(qin_ready))
                for st, i in SCHEDULE:
                    do(st, i)
                ring_at.next(FRONT)
                with p.loop("merge", 2) as g:
                    split_low()
                    split_low()
                    for br in range(NB):
                        for j in range(4):
                            i = j % 2
                            if j == 0:
                                ring_at.next(3)
                            if br < NB - 1 and i == 0:
                                split_low()
                            p.mark(handed[2 + i])
                            if br:
                                eng.wait_ge(handed[i], p.next(handed[i]))
                                alone()
                                m = pick(merged, g * 4 + j)
                                eng.tensor_tensor(m, m, SC[:, 4 + i], ALU.add).then_inc(
                                    added[i], p.gives(added[i]))
                for _ in range(4):
                    split_low()
                p.mark(handed[0], NC // 2)
                p.mark(handed[1], NC // 2)
                p.mark(handed[2])
                p.mark(comb_ready)
                with p.loop("moe", NG) as g:
                    split_low()
                    split_low()
                    for e in range(4):
                        d = e % 2
                        if e == 0:
                            eng.wait_ge(comb_ready, p.so_far(comb_ready))
                        eng.wait_ge(diag_used[d], p.so_far(diag_used[d]))
                        alone()
                        p.mark(diag_used[d])
                        w = heads(rt[:, 4], NT)[:, :, bass.ds(g * 4 + e, 1)].to_broadcast([P, NT, P])
                        eng.tensor_tensor(heads(SC[:, 4 + d], NT), repeat(ident[:, :], NT), w, ALU.mult).then_inc(
                            diag_ready[d], p.gives(diag_ready[d]))
                        for m in range(2):
                            p.mark(handed[2 + m])
                            p.mark(handed[m])
                        split_low()
                        split_low()
                    split_low()
                    split_low()
                ring_at.wrap()


_INS = ("x c positions ada_w ada_b norm_mix norm_ffn w_in hg_lb_logits hg_onorm mla_q_norm mla_kv_norm "
        "mla_w_uq mla_w_ukv mla_qk_norm diff_qk_norm diff_lam diff_onorm swa_qk_norm swa_sinks w_branch "
        "w_out router_w router_bias moe_w_gate moe_w_up moe_w_down").split()


def program(nc, inputs, rate):
    dts = {"float32": F32, "int32": I32}
    args = {n: nc.dram_tensor(f"in_{n}", inputs[n].shape, dts[str(inputs[n].dtype)], kind="ExternalInput").ap()
            for n in _INS}
    out = nc.dram_tensor("out_x", (1, S, D), F32, kind="ExternalOutput").ap()
    build(nc, args, out, rate)


def kernel(**inputs):
    import numpy as _np
    import concourse.bacc as _bacc
    from concourse.bass_utils import run_bass_kernel_spmd as _run

    arrays = {n: _np.ascontiguousarray(inputs[n]) for n in _INS}
    rate = {}
    for _ in range(2):
        nc = _bacc.Bacc("TRN2", target_bir_lowering=False, num_devices=1)
        program(nc, arrays, rate)
    r = _run(nc, [{f"in_{n}": x for n, x in arrays.items()}], core_ids=[0])
    return r.results[0]["out_x"]
```
